# Optimizing a Trainium2 kernel written in Bass

```python
import math
import jax
import jax.numpy as jnp
from jax import lax
import numpy as np

D_MODEL = 1024
BATCH = 1
SEQ = 512
DEPTH = 1
DEC_BATCH = 1
DEC_SEQ = 256
PAST_LEN = 128

A_HEADS = 4
A_HD = 64
A_VD = 2 * A_HD
A_ROT = A_HD // 4
A_THETA = 500000.0
Q_BLOCK = 128
R_HEADS = 4
R_DK = 64
R_DV = 2 * R_DK
R_CHUNK = 128
R_THETA = 10000.0
N_GROUPS = 4
EXPERTS_PER_GROUP = 8
N_EXPERTS = N_GROUPS * EXPERTS_PER_GROUP
TOP_K = 2
D_EXPERT = 512
EXPERT_BLOCK = 256
EPS = 1e-6

A_QK_W = A_HEADS * 2 * A_HD
A_V_W = A_HEADS * A_VD
R_QK_W = R_HEADS * R_DK
R_V_W = R_HEADS * R_DV
IN_WIDTHS = (A_QK_W, A_QK_W, A_V_W, R_QK_W, R_QK_W, R_V_W, R_V_W, D_MODEL, D_MODEL)
D_IN = sum(IN_WIDTHS)

kernel_name = 'hybrid_diffattn_retention_hmoe'

def rmsnorm(x, g=None):
    xf = x.astype(jnp.float32)
    y = xf * lax.rsqrt(jnp.mean(xf * xf, axis=-1, keepdims=True) + EPS)
    if g is not None:
        y = y * g.astype(jnp.float32)
    return y.astype(x.dtype)

def partial_rotary(x, pos, rot_dim, theta):
    inv = theta ** (-jnp.arange(0, rot_dim, 2, dtype=jnp.float32) / rot_dim)
    ang = pos[:, None] * inv[None, :]
    cos = jnp.cos(ang)
    sin = jnp.sin(ang)
    xf = x.astype(jnp.float32)
    half = rot_dim // 2
    x1 = xf[..., :half]
    x2 = xf[..., half:rot_dim]
    out = jnp.concatenate([x1 * cos - x2 * sin, x2 * cos + x1 * sin, xf[..., rot_dim:]], axis=-1)
    return out.astype(x.dtype)

def diff_attention(q, k, v, lam, subln_g, lam_init):
    B, S = q.shape[0], q.shape[1]
    pos = jnp.arange(S, dtype=jnp.float32)
    q = partial_rotary(jnp.transpose(q, (0, 2, 3, 1, 4)), pos, A_ROT, A_THETA)
    k = partial_rotary(jnp.transpose(k, (0, 2, 3, 1, 4)), pos, A_ROT, A_THETA)
    v = jnp.transpose(v, (0, 2, 1, 3))
    nb = S // Q_BLOCK
    qb = jnp.moveaxis(q.reshape(B, A_HEADS, 2, nb, Q_BLOCK, A_HD), 3, 0)
    scale = A_HD ** -0.5

    def one_block(qblk):
        s = jnp.einsum('bhcqd,bhckd->bhcqk', qblk, k, preferred_element_type=jnp.float32) * scale
        p = jax.nn.softmax(s, axis=-1)
        a = p[:, :, 0] - lam * p[:, :, 1]
        return jnp.einsum('bhqk,bhkv->bhqv', a.astype(v.dtype), v)

    o = lax.map(one_block, qb)
    o = jnp.transpose(o, (1, 0, 3, 2, 4)).reshape(B, S, A_HEADS, A_VD)
    o = rmsnorm(o, subln_g) * (1.0 - lam_init)
    return o.reshape(B, S, A_V_W)

def _decay_scan(u, decay, reverse):
    def step(state, u_i):
        return decay * state + u_i, state
    _, states = lax.scan(step, jnp.zeros_like(u[:, :, 0]), jnp.moveaxis(u, 2, 0), reverse=reverse)
    return jnp.moveaxis(states, 0, 2)

def retention(q, k, v, decay_f, decay_b):
    B, S = q.shape[0], q.shape[1]
    C = R_CHUNK
    n = S // C
    f32 = jnp.float32
    pos = jnp.arange(S, dtype=f32)
    qf = partial_rotary(jnp.transpose(q, (0, 2, 1, 3)).astype(f32), pos, R_DK, R_THETA)
    kf = partial_rotary(jnp.transpose(k, (0, 2, 1, 3)).astype(f32), pos, R_DK, R_THETA) * (R_DK ** -0.5)
    vf = jnp.transpose(v, (0, 2, 1, 3)).astype(f32)
    qc = qf.reshape(B, R_HEADS, n, C, R_DK)
    kc = kf.reshape(B, R_HEADS, n, C, R_DK)
    vc = vf.reshape(B, R_HEADS, n, C, R_DV)
    lgf = -jnp.exp(decay_f.astype(f32))[:, None]
    lgb = -jnp.exp(decay_b.astype(f32))[:, None]
    idx = jnp.arange(C, dtype=f32)
    rel = idx[:, None] - idx[None, :]
    mask = (jnp.where(rel >= 0, jnp.exp(lgf[:, :, None] * jnp.maximum(rel, 0.0)), 0.0)
            + jnp.where(rel < 0, jnp.exp(lgb[:, :, None] * jnp.maximum(-rel, 0.0)), 0.0))
    s = jnp.einsum('bhncd,bhnmd->bhncm', qc, kc) * mask[None, :, None]
    y = jnp.einsum('bhncm,bhnmv->bhncv', s, vc)
    uf = jnp.einsum('bhncd,bhncv->bhndv', kc * jnp.exp(lgf * (C - 1 - idx))[None, :, None, :, None], vc)
    sf = _decay_scan(uf, jnp.exp(lgf * C)[:, :, None], reverse=False)
    y = y + jnp.einsum('bhncd,bhndv->bhncv', qc * jnp.exp(lgf * (idx + 1))[None, :, None, :, None], sf)
    ub = jnp.einsum('bhncd,bhncv->bhndv', kc * jnp.exp(lgb * idx)[None, :, None, :, None], vc)
    sb = _decay_scan(ub, jnp.exp(lgb * C)[:, :, None], reverse=True)
    y = y + jnp.einsum('bhncd,bhndv->bhncv', qc * jnp.exp(lgb * (C - idx))[None, :, None, :, None], sb)
    y = rmsnorm(y.reshape(B, R_HEADS, S, R_DV))
    return jnp.transpose(y, (0, 2, 1, 3)).reshape(B, S, R_V_W).astype(v.dtype)

def token_mixer(xn, w_in, lam_q1, lam_k1, lam_q2, lam_k2, subln_g, ret_decay_f, ret_decay_b,
                w_pa, w_pb, w_out, lam_init):
    B, S, _ = xn.shape
    f32 = jnp.float32
    z = jnp.einsum('bsd,de->bse', xn, w_in)
    qa, ka, va, qr, kr, vr, gr, ga, gb = jnp.split(z, np.cumsum(IN_WIDTHS)[:-1].tolist(), axis=-1)
    lam = (jnp.exp(jnp.sum(lam_q1.astype(f32) * lam_k1.astype(f32)))
           - jnp.exp(jnp.sum(lam_q2.astype(f32) * lam_k2.astype(f32))) + lam_init)
    oa = diff_attention(qa.reshape(B, S, A_HEADS, 2, A_HD), ka.reshape(B, S, A_HEADS, 2, A_HD),
                        va.reshape(B, S, A_HEADS, A_VD), lam, subln_g, lam_init)
    ob = retention(qr.reshape(B, S, R_HEADS, R_DK), kr.reshape(B, S, R_HEADS, R_DK),
                   vr.reshape(B, S, R_HEADS, R_DV), ret_decay_f, ret_decay_b)
    ob = jax.nn.silu(gr) * ob
    merged = jax.nn.sigmoid(ga) * (oa @ w_pa) + jax.nn.sigmoid(gb) * (ob @ w_pb)
    return merged @ w_out

def hier_moe(xn, w_rg, b_rg, w_re, b_re, w1, w3, w2):
    B, S, D = xn.shape
    f32 = jnp.float32
    xt = xn.reshape(-1, D)
    T = xt.shape[0]
    lg = jnp.einsum('td,dg->tg', xt, w_rg, preferred_element_type=f32) + b_rg.astype(f32)
    pg_top, g_sel = lax.top_k(jax.nn.softmax(lg, axis=-1), 1)
    le = jnp.einsum('td,gde->tge', xt, w_re, preferred_element_type=f32) + b_re.astype(f32)
    le = jnp.take_along_axis(le, g_sel[:, :, None], axis=1)[:, 0]
    pe_top, e_sel = lax.top_k(jax.nn.softmax(le, axis=-1), TOP_K)
    gate = pg_top * pe_top / jnp.sum(pe_top, axis=-1, keepdims=True)
    expert_id = (g_sel * EXPERTS_PER_GROUP + e_sel).reshape(-1)
    A = T * TOP_K
    tok = jnp.repeat(jnp.arange(T, dtype=jnp.int32), TOP_K)
    g_flat = gate.reshape(-1)
    order = jnp.argsort(expert_id)
    e_s = expert_id[order]
    tok_s = tok[order]
    g_s = g_flat[order]
    counts = jnp.bincount(expert_id, length=N_EXPERTS)
    start = jnp.cumsum(counts) - counts
    padded = (counts + EXPERT_BLOCK - 1) // EXPERT_BLOCK * EXPERT_BLOCK
    pend = jnp.cumsum(padded)
    pstart = pend - padded
    dest = pstart[e_s] + (jnp.arange(A, dtype=jnp.int32) - start[e_s])
    n_blocks = -(-A // EXPERT_BLOCK) + N_EXPERTS
    P = n_blocks * EXPERT_BLOCK
    slot_tok = jnp.zeros((P,), jnp.int32).at[dest].set(tok_s)
    slot_gate = jnp.zeros((P,), f32).at[dest].set(g_s)
    block_start = jnp.arange(n_blocks, dtype=pend.dtype) * EXPERT_BLOCK
    block_expert = jnp.minimum(jnp.searchsorted(pend, block_start, side='right'), N_EXPERTS - 1)

    def run_block(args):
        toks, gts, e = args
        xb = xt[toks]
        h = jax.nn.silu(xb @ w1[e]) * (xb @ w3[e])
        return (h @ w2[e]) * gts[:, None].astype(xt.dtype)

    yb = lax.map(run_block, (slot_tok.reshape(n_blocks, EXPERT_BLOCK),
                             slot_gate.reshape(n_blocks, EXPERT_BLOCK), block_expert))
    out = jnp.zeros_like(xt).at[slot_tok].add(yb.reshape(P, D))
    return out.reshape(B, S, D)

def trunk(x, attn_norm_g, w_in, lam_q1, lam_k1, lam_q2, lam_k2, subln_g, ret_decay_f, ret_decay_b,
          w_pa, w_pb, w_out, ffn_norm_g, w_rg, b_rg, w_re, b_re, w1, w3, w2, final_norm_g):
    for l in range(DEPTH):
        lam_init = 0.8 - 0.6 * math.exp(-0.3 * l)
        x = x + token_mixer(rmsnorm(x, attn_norm_g[l]), w_in[l], lam_q1[l], lam_k1[l], lam_q2[l],
                            lam_k2[l], subln_g[l], ret_decay_f[l], ret_decay_b[l], w_pa[l], w_pb[l],
                            w_out[l], lam_init)
        x = x + hier_moe(rmsnorm(x, ffn_norm_g[l]), w_rg[l], b_rg[l], w_re[l], b_re[l],
                         w1[l], w3[l], w2[l])
    return rmsnorm(x, final_norm_g)

def setup_inputs(seed: int = 0) -> dict:
    key = jax.random.key(seed)
    ks = jax.random.split(key, 24)
    f32 = jnp.float32

    def nrm(k, shape, scale):
        return jax.random.normal(k, shape, f32) * scale

    base_decay = jnp.log(-jnp.log1p(-(2.0 ** (-5.0 - jnp.arange(R_HEADS, dtype=f32)))))
    return {
        'x_prompt': nrm(ks[0], (BATCH, SEQ, D_MODEL), 1.0),
        'x_sample': nrm(ks[1], (DEC_BATCH, DEC_SEQ, D_MODEL), 1.0),
        'attn_norm_g': 1.0 + nrm(ks[2], (DEPTH, D_MODEL), 0.02),
        'w_in': nrm(ks[3], (DEPTH, D_MODEL, D_IN), D_MODEL ** -0.5),
        'lam_q1': nrm(ks[4], (DEPTH, A_HD), 0.1),
        'lam_k1': nrm(ks[5], (DEPTH, A_HD), 0.1),
        'lam_q2': nrm(ks[6], (DEPTH, A_HD), 0.1),
        'lam_k2': nrm(ks[7], (DEPTH, A_HD), 0.1),
        'subln_g': 1.0 + nrm(ks[8], (DEPTH, A_VD), 0.02),
        'ret_decay_f': base_decay[None, :] + nrm(ks[9], (DEPTH, R_HEADS), 0.05),
        'ret_decay_b': base_decay[None, :] + nrm(ks[10], (DEPTH, R_HEADS), 0.05),
        'w_pa': nrm(ks[11], (DEPTH, A_V_W, D_MODEL), A_V_W ** -0.5),
        'w_pb': nrm(ks[12], (DEPTH, R_V_W, D_MODEL), R_V_W ** -0.5),
        'w_out': nrm(ks[13], (DEPTH, D_MODEL, D_MODEL), D_MODEL ** -0.5),
        'ffn_norm_g': 1.0 + nrm(ks[14], (DEPTH, D_MODEL), 0.02),
        'w_rg': nrm(ks[15], (DEPTH, D_MODEL, N_GROUPS), D_MODEL ** -0.5),
        'b_rg': nrm(ks[16], (DEPTH, N_GROUPS), 0.01),
        'w_re': nrm(ks[17], (DEPTH, N_GROUPS, D_MODEL, EXPERTS_PER_GROUP), D_MODEL ** -0.5),
        'b_re': nrm(ks[18], (DEPTH, N_GROUPS, EXPERTS_PER_GROUP), 0.01),
        'w1': nrm(ks[19], (DEPTH, N_EXPERTS, D_MODEL, D_EXPERT), D_MODEL ** -0.5),
        'w3': nrm(ks[20], (DEPTH, N_EXPERTS, D_MODEL, D_EXPERT), D_MODEL ** -0.5),
        'w2': nrm(ks[21], (DEPTH, N_EXPERTS, D_EXPERT, D_MODEL), D_EXPERT ** -0.5),
        'final_norm_g': 1.0 + nrm(ks[22], (D_MODEL,), 0.02),
    }

def reference(x_prompt, x_sample, attn_norm_g, w_in, lam_q1, lam_k1, lam_q2, lam_k2, subln_g,
              ret_decay_f, ret_decay_b, w_pa, w_pb, w_out, ffn_norm_g, w_rg, b_rg, w_re, b_re,
              w1, w3, w2, final_norm_g):
    y_prompt = trunk(x_prompt, attn_norm_g, w_in, lam_q1, lam_k1, lam_q2, lam_k2, subln_g,
                     ret_decay_f, ret_decay_b, w_pa, w_pb, w_out, ffn_norm_g, w_rg, b_rg, w_re,
                     b_re, w1, w3, w2, final_norm_g)
    y_sample = trunk(x_sample, attn_norm_g, w_in, lam_q1, lam_k1, lam_q2, lam_k2, subln_g,
                     ret_decay_f, ret_decay_b, w_pa, w_pb, w_out, ffn_norm_g, w_rg, b_rg, w_re,
                     b_re, w1, w3, w2, final_norm_g)
    return (y_prompt, y_sample)


_drawn_inputs = setup_inputs


def setup_inputs(seed=0):
    import zlib

    import numpy as np

    out = dict(_drawn_inputs(seed))
    spreads = {}
    factors = {'subln_g': 2.948,
     'b_rg': 15.713,
     'b_re': 7.74,
     'final_norm_g': 22.544,
     'ffn_norm_g': 2.703}
    for name, (base, spread) in spreads.items():
        noise = np.random.default_rng([zlib.crc32(name.encode()), seed]).standard_normal(out[name].shape)
        drawn = base * np.exp(spread * noise) if base else spread * noise
        out[name] = jnp.asarray(drawn.astype(out[name].dtype))
    for name, factor in factors.items():
        out[name] = (out[name] * factor).astype(out[name].dtype)
    return out
```

```python
from contextlib import ExitStack

import concourse.bass as bass
from concourse import mybir

F32 = mybir.dt.float32
F32R = mybir.dt.float32r
I32 = mybir.dt.int32
U32 = mybir.dt.uint32
ALU = mybir.AluOpType
ACT = mybir.ActivationFunctionType
AX = mybir.AxisListType

P = 128
D = 1024
KC = D // P
SEQS = (512, 256)
T = sum(SEQS)
NT = T // P
H = 4
HD = 64
VD = 128
D_IN = 5120
NCH = D_IN // 512
C_Q, C_V, C_R, C_VR, C_GR, C_GA, C_GB = 0, 1024, 1536, 2048, 2560, 3072, 4096
NG, EPG = 4, 8
NE = NG * EPG
FF = 512
CAP = 128
MAXB = T // CAP
NOV = (2 * T) // (CAP + 1)
NB = NE + NOV
EPS = 1e-6
LAM_INIT = 0.8 - 0.6
KB = 1024
RELW = 7 * P
PIECE = 2048
RAWS = 6
HLS = 4
ZP = 2 * NCH
PP = 8
PRE = ZP + PP

_c = {}
_n = 0
for _name, _w in (("ident", P), ("tri", P), ("ones", P), ("rel", RELW), ("cosA", 32), ("sinA", 32),
                  ("cosR", 128), ("sinR", 128), ("e128", NE), ("grank", NG), ("erank", NE),
                  ("miota", NOV), ("tok", NT)):
    _c[_name] = (_n, _n + _w)
    _n += _w
NCST = _n


def constants():
    import numpy as np
    t = np.zeros((P, NCST), np.float32)

    def put(name, v):
        a, b = _c[name]
        t[:, a:b] = v
    i = np.arange(P)
    put("ident", np.eye(P))
    put("tri", (i[:, None] < i[None, :]).astype(np.float32))
    put("ones", 1.0)
    put("rel", np.arange(RELW)[None, :] - 3 * P - i[:, None])
    for rot, theta, cn, sn in ((16, 500000.0, "cosA", "sinA"), (64, 10000.0, "cosR", "sinR")):
        inv = np.float32(theta) ** (-np.arange(0, rot, 2, dtype=np.float32) / np.float32(rot))
        inv = inv.astype(np.float32)
        ang = (np.arange(512, dtype=np.float32)[:, None] * inv[None, :]).astype(np.float32)
        for f, n in ((np.cos, cn), (np.sin, sn)):
            v = f(ang.astype(np.float64)).astype(np.float32).reshape(4, P, rot // 2)
            put(n, v.transpose(1, 0, 2).reshape(P, -1))
    e = np.arange(NE)
    put("e128", e * CAP)
    put("grank", NG - np.arange(NG))
    put("erank", EPG - e % EPG)
    put("miota", np.arange(NOV))
    put("tok", i[:, None] + P * np.arange(NT)[None, :])
    return t


def hybrid_layer(nc, A):
    ctx = ExitStack()
    base = (nc.sbuf_base + 63) // 64 * 64
    RAW_O, HL_O, D_O, E_O = 0, 48 * KB, 112 * KB, 160 * KB

    def at(name, off, shape, dt=F32):
        return nc.alloc_sbuf_tensor_at(name, shape, dt, offset=base + off)

    raw = [at(f"raw{s}", RAW_O + s * 8 * KB, [P, PIECE]) for s in range(RAWS)]
    whi = [at(f"whi{s}", HL_O + s * 8 * KB, [P, PIECE], F32R) for s in range(HLS)]
    wlo = [at(f"wlo{s}", HL_O + (HLS + s) * 8 * KB, [P, PIECE], F32R) for s in range(HLS)]
    xTh = at("xTh", D_O, [P, KC, T], F32R)
    xTl = at("xTl", D_O + 24 * KB, [P, KC, T], F32R)
    oTh = [at(f"oTh{b}", D_O + b * 12 * KB, [P, H, T], F32R) for b in range(2)]
    oTl = [at(f"oTl{b}", D_O + (2 + b) * 12 * KB, [P, H, T], F32R) for b in range(2)]
    mTh = [at(f"mTh{s}", D_O + s * 4 * KB, [P, KC, P], F32R) for s in range(2)]
    mTl = [at(f"mTl{s}", D_O + 8 * KB + s * 4 * KB, [P, KC, P], F32R) for s in range(2)]
    x2 = at("x2", D_O + 16 * KB, [P, NT, D])
    CST_O = E_O
    cst = at("cst", CST_O, [P, NCST])
    W_O = CST_O + (NCST * 4 + 63) // 64 * 64
    off = [W_O]

    def small(name, shape, dt=F32):
        n = 4
        for s in shape[1:]:
            n *= s
        t = at(name, off[0], shape, dt)
        off[0] += (n + 31) // 32 * 32
        return t
    gn1 = small("gn1", [P, KC])
    ssq = small("ssq", [P, 16])
    rstd = small("rstd", [P, 16])
    rs_a = small("rs_a", [P, 16])
    rs_b = small("rs_b", [P, 16])
    gsub = small("gsub", [P, 1])
    lamv = small("lamv", [P, 4])
    decay = small("decay", [P, 8])
    mx = small("mx", [P, 2, 2])
    nm = small("nm", [P, 2, 2])
    sume = small("sume", [P, 2, 2])
    rc = small("rc", [P, 2, 2])
    gates = small("gates", [P, 2, NT])
    slotf = small("slotf", [P, 2, NT])
    sloti = small("sloti", [P, 2, NT], U32)
    toki = small("toki", [P, NT], I32)
    nbi = small("nbi", [1, 16], I32)
    F_O = off[0]
    FREE = 212800 - F_O
    assert FREE >= 38 * KB, FREE
    xin = at("xin", F_O, [P, NT, D])
    zst = [at(f"zst{s}", F_O + 24 * KB + s * 2 * KB, [P, 512]) for s in range(4)]
    junk = at("junk", F_O + 32 * KB, [P, D])
    zrow = at("zrow", F_O + 37 * KB, [P, 256])
    lamr = at("lamr", F_O + 36 * KB, [P, 4, HD])
    zqk = at("zqk", HL_O, [P, 4, 1024])
    zv = at("zv", HL_O + 16 * KB, [P, 4, 512])
    zr = at("zr", HL_O + 24 * KB, [P, 4, 512])
    zvr = at("zvr", HL_O + 32 * KB, [P, 4, 512])
    zgr = at("zgr", HL_O + 40 * KB, [P, 4, 512])
    qkT = at("qkT", HL_O + 48 * KB, [P, 2, H, 512])
    prob = [at(f"prob{s}", HL_O + s * 4 * KB, [P, 2, 512]) for s in range(2)]
    att = [at(f"att{s}", HL_O + 8 * KB + s * 2 * KB, [P, 512]) for s in range(2)]
    attT = [at(f"attT{s}", HL_O + 12 * KB + s * 2 * KB, [P, 512]) for s in range(2)]
    smk = at("smk", HL_O + 24 * KB, [P, 4, 512])
    rqkT = at("rqkT", F_O, [P, 2, 2, 512])
    rtmp = at("rtmp", F_O + 8 * KB, [P, 4, 1024])
    oun = at("oun", F_O + 8 * KB, [P, 4, 512])
    yun = at("yun", F_O + 16 * KB, [P, 4, 512])
    wdec = at("wdec", F_O + 24 * KB, [P, H, RELW])
    sqt = at("sqt", HL_O + 48 * KB, [P, 4, 512])
    otm = [at(f"otm{s}", HL_O + 56 * KB + s * 2 * KB, [P, 512]) for s in range(2)]
    mg = at("mg", F_O, [P, NT, D])
    gat = at("gat", F_O + 24 * KB, [P, 2 * D])
    prd = [at(f"prd{s}", F_O + 32 * KB + s * 2 * KB, [P, 512]) for s in range(2)]
    xres = at("xres", F_O + 24 * KB, [P, D])
    g2 = at("g2", F_O, [P, D])
    rrow = [at(f"rrow{s}", F_O + 4 * KB + s * 4 * KB, [P, D]) for s in range(2)]
    rT = [at(f"rT{s}", F_O + 12 * KB + s * 4 * KB, [P, KC, P]) for s in range(2)]
    wrt = at("wrt", F_O + 20 * KB, [P, KC, NG + NE])
    brt = at("brt", F_O + 22 * KB, [P, NG + NE])
    RO = F_O + 23 * KB
    lg = at("lg", RO, [P, NT, NG + NE])
    sel = at("sel", RO + 1 * KB, [P, NT, NE])
    A1 = at("A1", RO + 2 * KB, [P, NT, NE])
    A2 = at("A2", RO + 3 * KB, [P, NT, NE])
    t1 = at("t1", RO + 4 * KB, [P, NT, NE])
    t2 = at("t2", RO + 5 * KB, [P, NT, NE])
    Ab = at("Ab", RO + 6 * KB, [P, NT, NE])
    gq = at("gq", RO + 7 * KB, [P, 8, NT, NG])
    v6 = at("v6", RO + 8 * KB, [P, 12, NT])
    nov = at("nov", RO + 9 * KB, [P, 3, NE])
    ovb = at("ovb", RO + 9 * KB + 512, [P, NE])
    bt = at("bt", RO + 10 * KB, [1, NOV, NE])
    bts = at("bts", RO + 12 * KB, [1, NOV])
    zini = at("zini", RO + 13 * KB, [P, NB + 1], I32)
    XT_O = D_O
    eTh = at("eTh", XT_O, [P, KC, P], F32R)
    eTl = at("eTl", XT_O + 4 * KB, [P, KC, P], F32R)
    hTh = at("hTh", XT_O + 8 * KB, [P, 4, P], F32R)
    hTl = at("hTl", XT_O + 10 * KB, [P, 4, P], F32R)
    sg = at("sg", XT_O + 12 * KB, [P, 512])
    hh = at("hh", XT_O + 14 * KB, [P, 512])
    xg = at("xg", HL_O + 24 * KB, [P, D])
    idxb = at("idxb", HL_O + 28 * KB, [P, 1], I32)
    ystage = at("ystage", HL_O + 56 * KB, [P, D])
    ya = [[at(f"ya{s}{k}", RAW_O + (2 * s + k) * 4 * KB, [P, D]) for k in range(2)] for s in range(2)]
    gf = at("gf", RAW_O + 16 * KB, [P, D])
    yo = [at(f"yo{s}", RAW_O + 20 * KB + s * 4 * KB, [P, D]) for s in range(2)]
    fj = at("fj", RAW_O + 28 * KB, [P, D])

    ps = [ctx.enter_context(nc.psum_tensor(f"ps{i}", [P, 512], F32)) for i in range(8)]

    def C(name):
        a, b = _c[name]
        return cst[:, a:b]
    ident = C("ident")

    z_d = nc.dram_tensor("z_scratch", [T, D_IN], F32, kind="Internal").ap()
    xn_d = nc.dram_tensor("xn_scratch", [T, D], F32, kind="Internal").ap()
    st_d = nc.dram_tensor("slot_token", [(NB + 1) * CAP, 1], I32, kind="Internal").ap()
    y_d = nc.dram_tensor("y_scratch", [NB * CAP, D], F32, kind="Internal").ap()

    def sem(name):
        return ctx.enter_context(nc.semaphore(name))
    with ctx:
        s_cst = sem("s_cst")
        s_par = sem("s_par")
        s_x = sem("s_x")
        s_raw = [sem(f"s_raw{s}") for s in range(RAWS)]
        s_hi = sem("s_hi")
        s_lo = sem("s_lo")
        s_pe = sem("s_pe")
        s_sq = sem("s_sq")
        s_dv = sem("s_dv")
        s_rstd1 = sem("s_rstd1")
        s_xs = sem("s_xs")
        s_nT = sem("s_nT")
        s_nth = sem("s_nth")
        s_ntc = sem("s_ntc")
        s_ntl = sem("s_ntl")
        s_zmm = sem("s_zmm")
        s_zev = sem("s_zev")
        s_zst = [sem(f"s_zst{s}") for s in range(4)]
        s_zl = [sem(f"s_zl{s}") for s in range(2)]
        s_decay = sem("s_decay")
        s_lame = sem("s_lame")
        s_warg = sem("s_warg")
        s_wexp = sem("s_wexp")
        s_rot = sem("s_rot")
        s_qT = sem("s_qT")
        s_qTc = sem("s_qTc")
        s_sc = sem("s_sc")
        s_mx = sem("s_mx")
        s_ex = sem("s_ex")
        s_a = sem("s_a")
        s_aT = sem("s_aT")
        s_aTc = sem("s_aTc")
        s_o = sem("s_o")
        s_oc = sem("s_oc")
        s_rs = sem("s_rs")
        s_rm = sem("s_rm")
        s_ry = sem("s_ry")
        s_ryc = sem("s_ryc")
        s_sig = sem("s_sig")
        s_on = sem("s_on")
        s_oT = sem("s_oT")
        s_oTm = sem("s_oTm")
        s_oTh = sem("s_oTh")
        s_oTl = sem("s_oTl")
        s_gl = sem("s_gl")
        s_gs = sem("s_gs")
        s_pm = sem("s_pm")
        s_mgd = sem("s_mgd")
        s_mT = sem("s_mT")
        s_mTh = sem("s_mTh")
        s_mTl = sem("s_mTl")
        s_xr = sem("s_xr")
        s_w = sem("s_w")
        s_x2 = sem("s_x2")
        s_rp = sem("s_rp")
        s_sq2 = sem("s_sq2")
        s_rr = sem("s_rr")
        s_rst = [sem(f"s_rst{s}") for s in range(2)]
        s_rTm = sem("s_rTm")
        s_rTc = sem("s_rTc")
        s_lg = sem("s_lg")
        s_rx = sem("s_rx")
        s_re = sem("s_re")
        s_Ab = sem("s_Ab")
        s_rk = sem("s_rk")
        s_slot = sem("s_slot")
        s_zi = sem("s_zi")
        s_zt = sem("s_zt")
        s_sct = sem("s_sct")
        s_nb = sem("s_nb")
        s_ix = sem("s_ix")
        s_gx = sem("s_gx")
        s_idx = sem("s_idx")
        s_eT = sem("s_eT")
        s_eTh = sem("s_eTh")
        s_eTl = sem("s_eTl")
        s_h1 = sem("s_h1")
        s_sgm = sem("s_sgm")
        s_h = sem("s_h")
        s_hT = sem("s_hT")
        s_hTh = sem("s_hTh")
        s_hTl = sem("s_hTl")
        s_y = sem("s_y")
        s_yc = sem("s_yc")
        s_ys = sem("s_ys")
        s_md = sem("s_md")
        s_yz = sem("s_yz")
        s_zr = sem("s_zr")
        s_g1 = [sem(f"s_g1{s}") for s in range(2)]
        s_yf = sem("s_yf")
        s_gf = sem("s_gf")
        s_out = [sem(f"s_out{s}") for s in range(2)]
        block = ctx.enter_context(nc.Block())

        x_tiles = [A["x_prompt"][0, t * P:(t + 1) * P, :] for t in range(4)] + \
                  [A["x_sample"][0, t * P:(t + 1) * P, :] for t in range(2)]
        o_tiles = [A["y_prompt"][0, t * P:(t + 1) * P, :] for t in range(4)] + \
                  [A["y_sample"][0, t * P:(t + 1) * P, :] for t in range(2)]
        w_in = A["w_in"][0].rearrange("(p c) n -> p c n", c=KC)
        w_out = A["w_out"][0].rearrange("(p c) n -> p c n", c=KC)
        w_pab = [A[n][0].rearrange("(h p) n -> p h n", p=P) for n in ("w_pa", "w_pb")]
        e_w = {"w1": A["w1"][0].rearrange("e (p c) f -> e p (c f)", c=KC),
               "w3": A["w3"][0].rearrange("e (p c) f -> e p (c f)", c=KC),
               "w2": A["w2"][0].rearrange("e (p c) n -> e p (c n)", c=4)}

        SEQ_T0 = (0, 4)
        SEQ_NT = (4, 2)
        ITS = [(s, h, qt) for s in range(2) for h in range(H) for qt in range(SEQ_NT[s])]

        @block.sync
        def _(sp):
            sp.dma_start(cst[:, :], A["consts"]).then_inc(s_cst, 16)
            for t in range(NT):
                sp.dma_start(xin[:, t, :], x_tiles[t]).then_inc(s_x, 16)
            sp.dma_start(gn1[:, :], A["attn_norm_g"][0].rearrange("(p c) -> p c", c=KC)).then_inc(s_par, 16)
            sp.dma_start(gsub[:, :], A["subln_g"][0].rearrange("(p c) -> p c", c=1)).then_inc(s_par, 16)
            sp.dma_start(decay[:, 0:4], A["ret_decay_f"].partition_broadcast(P)[:, 0, :]).then_inc(s_par, 16)
            sp.dma_start(decay[:, 4:8], A["ret_decay_b"].partition_broadcast(P)[:, 0, :]).then_inc(s_par, 16)
            for k, n in enumerate(("lam_q1", "lam_k1", "lam_q2", "lam_k2")):
                sp.dma_start(lamr[:, k, :], A[n].partition_broadcast(P)[:, 0, :]).then_inc(s_par, 16)
            def z_piece(i, j):
                c = bass.ds(i * 1024 + (j // 2) * 512, 512)
                sp.dma_start(raw[j][:, :].rearrange("p (c n) -> p c n", n=512),
                             w_in[:, 4 * (j % 2):4 * (j % 2) + 4, c]).then_inc(s_raw[j], 16)
            for j in range(4):
                z_piece(0, j)
            with sp.Fori(1, NCH // 2) as i:
                for j in range(4):
                    sp.wait_ge(s_lo, 4 * i + (j - 3))
                    z_piece(i, j)
            def p_piece(p):
                slot = (4 + p) % RAWS
                if p >= 2:
                    sp.wait_ge(s_lo, (15 + p) if p < 6 else (ZP + p - 5))
                dst = raw[slot][:, :].rearrange("p (c n) -> p c n", n=512)
                if p < 4:
                    src = w_pab[p % 2][:, :, (p // 2) * 512:(p // 2) * 512 + 512]
                else:
                    q = p - 4
                    src = w_out[:, 4 * (q % 2):4 * (q % 2) + 4, (q // 2) * 512:(q // 2) * 512 + 512]
                sp.dma_start(dst, src).then_inc(s_raw[slot], 16)
            for p in range(2):
                p_piece(p)
            for p in range(2, 6):
                p_piece(p)
            for s in range(2):
                t0, nt = SEQ_T0[s], SEQ_NT[s]
                if s == 0:
                    for k in range(4):
                        sp.wait_ge(s_zst[k], 16 * NCH * NT // 4)
                else:
                    sp.wait_ge(s_oTl, 8)
                rows = z_d[t0 * P:(t0 + nt) * P, :].rearrange("(t p) n -> p t n", p=P)
                for dst, c0, n in ((zqk, C_Q, 1024), (zr, C_R, 512), (zv, C_V, 512), (zvr, C_VR, 512),
                                   (zgr, C_GR, 512)):
                    sp.dma_start(dst[:, 0:nt, :], rows[:, :, c0:c0 + n]).then_inc(s_zl[s], 16)
            for t in range(NT):
                if t == 0:
                    sp.wait_ge(s_oTl, 16)
                else:
                    sp.wait_ge(s_mgd, 2 * t)
                sp.dma_start(gat[:, :], z_d[t * P:(t + 1) * P, C_GA:C_GA + 2 * D]).then_inc(s_gl, 16)
                if t == 0:
                    for p in range(6, 8):
                        p_piece(p)
            for t in range(NT):
                if t == 0:
                    sp.wait_ge(s_mgd, 2 * NT)
                else:
                    sp.wait_ge(s_x2, 2 * t)
                sp.dma_start(xres[:, :], x_tiles[t]).then_inc(s_xr, 16)
            sp.wait_ge(s_x2, 2 * NT)
            sp.dma_start(g2[:, :], A["ffn_norm_g"].partition_broadcast(P)[:, 0, :]).then_inc(s_rp, 16)
            sp.dma_start(wrt[:, :, 0:NG], A["w_rg"][0].rearrange("(p c) g -> p c g", c=KC)).then_inc(s_rp, 16)
            for g in range(NG):
                sp.dma_start(wrt[:, :, NG + g * EPG:NG + (g + 1) * EPG],
                             A["w_re"][0, g].rearrange("(p c) e -> p c e", c=KC)).then_inc(s_rp, 16)
            sp.dma_start(brt[:, 0:NG], A["b_rg"].partition_broadcast(P)[:, 0, :]).then_inc(s_rp, 16)
            sp.dma_start(brt[:, NG:NG + NE],
                         A["b_re"].rearrange("a g e -> a (g e)").partition_broadcast(P)[:, 0, :]).then_inc(s_rp, 16)

            def e_pieces(b, e):
                for j in range(6):
                    sp.wait_ge(s_lo, 6 * b + (PRE - 5 + j))
                    src = e_w[("w1", "w3", "w2")[j // 2]][bass.ds(e, 1), :, (j % 2) * PIECE:(j % 2 + 1) * PIECE]
                    sp.dma_start(raw[j][:, :], src[0]).then_inc(s_raw[j], 16)
            with sp.Fori(0, NE) as b:
                e_pieces(b, b)
            sp.wait_ge(s_nb, 1)
            nb = sp.value_load(nbi[0:1, 0:1], min_val=NE, max_val=NB)
            with sp.If(nb > NE):
                with sp.Fori(NE, nb) as b:
                    e = sp.value_load(nbi[0:1, bass.ds(b - (NE - 1), 1)], min_val=0, max_val=NE - 1)
                    e_pieces(b, e)
            sp.wait_ge(s_md, 1)
            sp.dma_start(gf[:, :], A["final_norm_g"].rearrange("(a n) -> a n", a=1).partition_broadcast(P)[:, 0, :]).then_inc(s_gf, 16)
            for t in range(NT):
                sp.wait_ge(s_yf, t + 1)
                sp.dma_start(o_tiles[t], yo[t % 2][:, :]).then_inc(s_out[t % 2], 16)
            for k in range(2):
                sp.wait_ge(s_out[k], 16 * NT // 2)

        @block.tensor
        def _(pe):
            def split_mm(out, ah, al, bh, bl, first, last):
                pe.matmul(out, ah, bh, start=first, stop=False)
                pe.matmul(out, ah, bl, start=False, stop=False)
                return pe.matmul(out, al, bh, start=False, stop=last)

            pe.wait_ge(s_cst, 16)
            for t in range(NT):
                pe.wait_ge(s_xs, t + 1)
                for j in range(2):
                    n = 2 * t + j
                    if n >= 4:
                        pe.wait_ge(s_ntc, n - 3)
                    for c in range(4):
                        mm = pe.transpose(ps[4 + n % 4][:, c * P:(c + 1) * P],
                                          xin[:, t, 4 * j + c::KC], ident)
                    mm.then_inc(s_nT, 1)
            pe.wait_ge(s_nth, 2 * NT)
            pe.wait_ge(s_ntl, 2 * NT)

            def z_chunk(i, m):
                for t in range(NT):
                    bank = ps[(6 * m + t) % 4]
                    n = 12 * i + 6 * m + t
                    if not (isinstance(i, int) and i == 0 and 6 * m + t < 4):
                        pe.wait_ge(s_zev, n - 3)
                    for j in range(2):
                        s = 2 * m + j
                        if t == 0:
                            pe.wait_ge(s_lo, 4 * i + (s + 1))
                        for k in range(4):
                            c = 4 * j + k
                            mm = split_mm(bank[:, :], xTh[:, c, t * P:(t + 1) * P], xTl[:, c, t * P:(t + 1) * P],
                                          whi[s][:, k * 512:(k + 1) * 512], wlo[s][:, k * 512:(k + 1) * 512],
                                          c == 0, c == KC - 1)
                        if t == NT - 1 and j == 0:
                            mm.then_inc(s_pe, 1)
                    mm.then_inc(s_zmm, 1)

            z_chunk(0, 0)
            z_chunk(0, 1)
            with pe.Fori(1, NCH // 2) as i:
                z_chunk(i, 0)
                z_chunk(i, 1)

            it = 0
            for s in range(2):
                nt = SEQ_NT[s]
                S = nt * P
                pe.wait_ge(s_rot, s + 1)
                for g in range(12):
                    G = 12 * s + g
                    if G >= 2:
                        pe.wait_ge(s_qTc, G - 1)
                    if G < 2:
                        pe.wait_ge(s_ntc, 2 * NT)
                    if s == 1 and g < 2:
                        pe.wait_ge(s_oTm, 8)
                    for t in range(nt):
                        src = zqk[:, t, g * P:(g + 1) * P] if g < 8 else zr[:, t, (g - 8) * P:(g - 7) * P]
                        mm = pe.transpose(ps[4 + g % 2][:, t * P:(t + 1) * P], src, ident)
                    mm.then_inc(s_qT, 1)

                def scores(n):
                    _, h, qt = ITS[n]
                    pair = 2 * (n % 2)
                    if n >= 2:
                        pe.wait_ge(s_ex, n - 1)
                    for c in range(2):
                        rows = slice(c * HD, (c + 1) * HD)
                        mm = pe.matmul(ps[pair + c][:, 0:S], qkT[rows, 0, h, qt * P:(qt + 1) * P],
                                       qkT[rows, 1, h, 0:S], start=True, stop=True)
                    mm.then_inc(s_sc, 1)

                pe.wait_ge(s_qTc, 12 * (s + 1))
                if s == 0:
                    pe.wait_ge(s_zev, NCH * NT)
                else:
                    pe.wait_ge(s_rm, 16)
                    pe.wait_ge(s_ryc, 4)
                scores(it)
                for k in range(H * nt):
                    n = it + k
                    if k + 1 < H * nt:
                        scores(n + 1)
                    _, h, qt = ITS[n]
                    pe.wait_ge(s_a, n + 1)
                    if n >= 2:
                        pe.wait_ge(s_aTc, n - 1)
                    for kt in range(nt):
                        mm = pe.transpose(ps[4 + n % 2][:, kt * P:(kt + 1) * P],
                                          att[n % 2][:, kt * P:(kt + 1) * P], ident)
                    mm.then_inc(s_aT, 1)
                    pe.wait_ge(s_aTc, n + 1)
                    if n >= 2:
                        pe.wait_ge(s_oc, n - 1)
                    for kt in range(nt):
                        mm = pe.matmul(ps[6 + n % 2][:, 0:VD], attT[n % 2][:, kt * P:(kt + 1) * P],
                                       zv[:, kt, h * VD:(h + 1) * VD], start=(kt == 0), stop=(kt == nt - 1))
                    mm.then_inc(s_o, 1)
                it += H * nt
                pe.wait_ge(s_ex, it)
                pe.wait_ge(s_oc, it)
                for h in range(H):
                    rows = slice((h % 2) * HD, (h % 2 + 1) * HD)
                    R = [0, 4 * 4][s] + h * nt
                    for kt in range(nt):
                        if h >= 1:
                            pe.wait_ge(s_rm, R - nt + kt + 1)
                        pe.matmul(ps[kt][:, 0:S], rqkT[rows, 1, h // 2, kt * P:(kt + 1) * P],
                                  rqkT[rows, 0, h // 2, 0:S], start=True, stop=True).then_inc(s_rs, 1)
                    pe.wait_ge(s_rm, R + nt)
                    if h >= 2:
                        pe.wait_ge(s_ryc, 4 * s + h - 1)
                    for qt in range(nt):
                        for kt in range(nt):
                            mm = pe.matmul(ps[6 + h % 2][:, qt * VD:(qt + 1) * VD],
                                           smk[:, kt, qt * P:(qt + 1) * P], zvr[:, kt, h * VD:(h + 1) * VD],
                                           start=(kt == 0), stop=(kt == nt - 1))
                    mm.then_inc(s_ry, 1)
                for b in range(2):
                    pe.wait_ge(s_on, 2 * s + b + 1)
                    if b == 0:
                        pe.wait_ge(s_aTc, it)
                    src = (oun, yun)[b]
                    for h in range(H):
                        O = 8 * s + 4 * b + h
                        if O >= 2:
                            pe.wait_ge(s_oTm, O - 1)
                        for t in range(nt):
                            mm = pe.transpose(ps[4 + h % 2][:, t * P:(t + 1) * P],
                                              src[:, t, h * VD:(h + 1) * VD], ident)
                        mm.then_inc(s_oT, 1)

            pe.wait_ge(s_oTh, 16)
            pe.wait_ge(s_oTl, 16)
            pe.wait_ge(s_ryc, 8)
            pe.wait_ge(s_rm, 24)
            for t in range(NT):
                for m in range(4):
                    n = 4 * t + m
                    if n >= 4:
                        pe.wait_ge(s_pm, n - 3)
                    if t == 0:
                        pe.wait_ge(s_lo, ZP + m + 1)
                    for h in range(H):
                        mm = split_mm(ps[n % 4][:, :], oTh[m % 2][:, h, t * P:(t + 1) * P],
                                      oTl[m % 2][:, h, t * P:(t + 1) * P], whi[m][:, h * 512:(h + 1) * 512],
                                      wlo[m][:, h * 512:(h + 1) * 512], h == 0, h == H - 1)
                    mm.then_inc(s_gs, 1)
            def merged_to_columns(t):
                pe.wait_ge(s_mgd, 2 * NT)
                for j in range(2):
                    n = 2 * t + j
                    if n >= 2:
                        pe.wait_ge(s_mTl, n - 1)
                    for c in range(4):
                        mm = pe.transpose(ps[4 + n % 2][:, c * P:(c + 1) * P], mg[:, t, 4 * j + c::KC], ident)
                    mm.then_inc(s_mT, 1)
            merged_to_columns(0)
            for t in range(NT):
                if t + 1 < NT:
                    merged_to_columns(t + 1)
                pe.wait_ge(s_mTl, 2 * t + 2)
                for n in range(2):
                    if t >= 1:
                        pe.wait_ge(s_x2, 2 * t + n - 1)
                    for j in range(2):
                        p = 2 * n + j
                        if t == 0:
                            pe.wait_ge(s_lo, ZP + 4 + p + 1)
                        for k in range(4):
                            c = 4 * j + k
                            mm = split_mm(ps[6 + n][:, :], mTh[t % 2][:, c, :], mTl[t % 2][:, c, :],
                                          whi[p][:, k * 512:(k + 1) * 512], wlo[p][:, k * 512:(k + 1) * 512],
                                          c == 0, c == KC - 1)
                        if t == NT - 1 and j == 0:
                            mm.then_inc(s_pe, 1)
                    mm.then_inc(s_w, 1)
            for t in range(NT):
                pe.wait_ge(s_rr, t + 1)
                for j in range(2):
                    n = 2 * t + j
                    if n >= 2:
                        pe.wait_ge(s_rTc, n - 1)
                    for c in range(4):
                        mm = pe.transpose(ps[n % 2][:, c * P:(c + 1) * P], rrow[t % 2][:, 4 * j + c::KC], ident)
                    mm.then_inc(s_rTm, 1)
                pe.wait_ge(s_rTc, 2 * t + 2)
                if t == 0:
                    pe.wait_ge(s_rp, 16 * 8)
                if t >= 1:
                    pe.wait_ge(s_rx, t)
                for c in range(KC):
                    mm = pe.matmul(ps[2][:, 0:NG + NE], rT[t % 2][:, c, :], wrt[:, c, :],
                                   start=(c == 0), stop=(c == KC - 1))
                mm.then_inc(s_lg, 1)
            pe.wait_ge(s_Ab, 1)
            for t in range(NT):
                pe.matmul(ps[3][:, t * NE:(t + 1) * NE], C("tri"), Ab[:, t, :], start=True, stop=(t == 0))
                for u in range(t):
                    pe.matmul(ps[3][:, t * NE:(t + 1) * NE], C("ones"), Ab[:, u, :], start=False, stop=(u == t - 1))
            for u in range(NT):
                mm = pe.matmul(ps[3][:, NT * NE:(NT + 1) * NE], C("ones"), Ab[:, u, :],
                               start=(u == 0), stop=(u == NT - 1))
            mm.then_inc(s_rk, 1)

            pe.wait_ge(s_nb, 1)
            nb = pe.value_load(nbi[0:1, 0:1], min_val=NE, max_val=NB)

            def x_to_columns(b):
                pe.wait_ge(s_gx, 16 * b + 16)
                for j in range(2):
                    for c in range(4):
                        mm = pe.transpose(ps[2 + j][:, c * P:(c + 1) * P], xg[:, 4 * j + c::KC], ident)
                    mm.then_inc(s_eT, 1)
            x_to_columns(0)
            pe.sem_inc(s_h1, 2)
            pe.sem_inc(s_hT, 1)
            pe.sem_inc(s_y, 1)
            with pe.Fori(0, nb) as b:
                pe.wait_ge(s_eTl, 2 * b + 2)
                for m in range(2):
                    for j in range(2):
                        q = 2 * m + j
                        pe.wait_ge(s_lo, 6 * b + (PRE + q + 1))
                        for k in range(4):
                            c = 4 * j + k
                            mm = split_mm(ps[m][:, :], eTh[:, c, :], eTl[:, c, :],
                                          whi[q % 3][:, k * 512:(k + 1) * 512], wlo[q % 3][:, k * 512:(k + 1) * 512],
                                          c == 0, c == KC - 1)
                        if j == 0:
                            mm.then_inc(s_pe, 1)
                    mm.then_inc(s_h1, 1)
                x_to_columns(b + 1)
                pe.wait_ge(s_h, b + 2)
                for c in range(4):
                    mm = pe.transpose(ps[4][:, c * P:(c + 1) * P], hh[:, c::4], ident)
                mm.then_inc(s_hT, 1)
                pe.wait_ge(s_hTl, b + 1)
                pe.wait_ge(s_yc, 2 * b + 2)
                for j in range(2):
                    q = 4 + j
                    pe.wait_ge(s_lo, 6 * b + (PRE + q + 1))
                    for n in range(2):
                        for k in range(2):
                            c = 2 * j + k
                            w = slice(k * D + n * 512, k * D + n * 512 + 512)
                            mm = split_mm(ps[6 + n][:, :], hTh[:, c, :], hTl[:, c, :],
                                          whi[q % 3][:, w], wlo[q % 3][:, w], c == 0, c == 3)
                    if j == 0:
                        mm.then_inc(s_pe, 1)
                mm.then_inc(s_y, 1)

        @block.scalar
        def _(act):
            def hi_piece(slot_raw, use, slot, freed=None):
                act.wait_ge(s_raw[slot_raw], 16 * use)
                if freed is not None:
                    act.wait_ge(*freed)
                act.activation(whi[slot][:, :], raw[slot_raw][:, :], ACT.Copy).then_inc(s_hi, 1)

            for t in range(NT):
                act.wait_ge(s_x, 16 * NT)
                if t >= 1:
                    act.wait_ge(s_sq, t)
                act.activation(junk[:, :], xin[:, t, :], ACT.Square, accum_out=ssq[:, t:t + 1]).then_inc(s_sq, 1)
            act.wait_ge(s_rstd1, 1)
            for t in range(NT):
                act.mul(xin[:, t, :], xin[:, t, :], rstd[:, t:t + 1]).then_inc(s_xs, 1)
            for q in range(2):
                hi_piece(q, 1, q)
            for n in range(2 * NT):
                act.wait_ge(s_ntc, n + 1)
                act.activation(xTh[:, 4 * (n % 2):4 * (n % 2) + 4, (n // 2) * P:(n // 2 + 1) * P],
                               junk[:, (n % 2) * 512:(n % 2 + 1) * 512].rearrange("p (c k) -> p c k", k=P),
                               ACT.Copy).then_inc(s_nth, 1)

            def z_out(i, m, t):
                n = 12 * i + 6 * m + t
                k = (6 * m + t) % 4
                act.wait_ge(s_zmm, n + 1)
                if not (isinstance(i, int) and i == 0 and 6 * m + t < 4):
                    act.wait_ge(s_zst[k], 48 * i + 16 * ((6 * m + t) // 4))
                act.activation(zst[k][:, :], ps[k][:, :], ACT.Copy).then_inc(s_zev, 1)

            def z_step(i, last=False):
                first = isinstance(i, int) and i == 0
                for m in range(2):
                    for t in range(NT):
                        z_out(i, m, t)
                        if t in (0, 2):
                            j = t // 2
                            if m == 0:
                                hi_piece(2 + j, i + 1, 2 + j,
                                         None if first else (s_zmm, 12 * i) if j else (s_pe, 2 * i))
                            elif not last:
                                hi_piece(j, i + 2, j, (s_zmm, 12 * i + 6) if j else (s_pe, 2 * i + 1))
            z_step(0)
            with act.Fori(1, NCH // 2 - 1) as i:
                z_step(i)
            z_step(NCH // 2 - 1, last=True)

            act.wait_ge(s_lame, 1)
            act.activation(lamv[:, 2:4], lamv[:, 0:2], ACT.Exp).then_inc(s_lame, 1)
            act.activation(decay[:, :], decay[:, :], ACT.Exp).then_inc(s_decay, 1)
            act.wait_ge(s_warg, 1)
            act.activation(wdec[:, :, :], wdec[:, :, :], ACT.Exp).then_inc(s_wexp, 1)

            it = 0
            for s in range(2):
                nt = SEQ_NT[s]
                S = nt * P
                for g in range(12):
                    act.wait_ge(s_qT, 12 * s + g + 1)
                    dst = qkT[:, g // 4, g % 4, 0:S] if g < 8 else rqkT[:, (g - 8) // 2, g % 2, 0:S]
                    act.activation(dst, ps[4 + g % 2][:, 0:S], ACT.Copy).then_inc(s_qTc, 1)

                def exps(n):
                    act.wait_ge(s_mx, n + 1)
                    if n >= 2:
                        act.wait_ge(s_a, n - 1)
                    if n == it:
                        act.wait_ge(s_qT, 12 * s + 8)
                    for c in range(2):
                        e = act.activation(prob[n % 2][:, c, 0:S], ps[2 * (n % 2) + c][:, 0:S], ACT.Exp,
                                           bias=nm[:, n % 2, c:c + 1], scale=HD ** -0.5,
                                           accum_out=sume[:, n % 2, c:c + 1])
                    e.then_inc(s_ex, 1)
                exps(it)
                for k in range(H * nt):
                    n = it + k
                    if k + 1 < H * nt:
                        exps(n + 1)
                    act.wait_ge(s_aT, n + 1)
                    if n >= 2:
                        act.wait_ge(s_o, n - 1)
                    act.activation(attT[n % 2][:, 0:S], ps[4 + n % 2][:, 0:S], ACT.Copy).then_inc(s_aTc, 1)
                it += H * nt
                act.wait_ge(s_zl[s], 16 * 5)
                act.wait_ge(s_rm, [16, 24][s])
                act.wait_ge(s_ry, 4 * (s + 1))
                act.activation(smk[:, 0:nt, :], zgr[:, 0:nt, :], ACT.Sigmoid).then_inc(s_sig, 1)
                for o in range(8):
                    O = 8 * s + o
                    b, h = o // 4, o % 4
                    act.wait_ge(s_oTm, O + 1)
                    act.activation(oTh[b][:, h, SEQ_T0[s] * P:SEQ_T0[s] * P + S], otm[O % 2][:, 0:S],
                                   ACT.Copy).then_inc(s_oTh, 1)

            for p in range(4):
                if p == 0:
                    act.wait_ge(s_oTl, 16)
                hi_piece((4 + p) % RAWS, [1, 1, 6, 6][p], p)
            for t in range(NT):
                act.wait_ge(s_gl, 16 * (t + 1))
                act.activation(gat[:, :], gat[:, :], ACT.Sigmoid).then_inc(s_sgm, 1)
            for p in range(4, 8):
                hi_piece((4 + p) % RAWS, [6, 6, 2, 2][p - 4], p % 4,
                         (s_gs, 4 * (NT - 1) + p - 3))
            for n in range(2 * NT):
                t, j = n // 2, n % 2
                act.wait_ge(s_mT, n + 1)
                if t >= 2:
                    act.wait_ge(s_w, 2 * (t - 1))
                act.activation(mTh[t % 2][:, 4 * j:4 * j + 4, :].rearrange("p c k -> p (c k)"),
                               ps[4 + n % 2][:, :], ACT.Copy).then_inc(s_mTh, 1)
            for t in range(NT):
                act.wait_ge(s_x2, 2 * NT)
                act.activation(rrow[1][:, :], x2[:, t, :], ACT.Square, accum_out=ssq[:, t:t + 1]).then_inc(s_sq2, 1)
                act.wait_ge(s_sq2, t + 1)
            for n in range(2 * NT):
                t, j = n // 2, n % 2
                act.wait_ge(s_rTm, n + 1)
                if t >= 2:
                    act.wait_ge(s_lg, t - 1)
                act.activation(rT[t % 2][:, 4 * j:4 * j + 4, :].rearrange("p c k -> p (c k)"),
                               ps[n % 2][:, :], ACT.Copy).then_inc(s_rTc, 1)
            act.wait_ge(s_re, 1)
            act.activation(gq[:, 1, :, :], gq[:, 0, :, :], ACT.Exp).then_inc(s_re, 1)
            act.activation(v6[:, 3, :], v6[:, 2, :], ACT.Exp).then_inc(s_re, 1)

            act.wait_ge(s_nb, 1)
            nb = act.value_load(nbi[0:1, 0:1], min_val=NE, max_val=NB)

            def x_hi(n):
                for j in range(2):
                    act.wait_ge(s_eT, n * 2 + (j + 1))
                    act.activation(eTh[:, 4 * j:4 * j + 4, :].rearrange("p c k -> p (c k)"), ps[2 + j][:, :],
                                   ACT.Copy).then_inc(s_eTh, 1)
            def e_hi(b, j):
                freed = ((s_h1, 2 * b + 2), (s_pe, 3 * b + (NCH + 2)), (s_y, b + 1),
                         (s_pe, 3 * b + (NCH + 3)), (s_h1, 2 * b + 3), (s_pe, 3 * b + (NCH + 4)))[j]
                hi_piece(j, b + (7 if j < 4 else 3), j % 3, freed)
            x_hi(0)
            act.wait_ge(s_yz, 16 * NOV)
            act.sem_inc(s_ys, 16)
            act.sem_inc(s_yc, 2)
            with act.Fori(0, nb) as b:
                for j in range(4):
                    e_hi(b, j)
                act.wait_ge(s_h1, 2 * b + 3)
                act.wait_ge(s_h, b + 1)
                act.activation(sg[:, :], ps[0][:, :], ACT.Sigmoid).then_inc(s_sgm, 1)
                e_hi(b, 4)
                act.wait_ge(s_h1, 2 * b + 4)
                x_hi(b + 1)
                act.wait_ge(s_hT, b + 2)
                act.wait_ge(s_y, b + 1)
                act.activation(hTh[:, :, :].rearrange("p c k -> p (c k)"), ps[4][:, :], ACT.Copy).then_inc(s_hTh, 1)
                e_hi(b, 5)
                act.wait_ge(s_y, b + 2)
                act.wait_ge(s_ys, 16 * b + 16)
                for n in range(2):
                    act.activation(ystage[:, n * 512:(n + 1) * 512], ps[6 + n][:, :], ACT.Copy).then_inc(s_yc, 1)
                act.wait_ge(s_yc, 2 * b + 4)
                act.dma_start(y_d[bass.ds(b * CAP, CAP), :], ystage[:, :]).then_inc(s_ys, 16)

        @block.vector
        def _(dve):
            n_link = [0]

            def link(ins):
                n_link[0] += 1
                ins.then_inc(s_dv, 1)
                dve.wait_ge(s_dv, n_link[0])

            def lo_piece(slot_raw, slot, q):
                dve.wait_ge(s_hi, q)
                dve.tensor_tensor(wlo[slot][:, :], raw[slot_raw][:, :], whi[slot][:, :].bitcast(F32),
                                  ALU.subtract).then_inc(s_lo, 1)

            def rsqrt(out, v, w, n_mean, link):
                a, y = rs_a[:, 0:w], out
                link(dve.tensor_scalar(v, v, 1.0 / n_mean, EPS, ALU.mult, ALU.add))
                link(dve.tensor_scalar(a.bitcast(I32), v.bitcast(I32), 1, None, ALU.arith_shift_right))
                link(dve.tensor_scalar(y.bitcast(I32), a.bitcast(I32), -1.0, float(0x5f3759df), ALU.mult, ALU.add))
                for _ in range(4):
                    link(dve.tensor_tensor(a, y, y, ALU.mult))
                    link(dve.tensor_tensor(a, a, v, ALU.mult))
                    link(dve.tensor_scalar(a, a, -0.5, 1.5, ALU.mult, ALU.add))
                    link(dve.tensor_tensor(y, y, a, ALU.mult))

            dve.wait_ge(s_sq, NT)
            rsqrt(rstd[:, 0:NT], ssq[:, 0:NT], NT, D, link)
            dve.wait_ge(s_par, 16 * 8)
            dve.sem_inc(s_rstd1, 1)
            for n in range(2 * NT):
                t, j = n // 2, n % 2
                dve.wait_ge(s_nT, n + 1)
                if n >= 2:
                    dve.wait_ge(s_ntl, n - 1)
                    dve.wait_ge(s_nth, n - 1)
                half = junk[:, j * 512:(j + 1) * 512].rearrange("p (c k) -> p c k", k=P)
                dve.tensor_tensor(half, ps[4 + n % 4][:, :].rearrange("p (c k) -> p c k", k=P),
                                  gn1[:, 4 * j:4 * j + 4].unsqueeze(2).to_broadcast([P, 4, P]),
                                  ALU.mult).then_inc(s_ntc, 1)
                dve.wait_ge(s_nth, n + 1)
                sl = (slice(None), slice(4 * j, 4 * j + 4), slice(t * P, (t + 1) * P))
                dve.tensor_tensor(xTl[sl], half, xTh[sl].bitcast(F32), ALU.subtract).then_inc(s_ntl, 1)
            with dve.Fori(0, NCH // 2) as i:
                for j in range(4):
                    lo_piece(j, j, 4 * i + (j + 1))

            for k in range(2):
                link(dve.tensor_tensor_reduce(out=lamr[:, 2 * k, :], in0=lamr[:, 2 * k, :], in1=lamr[:, 2 * k + 1, :],
                                              scale=1.0, scalar=0.0, op0=ALU.mult, op1=ALU.add,
                                              accum_out=lamv[:, k:k + 1]))
            dve.sem_inc(s_lame, 1)
            dve.wait_ge(s_lame, 2)
            link(dve.tensor_tensor(lamv[:, 0:1], lamv[:, 3:4], lamv[:, 2:3], ALU.subtract))
            link(dve.tensor_scalar(lamv[:, 0:1], lamv[:, 0:1], -LAM_INIT, None, ALU.add))
            link(dve.tensor_scalar(gsub[:, :], gsub[:, :], 1.0 - LAM_INIT, None, ALU.mult))
            dve.wait_ge(s_decay, 1)
            link(dve.tensor_scalar(decay[:, 0:4], decay[:, 0:4], -1.0, None, ALU.mult))
            rt = rtmp[:, 0, 0:RELW]
            dve.wait_ge(s_zev, NCH * NT)
            for k in range(4):
                dve.wait_ge(s_zst[k], 16 * NCH * NT // 4)
            dve.wait_ge(s_yz, 16 * NOV)
            for h in range(H):
                link(dve.tensor_scalar(wdec[:, h, :], C("rel"), 0.0, decay[:, h:h + 1], ALU.max, ALU.mult))
                link(dve.tensor_scalar(rt, C("rel"), 0.0, decay[:, 4 + h:5 + h], ALU.min, ALU.mult))
                link(dve.tensor_tensor(wdec[:, h, :], wdec[:, h, :], rt, ALU.add))
            dve.sem_inc(s_warg, 1)

            it = 0
            for s in range(2):
                nt = SEQ_NT[s]
                S = nt * P
                dve.wait_ge(s_zl[s], 16 * 5)
                if s == 1:
                    dve.wait_ge(s_oT, 8)
                for z, groups, half, cn, sn in ((zqk, 16, 8, "cosA", "sinA"), (zr, 8, 32, "cosR", "sinR")):
                    for t in range(nt):
                        v = z[:, t, :].rearrange("p (g d) -> p g d", d=HD)
                        x1, x2_ = v[:, :, 0:half], v[:, :, half:2 * half]
                        cs = C(cn)[:, t * half:(t + 1) * half].unsqueeze(1).to_broadcast([P, groups, half])
                        sn_ = C(sn)[:, t * half:(t + 1) * half].unsqueeze(1).to_broadcast([P, groups, half])
                        w = groups * half
                        r = [rtmp[:, k, 0:w].rearrange("p (g d) -> p g d", d=half) for k in range(4)]
                        dve.tensor_tensor(r[0], x1, cs, ALU.mult)
                        dve.tensor_tensor(r[1], x2_, sn_, ALU.mult)
                        dve.tensor_tensor(r[2], x2_, cs, ALU.mult)
                        link(dve.tensor_tensor(r[3], x1, sn_, ALU.mult))
                        dve.tensor_tensor(x1, r[0], r[1], ALU.subtract)
                        link(dve.tensor_tensor(x2_, r[2], r[3], ALU.add))
                dve.sem_inc(s_rot, 1)
                if s == 0:
                    dve.wait_ge(s_wexp, 1)

                def maxes(n):
                    b = 2 * (n % 2)
                    dve.wait_ge(s_sc, n + 1)
                    dve.tensor_reduce(mx[:, n % 2, 0:1], ps[b][:, 0:S], AX.X, ALU.max)
                    link(dve.tensor_reduce(mx[:, n % 2, 1:2], ps[b + 1][:, 0:S], AX.X, ALU.max))
                    dve.tensor_scalar(nm[:, n % 2, :], mx[:, n % 2, :], -HD ** -0.5, None,
                                      ALU.mult).then_inc(s_mx, 1)
                maxes(it)
                for k in range(H * nt):
                    n = it + k
                    if k + 1 < H * nt:
                        maxes(n + 1)
                    _, h, qt = ITS[n]
                    dve.wait_ge(s_ex, n + 1)
                    if n >= 2:
                        dve.wait_ge(s_aT, n - 1)
                    link(dve.reciprocal(rc[:, n % 2, :], sume[:, n % 2, :]))
                    link(dve.tensor_tensor(rc[:, n % 2, 1:2], rc[:, n % 2, 1:2], lamv[:, 0:1], ALU.mult))
                    pr = prob[n % 2]
                    link(dve.tensor_scalar(pr[:, 1, 0:S], pr[:, 1, 0:S], rc[:, n % 2, 1:2], None, ALU.mult))
                    dve.scalar_tensor_tensor(out=att[n % 2][:, 0:S], in0=pr[:, 0, 0:S], scalar=rc[:, n % 2, 0:1],
                                             in1=pr[:, 1, 0:S], op0=ALU.mult, op1=ALU.add).then_inc(s_a, 1)
                    if k >= 1:
                        _, h0, q0 = ITS[n - 1]
                        dve.wait_ge(s_o, n)
                        dve.tensor_copy(oun[:, q0, h0 * VD:(h0 + 1) * VD], ps[6 + (n - 1) % 2][:, 0:VD]).then_inc(s_oc, 1)
                it += H * nt
                _, h0, q0 = ITS[it - 1]
                dve.wait_ge(s_o, it)
                dve.tensor_copy(oun[:, q0, h0 * VD:(h0 + 1) * VD], ps[6 + (it - 1) % 2][:, 0:VD]).then_inc(s_oc, 1)
                for h in range(H):
                    R = [0, 16][s] + h * nt
                    for kt in range(nt):
                        dve.wait_ge(s_rs, R + kt + 1)
                        if kt == 0:
                            if h == 0:
                                dve.wait_ge(s_qT, 12 * (s + 1))
                            else:
                                dve.wait_ge(s_ry, 4 * s + h)
                        dve.scalar_tensor_tensor(out=smk[:, kt, 0:S], in0=ps[kt][:, 0:S], scalar=HD ** -0.5,
                                                 in1=wdec[:, h, (3 - kt) * P:(3 - kt) * P + S],
                                                 op0=ALU.mult, op1=ALU.mult).then_inc(s_rm, 1)
                    dve.wait_ge(s_ry, 4 * s + h + 1)
                    dve.tensor_copy(yun[:, 0:nt, h * VD:(h + 1) * VD],
                                    ps[6 + h % 2][:, 0:S].rearrange("p (t v) -> p t v", v=VD)).then_inc(s_ryc, 1)
                dve.wait_ge(s_oc, it)
                dve.wait_ge(s_ryc, 4 * (s + 1))
                for b, src in enumerate((oun, yun)):
                    w = 4 * nt
                    v = src[:, 0:nt, :]
                    link(dve.tensor_tensor(sqt[:, 0:nt, :], v, v, ALU.mult))
                    link(dve.tensor_reduce(ssq[:, 0:w], sqt[:, 0:nt, :].rearrange("p t (h v) -> p (t h) v", v=VD),
                                           AX.X, ALU.add))
                    rsqrt(rstd[:, 0:w], ssq[:, 0:w], w, VD, link)
                    vg = v.rearrange("p t (h v) -> p (t h) v", v=VD)
                    o = dve.tensor_tensor(vg, vg, rstd[:, 0:w].unsqueeze(2).to_broadcast([P, w, VD]), ALU.mult)
                    if b == 1:
                        link(o)
                        dve.wait_ge(s_sig, s + 1)
                        link(dve.tensor_tensor(smk[:, 0:nt, :], smk[:, 0:nt, :], zgr[:, 0:nt, :], ALU.mult))
                        o = dve.tensor_tensor(v, v, smk[:, 0:nt, :], ALU.mult)
                    o.then_inc(s_on, 1)
                for o in range(8):
                    O = 8 * s + o
                    b, h = o // 4, o % 4
                    dve.wait_ge(s_oT, O + 1)
                    if O >= 2:
                        dve.wait_ge(s_oTh, O - 1)
                        dve.wait_ge(s_oTl, O - 1)
                    if b == 0:
                        dve.tensor_scalar(otm[O % 2][:, 0:S], ps[4 + h % 2][:, 0:S], gsub[:, 0:1], None,
                                          ALU.mult).then_inc(s_oTm, 1)
                    else:
                        dve.tensor_copy(otm[O % 2][:, 0:S], ps[4 + h % 2][:, 0:S]).then_inc(s_oTm, 1)
                    dve.wait_ge(s_oTh, O + 1)
                    cols = slice(SEQ_T0[s] * P, SEQ_T0[s] * P + S)
                    dve.tensor_tensor(oTl[b][:, h, cols], otm[O % 2][:, 0:S], oTh[b][:, h, cols].bitcast(F32),
                                      ALU.subtract).then_inc(s_oTl, 1)

            for p in range(4):
                lo_piece((4 + p) % RAWS, p, ZP + p + 1)
            for t in range(NT):
                dve.wait_ge(s_sgm, t + 1)
                for m in range(4):
                    n = 4 * t + m
                    g = gat[:, (m % 2) * D + (m // 2) * 512:(m % 2) * D + (m // 2) * 512 + 512]
                    dst = mg[:, t, (m // 2) * 512:(m // 2) * 512 + 512]
                    dve.wait_ge(s_gs, n + 1)
                    if m % 2 == 0:
                        dve.wait_ge(s_pm, n)
                        dve.tensor_tensor(dst, ps[n % 4][:, :], g, ALU.mult).then_inc(s_pm, 1)
                    else:
                        k = 2 * t + m // 2
                        if k >= 2:
                            dve.wait_ge(s_mgd, k - 1)
                        dve.tensor_tensor(prd[k % 2][:, :], ps[n % 4][:, :], g, ALU.mult).then_inc(s_pm, 1)
                        dve.wait_ge(s_pm, n + 1)
                        dve.tensor_tensor(dst, dst, prd[k % 2][:, :], ALU.add).then_inc(s_mgd, 1)
            for p in range(4, 8):
                lo_piece((4 + p) % RAWS, p % 4, ZP + p + 1)
            def merged_lo(t):
                for j in range(2):
                    n = 2 * t + j
                    dve.wait_ge(s_mTh, n + 1)
                    dve.tensor_tensor(mTl[t % 2][:, 4 * j:4 * j + 4, :].rearrange("p c k -> p (c k)"),
                                      ps[4 + n % 2][:, :],
                                      mTh[t % 2][:, 4 * j:4 * j + 4, :].rearrange("p c k -> p (c k)").bitcast(F32),
                                      ALU.subtract).then_inc(s_mTl, 1)
            merged_lo(0)
            for t in range(NT):
                if t + 1 < NT:
                    merged_lo(t + 1)
                dve.wait_ge(s_xr, 16 * (t + 1))
                for n in range(2):
                    dve.wait_ge(s_w, 2 * t + n + 1)
                    dve.tensor_tensor(x2[:, t, n * 512:(n + 1) * 512], ps[6 + n][:, :],
                                      xres[:, n * 512:(n + 1) * 512], ALU.add).then_inc(s_x2, 1)
            dve.wait_ge(s_sq2, NT)
            rsqrt(rstd[:, 0:NT], ssq[:, 0:NT], NT, D, link)
            dve.wait_ge(s_rp, 16 * 8)
            for t in range(NT):
                if t >= 2:
                    dve.wait_ge(s_rst[t % 2], 16 * (t // 2))
                    dve.wait_ge(s_rTm, 2 * (t - 1))
                dve.scalar_tensor_tensor(out=rrow[t % 2][:, :], in0=x2[:, t, :], scalar=rstd[:, t:t + 1],
                                         in1=g2[:, :], op0=ALU.mult, op1=ALU.mult).then_inc(s_rr, 1)
                if t >= 1:
                    dve.wait_ge(s_lg, t)
                    dve.tensor_tensor(lg[:, t - 1, :], ps[2][:, 0:NG + NE], brt[:, :], ALU.add).then_inc(s_rx, 1)
            dve.wait_ge(s_lg, NT)
            dve.tensor_tensor(lg[:, NT - 1, :], ps[2][:, 0:NG + NE], brt[:, :], ALU.add).then_inc(s_rx, 1)
            dve.wait_ge(s_rx, NT)

            def b4(v):
                return v.unsqueeze(2).to_broadcast([P, NT, NG])

            def b32(v):
                return v.unsqueeze(2).to_broadcast([P, NT, NE])

            grp = lg[:, :, 0:NG]
            link(dve.tensor_reduce(v6[:, 0, :], grp, AX.X, ALU.max))
            link(dve.tensor_tensor(gq[:, 0, :, :], grp, b4(v6[:, 0, :]), ALU.subtract))
            link(dve.tensor_scalar(gq[:, 2, :, :], gq[:, 0, :, :], 0.0, None, ALU.is_equal))
            link(dve.tensor_tensor(gq[:, 2, :, :], gq[:, 2, :, :],
                                   C("grank").unsqueeze(1).to_broadcast([P, NT, NG]), ALU.mult))
            link(dve.tensor_reduce(v6[:, 1, :], gq[:, 2, :, :], AX.X, ALU.max))
            link(dve.tensor_tensor(gq[:, 3, :, :], gq[:, 2, :, :], b4(v6[:, 1, :]), ALU.is_equal))

            def pick(out, vals, top):
                link(dve.tensor_reduce(top, vals, AX.X, ALU.max))
                link(dve.tensor_tensor(t1[:, :, :], vals, b32(top), ALU.is_equal))
                link(dve.tensor_tensor(t1[:, :, :], t1[:, :, :], C("erank").unsqueeze(1).to_broadcast([P, NT, NE]),
                                       ALU.mult))
                link(dve.tensor_reduce(v6[:, 4, :], t1[:, :, :], AX.X, ALU.max))
                link(dve.tensor_tensor(out, t1[:, :, :], b32(v6[:, 4, :]), ALU.is_equal))

            BIG = 3.0e38
            for t in range(NT):
                oh = gq[:, 3, t, :].unsqueeze(2).to_broadcast([P, NG, EPG])
                link(dve.tensor_tensor(sel[:, t, :].rearrange("p (g e) -> p g e", e=EPG),
                                       lg[:, t, NG:].rearrange("p (g e) -> p g e", e=EPG), oh, ALU.mult))
                link(dve.tensor_scalar(t2[:, t, :].rearrange("p (g e) -> p g e", e=EPG), oh, -1.0, BIG,
                                       ALU.add, ALU.mult))
            link(dve.tensor_tensor(sel[:, :, :], sel[:, :, :], t2[:, :, :], ALU.add))
            pick(A1[:, :, :], sel[:, :, :], v6[:, 5, :])
            link(dve.tensor_scalar(t2[:, :, :], A1[:, :, :], -BIG, None, ALU.mult))
            link(dve.tensor_tensor(sel[:, :, :], sel[:, :, :], t2[:, :, :], ALU.add))
            pick(A2[:, :, :], sel[:, :, :], v6[:, 6, :])
            link(dve.tensor_tensor(v6[:, 2, :], v6[:, 6, :], v6[:, 5, :], ALU.subtract))
            dve.tensor_tensor(Ab[:, :, :], A1[:, :, :], A2[:, :, :], ALU.add).then_inc(s_Ab, 1)
            dve.sem_inc(s_re, 1)
            dve.wait_ge(s_re, 3)
            link(dve.tensor_reduce(v6[:, 7, :], gq[:, 1, :, :], AX.X, ALU.add))
            link(dve.tensor_scalar(v6[:, 8, :], v6[:, 3, :], 1.0, None, ALU.add))
            link(dve.tensor_tensor(v6[:, 7, :], v6[:, 7, :], v6[:, 8, :], ALU.mult))
            link(dve.reciprocal(gates[:, 0, :], v6[:, 7, :]))
            link(dve.tensor_tensor(gates[:, 1, :], gates[:, 0, :], v6[:, 3, :], ALU.mult))
            dve.wait_ge(s_rk, 1)
            cnt = ps[3][:, NT * NE:(NT + 1) * NE]
            link(dve.tensor_scalar(nov[:, 0, :], cnt, float(CAP), None, ALU.is_gt))
            for j in range(2, MAXB):
                link(dve.tensor_scalar(nov[:, 1, :], cnt, float(CAP * j), None, ALU.is_gt))
                link(dve.tensor_tensor(nov[:, 0, :], nov[:, 0, :], nov[:, 1, :], ALU.add))
            link(dve.tensor_copy(nov[:, 1, :], nov[:, 0, :]))
            a, d = 1, 1
            while d < NE:
                link(dve.tensor_copy(nov[:, 3 - a, 0:d], nov[:, a, 0:d]))
                link(dve.tensor_tensor(nov[:, 3 - a, d:NE], nov[:, a, d:NE], nov[:, a, 0:NE - d], ALU.add))
                a, d = 3 - a, 2 * d
            incl = nov[:, a, :]
            link(dve.tensor_tensor(ovb[:, :], incl, nov[:, 0, :], ALU.subtract))
            link(dve.tensor_scalar(ovb[:, :], ovb[:, :], float(CAP), float((NE - 1) * CAP), ALU.mult, ALU.add))
            link(dve.tensor_tensor(ovb[:, :], ovb[:, :], C("e128"), ALU.subtract))
            rank = ps[3][:, 0:NT * NE].rearrange("p (t e) -> p t e", e=NE)
            link(dve.tensor_scalar(t1[:, :, :], rank, float(CAP), None, ALU.is_ge))
            link(dve.tensor_tensor(t1[:, :, :], t1[:, :, :], ovb[:, :].unsqueeze(1).to_broadcast([P, NT, NE]), ALU.mult))
            link(dve.tensor_tensor(t1[:, :, :], t1[:, :, :], rank, ALU.add))
            link(dve.tensor_tensor(t1[:, :, :], t1[:, :, :], C("e128").unsqueeze(1).to_broadcast([P, NT, NE]), ALU.add))
            for k, Ak in enumerate((A1, A2)):
                link(dve.tensor_tensor(t2[:, :, :], t1[:, :, :], Ak[:, :, :], ALU.mult))
                link(dve.tensor_reduce(slotf[:, k, :], t2[:, :, :], AX.X, ALU.add))
            link(dve.tensor_copy(sloti[:, :, :], slotf[:, :, :]))
            link(dve.tensor_copy(toki[:, :], C("tok")))
            link(dve.tensor_tensor(bt[:, :, :], nov[0:1, a, :].unsqueeze(1).to_broadcast([1, NOV, NE]),
                                   C("miota")[0:1, :].unsqueeze(2).to_broadcast([1, NOV, NE]), ALU.is_le))
            link(dve.tensor_reduce(bts[:, :], bt[:, :, :], AX.X, ALU.add))
            link(dve.tensor_scalar(nbi[:, 1:1 + NOV], bts[:, :], float(NE - 1), None, ALU.min))
            link(dve.tensor_scalar(nbi[:, 0:1], nov[0:1, a, NE - 1:NE], float(NE), None, ALU.add))
            dve.sem_inc(s_slot, 1)
            dve.sem_inc(s_nb, 1)

            nb = dve.value_load(nbi[0:1, 0:1], min_val=NE, max_val=NB)

            def x_lo(n):
                for j in range(2):
                    dve.wait_ge(s_eTh, n * 2 + (j + 1))
                    dve.tensor_tensor(eTl[:, 4 * j:4 * j + 4, :].rearrange("p c k -> p (c k)"), ps[2 + j][:, :],
                                      eTh[:, 4 * j:4 * j + 4, :].rearrange("p c k -> p (c k)").bitcast(F32),
                                      ALU.subtract).then_inc(s_eTl, 1)

            def e_lo(b, j):
                lo_piece(j, j % 3, 6 * b + (PRE + j + 1))
            x_lo(0)
            dve.sem_inc(s_h, 1)
            with dve.Fori(0, nb) as b:
                for j in range(4):
                    e_lo(b, j)
                dve.wait_ge(s_sgm, b + (NT + 1))
                dve.wait_ge(s_hT, b + 1)
                dve.tensor_tensor(hh[:, :], ps[0][:, :], sg[:, :], ALU.mult).then_inc(s_ix, 1)
                dve.wait_ge(s_ix, b + 1)
                dve.wait_ge(s_h1, 2 * b + 4)
                dve.tensor_tensor(hh[:, :], ps[1][:, :], hh[:, :], ALU.mult).then_inc(s_h, 1)
                e_lo(b, 4)
                x_lo(b + 1)
                dve.wait_ge(s_hTh, b + 1)
                dve.tensor_tensor(hTl[:, :, :].rearrange("p c k -> p (c k)"), ps[4][:, :],
                                  hTh[:, :, :].rearrange("p c k -> p (c k)").bitcast(F32),
                                  ALU.subtract).then_inc(s_hTl, 1)
                e_lo(b, 5)
            dve.wait_ge(s_gf, 16)
            for t in range(NT):
                k = t % 2
                dve.wait_ge(s_g1[k], 32 * (t // 2 + 1))
                for m in range(2):
                    link(dve.scalar_tensor_tensor(out=x2[:, t, :], in0=ya[k][m][:, :], scalar=gates[:, m, t:t + 1],
                                                  in1=x2[:, t, :], op0=ALU.mult, op1=ALU.add))
                link(dve.tensor_tensor_reduce(out=fj[:, :], in0=x2[:, t, :], in1=x2[:, t, :], scale=1.0, scalar=0.0,
                                              op0=ALU.mult, op1=ALU.add, accum_out=ssq[:, 0:1]))
                rsqrt(rstd[:, 0:1], ssq[:, 0:1], 1, D, link)
                if t >= 2:
                    dve.wait_ge(s_out[t % 2], 16 * (t // 2))
                dve.scalar_tensor_tensor(out=yo[k][:, :], in0=x2[:, t, :], scalar=rstd[:, 0:1],
                                         in1=gf[:, :], op0=ALU.mult, op1=ALU.mult).then_inc(s_yf, 1)

        @block.gpsimd
        def _(pool):
            pool.memset(zrow[:, :], 0.0).then_inc(s_zr, 1)
            pool.wait_ge(s_zr, 1)
            for b in range(NE, NB):
                pool.dma_start(y_d[b * CAP:(b + 1) * CAP, :].rearrange("p (r c) -> p r c", c=256),
                               zrow[:, :].unsqueeze(1).to_broadcast([P, D // 256, 256])).then_inc(s_yz, 16)
            def z_store(i, u):
                pool.wait_ge(s_zev, 12 * i + (u + 1))
                pool.dma_start(z_d[(u % 6) * P:(u % 6 + 1) * P, bass.ds(i * 1024 + (u // 6) * 512, 512)],
                               zst[u % 4][:, :]).then_inc(s_zst[u % 4], 16)
            with pool.Fori(0, NCH // 2) as i:
                for u in range(12):
                    z_store(i, u)
            for t in range(NT):
                pool.wait_ge(s_rr, t + 1)
                pool.dma_start(xn_d[t * P:(t + 1) * P, :], rrow[t % 2][:, :]).then_inc(s_rst[t % 2], 16)
            pool.memset(zini[:, :], 0).then_inc(s_zi, 1)
            pool.wait_ge(s_zi, 1)
            pool.dma_start(st_d.rearrange("(p b) o -> p (b o)", b=NB + 1), zini[:, :]).then_inc(s_zt, 16)
            pool.wait_ge(s_zt, 16)
            pool.wait_ge(s_slot, 1)
            for t in range(NT):
                for k in range(2):
                    pool.indirect_dma_start(out=st_d, out_offset=bass.IndirectOffsetOnAxis(ap=sloti[:, k, t:t + 1], axis=0),
                                            in_=toki[:, t:t + 1], in_offset=None).then_inc(s_sct, 16)
            pool.wait_ge(s_sct, 16 * 2 * NT)
            for k in range(2):
                pool.wait_ge(s_rst[k], 16 * NT // 2)
            pool.wait_ge(s_nb, 1)
            nb = pool.value_load(nbi[0:1, 0:1], min_val=NE, max_val=NB)

            def gather(b, n):
                pool.dma_start(idxb[:, :], st_d[bass.ds(b * CAP, CAP), :]).then_inc(s_zt, 16)
                pool.wait_ge(s_zt, 16 * n + 32)
                pool.sem_inc(s_idx, 1)
                pool.indirect_dma_start(out=xg[:, :], out_offset=None, in_=xn_d,
                                        in_offset=bass.IndirectOffsetOnAxis(ap=idxb[:, 0:1], axis=0)).then_inc(s_gx, 16)
            gather(0, 0)
            with pool.Fori(0, nb) as b:
                pool.wait_ge(s_eT, 2 * b + 2)
                pool.wait_ge(s_gx, 16 * b + 16)
                bn = pool.snap(b + 1)
                gather(bn, bn)
            pool.wait_ge(s_ys, 16 * nb + 16)
            pool.wait_ge(s_gx, 16 * nb + 16)
            pool.sem_inc(s_md, 1)
            for t in range(NT):
                if t >= 2:
                    pool.wait_ge(s_yf, t - 1)
                for k in range(2):
                    pool.indirect_dma_start(out=ya[t % 2][k][:, :], out_offset=None, in_=y_d,
                                            in_offset=bass.IndirectOffsetOnAxis(ap=sloti[:, k, t:t + 1], axis=0)
                                            ).then_inc(s_g1[t % 2], 16)


_INS = ['x_prompt', 'x_sample', 'attn_norm_g', 'w_in', 'lam_q1', 'lam_k1', 'lam_q2', 'lam_k2', 'subln_g',
        'ret_decay_f', 'ret_decay_b', 'w_pa', 'w_pb', 'w_out', 'ffn_norm_g', 'w_rg', 'b_rg', 'w_re', 'b_re',
        'w1', 'w3', 'w2', 'final_norm_g']
_OUTS = [('y_prompt', (1, 512, D)), ('y_sample', (1, 256, D))]


def kernel(**inputs):
    import numpy as _np
    import concourse.bacc as _bacc
    from concourse import mybir as _mybir
    from concourse.bass_utils import run_bass_kernel_spmd as _run

    nc = _bacc.Bacc("TRN2", target_bir_lowering=False, num_devices=1)
    arrays, aps = {}, {}
    for name in _INS + ["consts"]:
        a = constants() if name == "consts" else _np.ascontiguousarray(inputs[name])
        arrays[f"in_{name}"] = a
        aps[name] = nc.dram_tensor(f"in_{name}", a.shape, _mybir.dt.from_np(a.dtype), kind="ExternalInput").ap()
    for name, shape in _OUTS:
        aps[name] = nc.dram_tensor(f"out_{name}", shape, _mybir.dt.float32, kind="ExternalOutput").ap()
    hybrid_layer(nc, aps)
    r = _run(nc, [arrays], core_ids=[0])
    return tuple(r.results[0][f"out_{name}"] for name, _ in _OUTS)
```

```python
from contextlib import ExitStack

import concourse.bass as bass
from concourse import mybir

F32 = mybir.dt.float32
F32R = mybir.dt.float32r
I32 = mybir.dt.int32
U32 = mybir.dt.uint32
ALU = mybir.AluOpType
ACT = mybir.ActivationFunctionType
AX = mybir.AxisListType

P = 128
D = 1024
KC = D // P
SEQS = (512, 256)
T = sum(SEQS)
NT = T // P
H = 4
HD = 64
VD = 128
D_IN = 5120
NCH = D_IN // 512
C_Q, C_V, C_R, C_VR, C_GR, C_GA, C_GB = 0, 1024, 1536, 2048, 2560, 3072, 4096
NG, EPG = 4, 8
NE = NG * EPG
FF = 512
CAP = 128
MAXB = T // CAP
NOV = (2 * T) // (CAP + 1)
NB = NE + NOV
QR = CAP // 4
EPS = 1e-6
LAM_INIT = 0.8 - 0.6
KB = 1024
RELW = 7 * P
PIECE = 2048
RAWS = 6
HLS = 4
ZP = 2 * NCH
PP = 8
PRE = ZP + PP

_c = {}
_n = 0
for _name, _w in (("ident", P), ("tri", P), ("ones", P), ("rel", RELW), ("cosA", 32), ("sinA", 32),
                  ("cosR", 128), ("sinR", 128), ("e128", NE), ("grank", NG), ("erank", NE),
                  ("iota", P), ("thr", MAXB - 1), ("quart", 3), ("tok", NT)):
    _c[_name] = (_n, _n + _w)
    _n += _w
NCST = _n


def constants():
    import numpy as np
    t = np.zeros((P, NCST), np.float32)

    def put(name, v):
        a, b = _c[name]
        t[:, a:b] = v
    i = np.arange(P)
    put("ident", np.eye(P))
    put("tri", (i[:, None] < i[None, :]).astype(np.float32))
    put("ones", 1.0)
    put("rel", np.arange(RELW)[None, :] - 3 * P - i[:, None])
    for rot, theta, cn, sn in ((16, 500000.0, "cosA", "sinA"), (64, 10000.0, "cosR", "sinR")):
        inv = np.float32(theta) ** (-np.arange(0, rot, 2, dtype=np.float32) / np.float32(rot))
        inv = inv.astype(np.float32)
        ang = (np.arange(512, dtype=np.float32)[:, None] * inv[None, :]).astype(np.float32)
        for f, n in ((np.cos, cn), (np.sin, sn)):
            v = f(ang.astype(np.float64)).astype(np.float32).reshape(4, P, rot // 2)
            put(n, v.transpose(1, 0, 2).reshape(P, -1))
    e = np.arange(NE)
    put("e128", e * CAP)
    put("grank", NG - np.arange(NG))
    put("erank", EPG - e % EPG)
    put("iota", np.arange(P))
    put("thr", CAP * np.arange(1, MAXB))
    put("quart", QR * np.arange(1, 4))
    put("tok", i[:, None] + P * np.arange(NT)[None, :])
    return t


def hybrid_layer(nc, A):
    ctx = ExitStack()
    base = (nc.sbuf_base + 63) // 64 * 64
    RAW_O, HL_O, D_O, E_O = 0, 48 * KB, 112 * KB, 160 * KB

    def at(name, off, shape, dt=F32):
        return nc.alloc_sbuf_tensor_at(name, shape, dt, offset=base + off)

    raw = [at(f"raw{s}", RAW_O + s * 8 * KB, [P, PIECE]) for s in range(RAWS)]
    whi = [at(f"whi{s}", HL_O + s * 8 * KB, [P, PIECE], F32R) for s in range(HLS)]
    wlo = [at(f"wlo{s}", HL_O + (HLS + s) * 8 * KB, [P, PIECE], F32R) for s in range(HLS)]
    xTh = at("xTh", D_O, [P, KC, T], F32R)
    xTl = at("xTl", D_O + 24 * KB, [P, KC, T], F32R)
    oTh = [at(f"oTh{b}", D_O + b * 12 * KB, [P, H, T], F32R) for b in range(2)]
    oTl = [at(f"oTl{b}", D_O + (2 + b) * 12 * KB, [P, H, T], F32R) for b in range(2)]
    mTh = [at(f"mTh{s}", D_O + s * 4 * KB, [P, KC, P], F32R) for s in range(2)]
    mTl = [at(f"mTl{s}", D_O + 8 * KB + s * 4 * KB, [P, KC, P], F32R) for s in range(2)]
    x2 = at("x2", D_O + 16 * KB, [P, NT, D])
    CST_O = E_O
    cst = at("cst", CST_O, [P, NCST])
    W_O = CST_O + (NCST * 4 + 63) // 64 * 64
    off = [W_O]

    def small(name, shape, dt=F32):
        n = 4
        for s in shape[1:]:
            n *= s
        t = at(name, off[0], shape, dt)
        off[0] += (n + 31) // 32 * 32
        return t
    gn1 = small("gn1", [P, KC])
    ssq = small("ssq", [P, 32])
    rstd = small("rstd", [P, 32])
    rs_a = small("rs_a", [P, 32])
    gsub = small("gsub", [P, 1])
    lamv = small("lamv", [P, 4])
    decay = small("decay", [P, 8])
    mx = small("mx", [P, 2, 2])
    nm = small("nm", [P, 2, 2])
    sume = small("sume", [P, 2, 2])
    rc = small("rc", [P, 2, 2])
    gates = small("gates", [P, 2, NT])
    slotf = small("slotf", [P, 2, NT])
    sloti = small("sloti", [P, 2, NT], U32)
    idxt = small("idxt", [P, NB + 1], I32)
    gq = small("gq", [P, 4, NT, NG])
    v6 = small("v6", [P, 9, NT])
    nbi = small("nbi", [1, 16], I32)
    quarters = small("quarters", [1, NB + 1], I32)
    idxb = small("idxb", [P, 1], I32)
    sdum = small("sdum", [P, 1])
    F_O = off[0]
    FREE = 212800 - F_O
    assert FREE >= 36 * KB + 2400, FREE
    xin = at("xin", F_O, [P, NT, D])
    zst = [at(f"zst{s}", F_O + 24 * KB + s * 2 * KB, [P, 512]) for s in range(4)]
    junk = at("junk", F_O + 32 * KB, [P, D])
    rt_sq = at("rt_sq", F_O + 24 * KB, [P, D])
    zrow = at("zrow", F_O + 36 * KB, [P, 256])
    lamr = at("lamr", F_O + 36 * KB, [P, 4, HD])
    rt_v = at("rt_v", F_O + 32 * KB, [P, 4, 128])
    rt_p = at("rt_p", F_O + 36 * KB, [P, 4, 128])
    zqk = [at("zqk0", F_O, [P, 4, 1024]), at("zqk1", RAW_O, [P, 2, 1024])]
    zr = [at("zr0", F_O + 16 * KB, [P, 4, 512]), at("zr1", RAW_O + 8 * KB, [P, 2, 512])]
    zv = [at("zv0", HL_O + 24 * KB, [P, 4, 512]), at("zv1", RAW_O + 12 * KB, [P, 2, 512])]
    zvr = [at("zvr0", HL_O + 32 * KB, [P, 4, 512]), at("zvr1", RAW_O + 16 * KB, [P, 2, 512])]
    zgr = [at("zgr0", HL_O + 40 * KB, [P, 4, 512]), at("zgr1", RAW_O + 20 * KB, [P, 2, 512])]
    silu = [at("silu0", HL_O + 48 * KB, [P, 4, 512]), at("silu1", HL_O + 56 * KB, [P, 2, 512])]
    sqj = at("sqj", HL_O + 60 * KB, [P, 4, VD])
    qkT = at("qkT", HL_O, [P, 2, H, 512])
    rqkT = at("rqkT", HL_O + 16 * KB, [P, 2, 2, 512])
    wdec = at("wdec", RAW_O + 32 * KB, [P, H, RELW])
    prob = [at(f"prob{s}", F_O + s * 4 * KB, [P, 2, 512]) for s in range(2)]
    att = [at(f"att{s}", F_O + 8 * KB + s * 2 * KB, [P, 512]) for s in range(2)]
    attT = [at(f"attT{s}", F_O + 12 * KB + s * 2 * KB, [P, 512]) for s in range(2)]
    smk = [at(f"smk{s}", F_O + 16 * KB + s * 2 * KB, [P, 512]) for s in range(2)]
    oun = at("oun", F_O + 20 * KB, [P, 4, 512])
    yun = at("yun", F_O + 28 * KB, [P, 4, 512])
    mg = at("mg", F_O, [P, NT, D])
    gat = [at(f"gat{s}", F_O + (24 + 4 * s) * KB, [P, 2, 512]) for s in range(2)]
    prd = [at(f"prd{s}", F_O + 32 * KB + s * 2 * KB, [P, 512]) for s in range(2)]
    xres = at("xres", F_O + 24 * KB, [P, D])
    g2 = at("g2", D_O + 40 * KB, [P, D])
    rT = at("rT", D_O + 44 * KB, [P, KC, P])
    rrow = [at(f"rrow{s}", F_O + (28 + 4 * s) * KB, [P, D]) for s in range(2)]
    wrt = at("wrt", F_O + 36 * KB, [P, KC, NG + NE])
    brt = at("brt", F_O + 36 * KB + 1280, [P, NG + NE])
    lg = at("lg", F_O + 36 * KB + 1536, [P, NT, NG + NE])
    sel = at("sel", D_O + 1 * KB, [P, NT, NE])
    A1 = at("A1", D_O + 2 * KB, [P, NT, NE])
    A2 = at("A2", D_O + 3 * KB, [P, NT, NE])
    t1 = at("t1", D_O + 4 * KB, [P, NT, NE])
    t2 = at("t2", D_O + 5 * KB, [P, NT, NE])
    Ab = at("Ab", D_O + 6 * KB, [P, NT, NE])
    nov = at("nov", D_O + 7 * KB, [P, NE])
    run = at("run", D_O + 7 * KB + 128, [P, 2, NE // 2 + NE])
    ovb = at("ovb", D_O + 7 * KB + 512, [P, NE])
    bt = at("bt", D_O + 8 * KB, [P, NOV * NE])
    bts = at("bts", D_O + 9 * KB + 512, [1, NE])
    sbf = at("sbf", D_O + 9 * KB + 640, [P, 2, 2, NT])
    Bt = at("Bt", D_O + 10 * KB, [P, 2 * NT, NB + 1])
    Rt = at("Rt", D_O + 12 * KB + 512, [P, NT, P])
    XT_O = D_O
    eTh = at("eTh", XT_O, [P, KC, P], F32R)
    eTl = at("eTl", XT_O + 4 * KB, [P, KC, P], F32R)
    hTh = at("hTh", XT_O + 8 * KB, [P, 4, P], F32R)
    hTl = at("hTl", XT_O + 10 * KB, [P, 4, P], F32R)
    sg = at("sg", XT_O + 12 * KB, [P, 512])
    hh = at("hh", XT_O + 14 * KB, [P, 512])
    xg = at("xg", XT_O + 40 * KB, [P, D])
    ystage = at("ystage", XT_O + 44 * KB, [P, D])
    ehi = whi + [at(f"whi{s}", F_O + s % 4 * 8 * KB, [P, PIECE], F32R) for s in (4, 5)]
    elo = wlo + [at(f"wlo{s}", F_O + (2 + s % 4) * 8 * KB, [P, PIECE], F32R) for s in (4, 5)]
    ya = [[at(f"ya{t}{k}", RAW_O + (2 * t + k) * 4 * KB, [P, D]) for k in range(2)] for t in range(NT)]
    gf = at("gf", HL_O, [P, D])
    yo = [at(f"yo{t}", HL_O + (1 + t) * 4 * KB, [P, D]) for t in range(NT)]
    fj = [at(f"fj{s}", HL_O + (7 + s) * 4 * KB, [P, D]) for s in range(2)]

    ps = [ctx.enter_context(nc.psum_tensor(f"ps{i}", [P, 512], F32)) for i in range(8)]

    def C(name):
        a, b = _c[name]
        return cst[:, a:b]
    ident = C("ident")

    z_d = nc.dram_tensor("z_scratch", [T, D_IN], F32, kind="Internal").ap()
    xn_d = nc.dram_tensor("xn_scratch", [T, D], F32, kind="Internal").ap()
    y_d = nc.dram_tensor("y_scratch", [NB * CAP, D], F32, kind="Internal").ap()

    def sem(name):
        return ctx.enter_context(nc.semaphore(name))
    with ctx:
        s_cst = sem("s_cst")
        s_par = sem("s_par")
        s_x = [sem(f"s_xt{t}") for t in range(NT)]
        s_sqv = sem("s_sqv")
        s_raw = [sem(f"s_raw{s}") for s in range(RAWS)]
        s_hi = sem("s_hi")
        s_lo = sem("s_lo")
        s_lo1 = sem("s_lo1")
        s_pe = sem("s_pe")
        s_sq = sem("s_sq")
        s_dv = sem("s_dv")
        s_rstd1 = sem("s_rstd1")
        s_xs = sem("s_xs")
        s_nT = sem("s_nT")
        s_nth = sem("s_nth")
        s_ntc = sem("s_ntc")
        s_ntl = sem("s_ntl")
        s_zmm = sem("s_zmm")
        s_zev = sem("s_zev")
        s_zst = [sem(f"s_zst{s}") for s in range(4)]
        s_zlq = [sem(f"s_zlq{s}") for s in range(2)]
        s_zlv = [sem(f"s_zlv{s}") for s in range(2)]
        s_decay = sem("s_decay")
        s_lame = sem("s_lame")
        s_warg = sem("s_warg")
        s_wexp = sem("s_wexp")
        s_gsub = sem("s_gsub")
        s_rotv = sem("s_rotv")
        s_rotp = sem("s_rotp")
        s_pl = sem("s_pl")
        s_osq = sem("s_osq")
        s_sg = sem("s_sg")
        s_silu = sem("s_silu")
        s_rstd2 = sem("s_rstd2")
        s_ony = sem("s_ony")
        s_qT = sem("s_qT")
        s_qTc = sem("s_qTc")
        s_sc = sem("s_sc")
        s_mx = sem("s_mx")
        s_ex = sem("s_ex")
        s_a = sem("s_a")
        s_aT = sem("s_aT")
        s_aTc = sem("s_aTc")
        s_o = sem("s_o")
        s_oc = sem("s_oc")
        s_rs = sem("s_rs")
        s_rm = sem("s_rm")
        s_ry = sem("s_ry")
        s_ryc = sem("s_ryc")
        s_on = sem("s_on")
        s_oT = sem("s_oT")
        s_oTh = sem("s_oTh")
        s_oTl = sem("s_oTl")
        s_gl = [sem(f"s_gl{s}") for s in range(2)]
        s_gs = sem("s_gs")
        s_pm = sem("s_pm")
        s_mgd = sem("s_mgd")
        s_mT = sem("s_mT")
        s_mTh = sem("s_mTh")
        s_mTl = sem("s_mTl")
        s_xr = sem("s_xr")
        s_w = sem("s_w")
        s_x2 = sem("s_x2")
        s_rp = sem("s_rp")
        s_sq2 = sem("s_sq2")
        s_rr = sem("s_rr")
        s_rst = [sem(f"s_rst{s}") for s in range(2)]
        s_rTm = sem("s_rTm")
        s_rTc = sem("s_rTc")
        s_lg = sem("s_lg")
        s_rx = sem("s_rx")
        s_re = sem("s_re")
        s_Ab = sem("s_Ab")
        s_rk = sem("s_rk")
        s_slot = sem("s_slot")
        s_tb = sem("s_tb")
        s_tbm = sem("s_tbm")
        s_ic = sem("s_ic")
        s_nb = sem("s_nb")
        s_h13 = sem("s_h13")
        s_gx = sem("s_gx")
        s_idx = sem("s_idx")
        s_eT = sem("s_eT")
        s_eTh = sem("s_eTh")
        s_eTl = sem("s_eTl")
        s_h1 = sem("s_h1")
        s_sgm = sem("s_sgm")
        s_h = sem("s_h")
        s_hT = sem("s_hT")
        s_hTh = sem("s_hTh")
        s_hTl = sem("s_hTl")
        s_y = sem("s_y")
        s_yc = sem("s_yc")
        s_ys = sem("s_ys")
        s_md = sem("s_md")
        s_zr = sem("s_zr")
        s_g1 = [sem(f"s_g1{t}") for t in range(NT)]
        s_c2 = sem("s_c2")
        s_sq3 = sem("s_sq3")
        s_yf = sem("s_yf")
        s_gf = sem("s_gf")
        s_out = sem("s_out")
        block = ctx.enter_context(nc.Block())

        x_tiles = [A["x_prompt"][0, t * P:(t + 1) * P, :] for t in range(4)] + \
                  [A["x_sample"][0, t * P:(t + 1) * P, :] for t in range(2)]
        o_tiles = [A["y_prompt"][0, t * P:(t + 1) * P, :] for t in range(4)] + \
                  [A["y_sample"][0, t * P:(t + 1) * P, :] for t in range(2)]
        w_in = A["w_in"][0].rearrange("(p c) n -> p c n", c=KC)
        w_out = A["w_out"][0].rearrange("(p c) n -> p c n", c=KC)
        w_pab = [A[n][0].rearrange("(h p) n -> p h n", p=P) for n in ("w_pa", "w_pb")]
        e_w = {"w1": A["w1"][0].rearrange("e (p c) f -> e p (c f)", c=KC),
               "w3": A["w3"][0].rearrange("e (p c) f -> e p (c f)", c=KC),
               "w2": A["w2"][0].rearrange("e (p c) n -> e p (c n)", c=4)}

        ZEROS = [(q, e, e + 8) for q in range(1, 4) for e in range(0, NE, 8)] + [(q, NE, NB) for q in range(4)]
        NZ = len(ZEROS)

        def rest_done(eng, b, j):
            if j == 1:
                eng.wait_ge(s_lo1, b + 1)
            else:
                eng.wait_ge(s_lo, 5 * b + (PRE + j + (j == 0)))
        SEQ_T0 = (0, 4)
        SEQ_NT = (4, 2)
        ITS = [(s, h, qt) for s in range(2) for h in range(H) for qt in range(SEQ_NT[s])]

        def rotary(eng, link, v, half, cs, sn, tmp):
            groups = v.shape[1]
            x1, x2_ = v[:, :, 0:half], v[:, :, half:2 * half]
            cb, sb = (a.unsqueeze(1).to_broadcast([P, groups, half]) for a in (cs, sn))
            r = [tmp[:, k, :].rearrange("p (g d) -> p g d", d=half) for k in range(4)]
            eng.tensor_tensor(r[0], x1, cb, ALU.mult)
            eng.tensor_tensor(r[1], x2_, sb, ALU.mult)
            eng.tensor_tensor(r[2], x2_, cb, ALU.mult)
            link(eng.tensor_tensor(r[3], x1, sb, ALU.mult))
            eng.tensor_tensor(x1, r[0], r[1], ALU.subtract)
            link(eng.tensor_tensor(x2_, r[2], r[3], ALU.add))

        @block.sync
        def _(sp):
            for t in range(2):
                sp.dma_start(xin[:, t, :], x_tiles[t]).then_inc(s_x[t], 16)
            sp.dma_start(cst[:, :], A["consts"]).then_inc(s_cst, 16)
            sp.dma_start(gn1[:, :], A["attn_norm_g"][0].rearrange("(p c) -> p c", c=KC)).then_inc(s_par, 16)
            sp.dma_start(gsub[:, :], A["subln_g"][0].rearrange("(p c) -> p c", c=1)).then_inc(s_par, 16)
            sp.dma_start(decay[:, 0:4], A["ret_decay_f"].partition_broadcast(P)[:, 0, :]).then_inc(s_par, 16)
            sp.dma_start(decay[:, 4:8], A["ret_decay_b"].partition_broadcast(P)[:, 0, :]).then_inc(s_par, 16)
            for k, n in enumerate(("lam_q1", "lam_k1", "lam_q2", "lam_k2")):
                sp.dma_start(lamr[:, k, :], A[n].partition_broadcast(P)[:, 0, :]).then_inc(s_par, 16)
            for t in range(2, NT):
                sp.dma_start(xin[:, t, :], x_tiles[t]).then_inc(s_x[t], 16)
            def z_piece(i, j):
                c = bass.ds(i * 1024 + (j // 2) * 512, 512)
                sp.dma_start(raw[j][:, :].rearrange("p (c n) -> p c n", n=512),
                             w_in[:, 4 * (j % 2):4 * (j % 2) + 4, c]).then_inc(s_raw[j], 16)
            for j in range(4):
                z_piece(0, j)
            def z_pieces(i):
                for j in range(4):
                    sp.wait_ge(s_lo, 4 * i + (j - 3))
                    z_piece(i, j)
            with sp.Fori(1, NCH // 2 - 1) as i:
                z_pieces(i)

            def z_rows(s, dst, c0, n, done):
                t0, nt = SEQ_T0[s], SEQ_NT[s]
                rows = z_d[t0 * P:(t0 + nt) * P, :].rearrange("(t p) n -> p t n", p=P)
                sp.dma_start(dst[s][:, :, :], rows[:, :, c0:c0 + n]).then_inc(done[s], 16)
            for k in range(4):
                sp.wait_ge(s_zst[k], 16 * 6 * NT // 4)
            z_rows(0, zqk, C_Q, 1024, s_zlq)
            z_rows(0, zr, C_R, 512, s_zlq)
            z_pieces(NCH // 2 - 1)
            sp.wait_ge(s_zmm, NCH * NT)
            z_rows(0, zv, C_V, 512, s_zlv)
            z_rows(0, zvr, C_VR, 512, s_zlv)
            z_rows(0, zgr, C_GR, 512, s_zlv)
            sp.wait_ge(s_lo, ZP)
            z_rows(1, zqk, C_Q, 1024, s_zlq)
            z_rows(1, zr, C_R, 512, s_zlq)
            z_rows(1, zv, C_V, 512, s_zlv)
            z_rows(1, zvr, C_VR, 512, s_zlv)
            z_rows(1, zgr, C_GR, 512, s_zlv)

            def p_piece(p):
                slot = (3 + p) % RAWS
                dst = raw[slot][:, :].rearrange("p (c n) -> p c n", n=512)
                if p < 4:
                    src = w_pab[p % 2][:, :, (p // 2) * 512:(p // 2) * 512 + 512]
                else:
                    q = p - 4
                    src = w_out[:, 4 * (q % 2):4 * (q % 2) + 4, (q // 2) * 512:(q // 2) * 512 + 512]
                sp.dma_start(dst, src).then_inc(s_raw[slot], 16)
            p_piece(0)
            sp.wait_ge(s_rm, 24)
            p_piece(1)
            p_piece(2)
            sp.wait_ge(s_ry, 24)
            sp.wait_ge(s_o, 24)
            sp.wait_ge(s_silu, 2)
            for p in range(3, 6):
                p_piece(p)

            def gate_half(k):
                m, t = k // NT, k % NT
                if k == 0:
                    sp.wait_ge(s_oTl, 16)
                if k >= 2:
                    sp.wait_ge(s_mgd, k - 1)
                rows = z_d[t * P:(t + 1) * P, C_GA:C_GA + 2 * D].rearrange("p (b n) -> p b n", b=2)
                sp.dma_start(gat[k % 2][:, :, :], rows[:, :, m * 512:(m + 1) * 512]).then_inc(s_gl[k % 2], 16)
            for k in range(4):
                sp.wait_ge(s_zst[k], 16 * NCH * NT // 4)
            for k in range(2 * NT):
                gate_half(k)
                if k == 1:
                    for p in range(6, 8):
                        sp.wait_ge(s_lo, ZP + p - 5)
                        p_piece(p)
            sp.wait_ge(s_mgd, 2 * NT)
            sp.wait_ge(s_ys, 16 * NZ)
            sp.dma_start(g2[:, :], A["ffn_norm_g"].partition_broadcast(P)[:, 0, :]).then_inc(s_rp, 16)
            sp.dma_start(wrt[:, :, 0:NG], A["w_rg"][0].rearrange("(p c) g -> p c g", c=KC)).then_inc(s_rp, 16)
            for g in range(NG):
                sp.dma_start(wrt[:, :, NG + g * EPG:NG + (g + 1) * EPG],
                             A["w_re"][0, g].rearrange("(p c) e -> p c e", c=KC)).then_inc(s_rp, 16)
            sp.dma_start(brt[:, 0:NG], A["b_rg"].partition_broadcast(P)[:, 0, :]).then_inc(s_rp, 16)
            sp.dma_start(brt[:, NG:NG + NE],
                         A["b_re"].rearrange("a g e -> a (g e)").partition_broadcast(P)[:, 0, :]).then_inc(s_rp, 16)
            for t in range(NT):
                if t == 0:
                    sp.wait_ge(s_mgd, 2 * NT)
                else:
                    sp.wait_ge(s_x2, 2 * t)
                sp.dma_start(xres[:, :], x_tiles[t]).then_inc(s_xr, 16)
            def e_pieces(b, e):
                for j in range(6):
                    if not isinstance(b, int):
                        rest_done(sp, b - 1, j)
                    src = e_w[("w1", "w3", "w2")[j // 2]][bass.ds(e, 1), :, (j % 2) * PIECE:(j % 2 + 1) * PIECE]
                    sp.dma_start(raw[j][:, :], src[0]).then_inc(s_raw[j], 16)
            sp.wait_ge(s_lo, PRE)
            e_pieces(0, 0)
            with sp.Fori(1, NE) as b:
                e_pieces(b, b)
            sp.wait_ge(s_nb, 1)
            nb = sp.value_load(nbi[0:1, 0:1], min_val=NE, max_val=NB)
            with sp.If(nb > NE):
                with sp.Fori(NE, nb) as b:
                    e = sp.value_load(nbi[0:1, bass.ds(b - (NE - 1), 1)], min_val=0, max_val=NE - 1)
                    e_pieces(b, e)
            sp.wait_ge(s_md, 1)
            sp.dma_start(gf[:, :], A["final_norm_g"].rearrange("(a n) -> a n", a=1).partition_broadcast(P)[:, 0, :]).then_inc(s_gf, 16)
            for t in range(NT):
                sp.wait_ge(s_yf, t + 1)
                sp.dma_start(o_tiles[t], yo[t][:, :]).then_inc(s_out, 16)
            sp.wait_ge(s_out, 16 * NT)

        @block.tensor
        def _(pe):
            def split_mm(out, ah, al, bh, bl, first, last):
                pe.matmul(out, ah, bh, start=first, stop=False)
                pe.matmul(out, ah, bl, start=False, stop=False)
                return pe.matmul(out, al, bh, start=False, stop=last)

            def input_columns(t):
                pe.wait_ge(s_xs, t + 1)
                for j in range(2):
                    n = 2 * t + j
                    if n >= 4:
                        pe.wait_ge(s_ntc, n - 3)
                    for c in range(4):
                        mm = pe.transpose(ps[4 + n % 4][:, c * P:(c + 1) * P],
                                          xin[:, t, 4 * j + c::KC], ident)
                    mm.then_inc(s_nT, 1)

            pe.wait_ge(s_cst, 16)
            input_columns(0)
            input_columns(1)
            def z_chunk(i, m):
                for t in range(NT):
                    if isinstance(i, int) and m == 0:
                        if t + 2 < NT:
                            input_columns(t + 2)
                        pe.wait_ge(s_nth, 2 * t + 2)
                        pe.wait_ge(s_ntl, 2 * t + 2)
                    bank = ps[(6 * m + t) % 4]
                    n = 12 * i + 6 * m + t
                    if not (isinstance(i, int) and i == 0 and 6 * m + t < 4):
                        pe.wait_ge(s_zev, n - 3)
                    for j in range(2):
                        s = 2 * m + j
                        if t == 0:
                            pe.wait_ge(s_lo, 4 * i + (s + 1))
                        for k in range(4):
                            c = 4 * j + k
                            mm = split_mm(bank[:, :], xTh[:, c, t * P:(t + 1) * P], xTl[:, c, t * P:(t + 1) * P],
                                          whi[s][:, k * 512:(k + 1) * 512], wlo[s][:, k * 512:(k + 1) * 512],
                                          c == 0, c == KC - 1)
                        if t == NT - 1 and j == 0:
                            mm.then_inc(s_pe, 1)
                    mm.then_inc(s_zmm, 1)

            z_chunk(0, 0)
            z_chunk(0, 1)
            with pe.Fori(1, NCH // 2) as i:
                z_chunk(i, 0)
                z_chunk(i, 1)

            def to_columns(s):
                for g in range(12):
                    G = 12 * s + g
                    if g == 0:
                        pe.wait_ge((s_rotv, s_rotp)[s], 1)
                    if g >= 2:
                        pe.wait_ge(s_qTc, G - 1)
                    for t in range(SEQ_NT[s]):
                        src = zqk[s][:, t, g * P:(g + 1) * P] if g < 8 else zr[s][:, t, (g - 8) * P:(g - 7) * P]
                        mm = pe.transpose(ps[4 + 2 * (g % 2)][:, t * P:(t + 1) * P], src, ident)
                    mm.then_inc(s_qT, 1)

            def outputs_to_columns(s, b):
                for h in range(H):
                    O = 8 * s + 4 * b + h
                    pe.wait_ge((s_on, s_ony)[b], 4 * s + h + 1)
                    if h >= 2 or b == 1:
                        pe.wait_ge(s_oTl, O - 1)
                    for t in range(SEQ_NT[s]):
                        mm = pe.transpose(ps[5 + 2 * (h % 2)][:, t * P:(t + 1) * P],
                                          (oun, yun)[b][:, t, h * VD:(h + 1) * VD], ident)
                    mm.then_inc(s_oT, 1)

            def attend(s, i0):
                nt = SEQ_NT[s]
                S = nt * P
                i1 = i0 + H * nt

                def scores(n):
                    _, h, qt = ITS[n]
                    if n >= 2:
                        pe.wait_ge(s_ex, n - 1)
                    for c in range(2):
                        rows = slice(c * HD, (c + 1) * HD)
                        mm = pe.matmul(ps[2 * (n % 2) + c][:, 0:S], qkT[rows, 0, h, qt * P:(qt + 1) * P],
                                       qkT[rows, 1, h, 0:S], start=True, stop=True)
                    mm.then_inc(s_sc, 1)

                def ret_scores(n):
                    _, h, kt = ITS[n]
                    rows = slice((h % 2) * HD, (h % 2 + 1) * HD)
                    if n >= 1:
                        pe.wait_ge(s_rm, n)
                    pe.matmul(ps[6][:, 0:S], rqkT[rows, 1, h // 2, kt * P:(kt + 1) * P],
                              rqkT[rows, 0, h // 2, 0:S], start=True, stop=True).then_inc(s_rs, 1)

                def values(n):
                    _, h, qt = ITS[n]
                    pe.wait_ge(s_aTc, n + 1)
                    if n >= 1:
                        pe.wait_ge(s_oc, n)
                    for kt in range(nt):
                        mm = pe.matmul(ps[5][:, (n % 4) * VD:(n % 4 + 1) * VD],
                                       attT[n % 2][:, kt * P:(kt + 1) * P],
                                       zv[s][:, kt, h * VD:(h + 1) * VD], start=(kt == 0), stop=(kt == nt - 1))
                    mm.then_inc(s_o, 1)

                def ret_values(n):
                    _, h, kt = ITS[n]
                    pe.wait_ge(s_rm, n + 1)
                    if kt == 0 and 4 * s + h >= 1:
                        pe.wait_ge(s_ryc, 4 * s + h)
                    for qt in range(nt):
                        mm = pe.matmul(ps[7][:, qt * VD:(qt + 1) * VD], smk[n % 2][:, qt * P:(qt + 1) * P],
                                       zvr[s][:, kt, h * VD:(h + 1) * VD], start=(kt == 0 and qt == 0),
                                       stop=(kt == nt - 1 and qt == nt - 1), skip_group_check=True)
                    mm.then_inc(s_ry, 1)

                pe.wait_ge(s_qTc, 12 * (s + 1))
                if s == 0:
                    pe.wait_ge(s_zev, NCH * NT)
                scores(i0)
                for n in range(i0, i1):
                    if n + 1 < i1:
                        scores(n + 1)
                    ret_scores(n)
                    if n == i0:
                        pe.wait_ge(s_zlv[s], 16 * 3)
                    if n > i0:
                        values(n - 1)
                        ret_values(n - 1)
                    pe.wait_ge(s_a, n + 1)
                    if n >= 1:
                        pe.wait_ge(s_aTc, n)
                    for kt in range(nt):
                        mm = pe.transpose(ps[4][:, kt * P:(kt + 1) * P], att[n % 2][:, kt * P:(kt + 1) * P], ident)
                    mm.then_inc(s_aT, 1)
                values(i1 - 1)
                ret_values(i1 - 1)

            to_columns(0)
            attend(0, 0)
            pe.wait_ge(s_aTc, 16)
            pe.wait_ge(s_rm, 16)
            to_columns(1)
            pe.wait_ge(s_oc, 16)
            pe.wait_ge(s_ryc, 4)
            outputs_to_columns(0, 0)
            outputs_to_columns(0, 1)
            pe.wait_ge(s_oTl, 8)
            attend(1, 16)
            pe.wait_ge(s_oc, 24)
            pe.wait_ge(s_ryc, 8)
            outputs_to_columns(1, 0)
            outputs_to_columns(1, 1)

            pe.wait_ge(s_oTh, 16)
            pe.wait_ge(s_oTl, 16)
            for n in range(4 * NT):
                t, m = n % (2 * NT) // 2, n // (2 * NT) * 2 + n % 2
                if n >= 4:
                    pe.wait_ge(s_pm, n - 3)
                if t == 0:
                    pe.wait_ge(s_lo, ZP + m + 1)
                for h in range(H):
                    mm = split_mm(ps[n % 4][:, :], oTh[m % 2][:, h, t * P:(t + 1) * P],
                                  oTl[m % 2][:, h, t * P:(t + 1) * P], whi[m][:, h * 512:(h + 1) * 512],
                                  wlo[m][:, h * 512:(h + 1) * 512], h == 0, h == H - 1)
                mm.then_inc(s_gs, 1)
            def merged_to_columns(t):
                pe.wait_ge(s_mgd, NT + t + 1)
                for j in range(2):
                    n = 2 * t + j
                    if n >= 2:
                        pe.wait_ge(s_mTl, n - 1)
                    for c in range(4):
                        mm = pe.transpose(ps[4 + n % 2][:, c * P:(c + 1) * P], mg[:, t, 4 * j + c::KC], ident)
                    mm.then_inc(s_mT, 1)

            def route_columns(t):
                pe.wait_ge(s_rr, t + 1)
                if t >= 1:
                    pe.wait_ge(s_rTc, 2 * t)
                for j in range(2):
                    for c in range(4):
                        mm = pe.transpose(ps[j][:, c * P:(c + 1) * P], rrow[t % 2][:, 4 * j + c::KC], ident)
                    mm.then_inc(s_rTm, 1)

            def logits(t):
                pe.wait_ge(s_rTc, 2 * t + 2)
                if t == 0:
                    pe.wait_ge(s_rp, 16 * 8)
                if t >= 1:
                    pe.wait_ge(s_rx, t)
                for c in range(KC):
                    mm = pe.matmul(ps[2][:, 0:NG + NE], rT[:, c, :], wrt[:, c, :],
                                   start=(c == 0), stop=(c == KC - 1))
                mm.then_inc(s_lg, 1)
            merged_to_columns(0)
            for t in range(NT):
                if t + 1 < NT:
                    merged_to_columns(t + 1)
                pe.wait_ge(s_mTl, 2 * t + 2)
                for n in range(2):
                    if t >= 1:
                        pe.wait_ge(s_x2, 2 * t + n - 1)
                    for j in range(2):
                        p = 2 * n + j
                        if t == 0:
                            pe.wait_ge(s_lo, ZP + 4 + p + 1)
                        for k in range(4):
                            c = 4 * j + k
                            mm = split_mm(ps[6 + n][:, :], mTh[t % 2][:, c, :], mTl[t % 2][:, c, :],
                                          whi[p][:, k * 512:(k + 1) * 512], wlo[p][:, k * 512:(k + 1) * 512],
                                          c == 0, c == KC - 1)
                        if t == NT - 1 and j == 0:
                            mm.then_inc(s_pe, 1)
                    mm.then_inc(s_w, 1)
                    if t >= 1 and n == 0:
                        route_columns(t - 1)
                if t >= 1:
                    logits(t - 1)
            route_columns(NT - 1)
            logits(NT - 1)
            pe.wait_ge(s_Ab, 1)
            picked = Ab[:, :, :].rearrange("p t e -> p (t e)")
            pe.matmul(ps[3][:, 0:NT * NE], C("tri"), picked, start=True, stop=False, skip_group_check=True)
            for u in range(1, NT + 1):
                mm = pe.matmul(ps[3][:, u * NE:(NT + 1) * NE], C("ones"), picked[:, 0:(NT + 1 - u) * NE],
                               start=False, stop=(u == NT), skip_group_check=True)
            mm.then_inc(s_rk, 1)
            for q in range(2 * NT):
                pe.wait_ge(s_tb, q + 1)
                pe.matmul(ps[4][:, 0:NB + 1], Rt[:, q % NT, :], Bt[:, q, :],
                          start=(q == 0), stop=(q == 2 * NT - 1)).then_inc(s_tbm, 1)

            pe.wait_ge(s_nb, 1)
            nb = pe.value_load(nbi[0:1, 0:1], min_val=NE, max_val=NB)

            def x_to_columns(b, j):
                pe.wait_ge(s_gx, 16 * b + 16)
                for c in range(4):
                    mm = pe.transpose(ps[2 + j][:, c * P:(c + 1) * P], xg[:, 4 * j + c::KC], ident)
                mm.then_inc(s_eT, 1)

            def e_block(b, last):
                pe.wait_ge(s_eTl, 2 * b + 2)
                for m in range(2):
                    for j in range(2):
                        q = 2 * m + j
                        rest_done(pe, b, q)
                        for k in range(4):
                            c = 4 * j + k
                            mm = split_mm(ps[m][:, :], eTh[:, c, :], eTl[:, c, :],
                                          ehi[q][:, k * 512:(k + 1) * 512], elo[q][:, k * 512:(k + 1) * 512],
                                          c == 0, c == KC - 1)
                        if j == 0:
                            mm.then_inc(s_pe, 1)
                    mm.then_inc(s_h1, 1)
                if not last:
                    x_to_columns(b + 1, 0)
                pe.wait_ge(s_h, b + 2)
                for c in range(4):
                    mm = pe.transpose(ps[4][:, c * P:(c + 1) * P], hh[:, c::4], ident)
                mm.then_inc(s_hT, 1)
                if not last:
                    x_to_columns(b + 1, 1)
                pe.wait_ge(s_hTh, b + 1)
                pe.wait_ge(s_yc, 2 * b + 2)
                for j in range(2):
                    q = 4 + j
                    rest_done(pe, b, q)
                    parts = [(k, n, slice(k * D + n * 512, k * D + n * 512 + 512)) for k in range(2) for n in range(2)]
                    for k, n, w in parts:
                        c = 2 * j + k
                        pe.matmul(ps[6 + n][:, :], hTh[:, c, :], ehi[q][:, w], start=(c == 0), stop=False)
                        pe.matmul(ps[6 + n][:, :], hTh[:, c, :], elo[q][:, w], start=False, stop=False)
                    if j == 0:
                        pe.wait_ge(s_hTl, b + 1)
                    for k, n, w in parts:
                        c = 2 * j + k
                        mm = pe.matmul(ps[6 + n][:, :], hTl[:, c, :], ehi[q][:, w], start=False, stop=(c == 3))
                    if j == 0:
                        mm.then_inc(s_pe, 1)
                mm.then_inc(s_y, 1)

            x_to_columns(0, 0)
            x_to_columns(0, 1)
            pe.sem_inc(s_h1, 2)
            pe.sem_inc(s_hT, 1)
            pe.sem_inc(s_y, 1)
            with pe.Fori(0, nb - 1) as b:
                e_block(b, last=False)
            e_block(nb - 1, last=True)

        @block.scalar
        def _(act):
            def hi_piece(slot_raw, use, slot, freed=None):
                act.wait_ge(s_raw[slot_raw], 16 * use)
                if freed is not None:
                    act.wait_ge(*freed)
                act.activation(ehi[slot][:, :], raw[slot_raw][:, :], ACT.Copy).then_inc(s_hi, 1)

            act.wait_ge(s_lame, 1)
            act.activation(lamv[:, 2:4], lamv[:, 0:2], ACT.Exp).then_inc(s_lame, 1)
            act.activation(decay[:, :], decay[:, :], ACT.Exp).then_inc(s_decay, 1)

            for t in range(0, NT, 2):
                act.wait_ge(s_x[t], 16)
                if t >= 2:
                    act.wait_ge(s_sq, t // 2)
                act.activation(junk[:, :], xin[:, t, :], ACT.Square, accum_out=ssq[:, t:t + 1]).then_inc(s_sq, 1)
            act.wait_ge(s_rstd1, 1)
            for t in range(NT):
                if t in (1, 3):
                    hi_piece(t // 2, 1, t // 2)
                act.mul(xin[:, t, :], xin[:, t, :], rstd[:, t:t + 1]).then_inc(s_xs, 1)
            for n in range(2 * NT):
                act.wait_ge(s_ntc, n + 1)
                act.activation(xTh[:, 4 * (n % 2):4 * (n % 2) + 4, (n // 2) * P:(n // 2 + 1) * P],
                               junk[:, (n % 2) * 512:(n % 2 + 1) * 512].rearrange("p (c k) -> p c k", k=P),
                               ACT.Copy).then_inc(s_nth, 1)

            def z_out(i, m, t):
                n = 12 * i + 6 * m + t
                k = (6 * m + t) % 4
                act.wait_ge(s_zmm, n + 1)
                if not (isinstance(i, int) and i == 0 and 6 * m + t < 4):
                    act.wait_ge(s_zst[k], 48 * i + 16 * ((6 * m + t) // 4))
                act.activation(zst[k][:, :], ps[k][:, :], ACT.Copy).then_inc(s_zev, 1)

            def z_step(i, last=False):
                first = isinstance(i, int) and i == 0
                for m in range(2):
                    for t in range(NT):
                        z_out(i, m, t)
                        if t in (0, 2):
                            j = t // 2
                            if m == 0:
                                hi_piece(2 + j, i + 1, 2 + j,
                                         None if first else (s_zmm, 12 * i) if j else (s_pe, 2 * i))
                            elif not last:
                                hi_piece(j, i + 2, j, (s_zmm, 12 * i + 6) if j else (s_pe, 2 * i + 1))
            z_step(0)
            with act.Fori(1, NCH // 2 - 1) as i:
                z_step(i)
            act.wait_ge(s_warg, 1)
            act.activation(wdec[:, :, :], wdec[:, :, :], ACT.Exp).then_inc(s_wexp, 1)
            z_step(NCH // 2 - 1, last=True)
            act.wait_ge(s_gsub, 1)

            def columns_out(s):
                S = SEQ_NT[s] * P
                for g in range(12):
                    act.wait_ge(s_qT, 12 * s + g + 1)
                    if s == 0 and g == 0:
                        act.wait_ge(s_zmm, NCH * NT)
                    dst = qkT[:, g // 4, g % 4, 0:S] if g < 8 else rqkT[:, (g - 8) // 2, g % 2, 0:S]
                    act.activation(dst, ps[4 + 2 * (g % 2)][:, 0:S], ACT.Copy).then_inc(s_qTc, 1)

            n_sq = [0]

            def square(src, col):
                q = n_sq[0]
                n_sq[0] += 1
                if q >= 4:
                    act.wait_ge(s_osq, q - 3)
                act.activation(sqj[:, q % 4, :], src, ACT.Square, accum_out=ssq[:, col:col + 1]).then_inc(s_osq, 1)

            def attend(s, i0):
                nt = SEQ_NT[s]
                S = nt * P
                i1 = i0 + H * nt

                def exps(n):
                    act.wait_ge(s_mx, n + 1)
                    if n >= 2:
                        act.wait_ge(s_a, n - 1)
                    for c in range(2):
                        e = act.activation(prob[n % 2][:, c, 0:S], ps[2 * (n % 2) + c][:, 0:S], ACT.Exp,
                                           bias=nm[:, n % 2, c:c + 1], scale=HD ** -0.5,
                                           accum_out=sume[:, n % 2, c:c + 1])
                    e.then_inc(s_ex, 1)

                def squares(n):
                    _, h, qt = ITS[n]
                    act.wait_ge(s_oc, n + 1)
                    square(oun[:, qt, h * VD:(h + 1) * VD], 4 * qt + h)
                    if qt == nt - 1:
                        act.wait_ge(s_ryc, 4 * s + h + 1)
                        for t in range(nt):
                            square(yun[:, t, h * VD:(h + 1) * VD], 4 * nt + 4 * t + h)
                exps(i0)
                for n in range(i0, i1):
                    if n + 1 < i1:
                        exps(n + 1)
                    if n == 2:
                        for q in range(2):
                            act.wait_ge(s_zlv[q], 16 * 3)
                            act.activation(silu[q][:, :, :], zgr[q][:, :, :], ACT.Sigmoid).then_inc(s_sg, 1)
                    if n >= i0 + 2:
                        squares(n - 2)
                    act.wait_ge(s_aT, n + 1)
                    if n >= 2:
                        act.wait_ge(s_o, n - 1)
                    act.activation(attT[n % 2][:, 0:S], ps[4][:, 0:S], ACT.Copy).then_inc(s_aTc, 1)
                squares(i1 - 2)
                squares(i1 - 1)

            def normalise(s):
                act.wait_ge(s_rstd2, s + 1)
                nt = SEQ_NT[s]
                for h in range(H):
                    for t in range(nt):
                        v = oun[:, t, h * VD:(h + 1) * VD]
                        o = act.mul(v, v, rstd[:, 4 * t + h:4 * t + h + 1])
                    o.then_inc(s_on, 1)

            def columns_hi(s, b):
                for h in range(H):
                    act.wait_ge(s_oT, 8 * s + 4 * b + h + 1)
                    cols = slice(SEQ_T0[s] * P, (SEQ_T0[s] + SEQ_NT[s]) * P)
                    act.activation(oTh[b][:, h, cols], ps[5 + 2 * (h % 2)][:, 0:SEQ_NT[s] * P], ACT.Copy,
                                   scale=gsub[:, 0:1] if b == 0 else 1.0).then_inc(s_oTh, 1)

            columns_out(0)
            attend(0, 0)
            columns_out(1)
            normalise(0)
            columns_hi(0, 0)
            columns_hi(0, 1)
            attend(1, 16)
            normalise(1)
            for p in range(2):
                if p == 0:
                    act.wait_ge(s_ry, 24)
                    act.wait_ge(s_o, 24)
                hi_piece((3 + p) % RAWS, [6, 1][p], p)
            columns_hi(1, 0)
            columns_hi(1, 1)

            for p in range(2, 4):
                hi_piece((3 + p) % RAWS, [1, 6][p - 2], p)
            def out_hi(p):
                hi_piece((3 + p) % RAWS, [6, 6, 7, 2][p - 4], p % 4, (s_gs, (p // 2 - 1) * 2 * NT - (p + 1) % 2))
            for k in range(2 * NT):
                act.wait_ge(s_gl[k % 2], 16 * (k // 2 + 1))
                act.activation(gat[k % 2][:, :, :], gat[k % 2][:, :, :], ACT.Sigmoid).then_inc(s_sgm, 1)
                if k == NT + 1:
                    out_hi(4)
                    out_hi(5)
            out_hi(6)
            out_hi(7)
            def e_hi0(j):
                hi_piece(j, (7, 7, 7, 8, 3, 2)[j], j)

            def merged_hi(t):
                for j in range(2):
                    n = 2 * t + j
                    act.wait_ge(s_mT, n + 1)
                    if t >= 2:
                        act.wait_ge(s_w, 2 * (t - 1))
                    act.activation(mTh[t % 2][:, 4 * j:4 * j + 4, :].rearrange("p c k -> p (c k)"),
                                   ps[4 + n % 2][:, :], ACT.Copy).then_inc(s_mTh, 1)

            def route_copy(t):
                for j in range(2):
                    act.wait_ge(s_rTm, 2 * t + j + 1)
                    if t >= 1:
                        act.wait_ge(s_lg, t)
                    act.activation(rT[:, 4 * j:4 * j + 4, :].rearrange("p c k -> p (c k)"),
                                   ps[j][:, :], ACT.Copy).then_inc(s_rTc, 1)
            merged_hi(0)
            for t in range(NT):
                if t + 1 < NT:
                    merged_hi(t + 1)
                if t >= 1:
                    route_copy(t - 1)
                act.wait_ge(s_x2, 2 * t + 2)
                if t >= 2:
                    act.wait_ge(s_rst[t % 2], 16 * (t // 2))
                    act.wait_ge(s_rTm, 2 * (t - 1))
                act.activation(rrow[t % 2][:, :], x2[:, t, :], ACT.Square, accum_out=ssq[:, t:t + 1]).then_inc(s_sq2, 1)
            route_copy(NT - 1)
            for j in range(6):
                e_hi0(j)
            act.wait_ge(s_re, 1)
            act.activation(gq[:, 1, :, :], gq[:, 0, :, :], ACT.Exp).then_inc(s_re, 1)
            act.activation(v6[:, 3, :], v6[:, 2, :], ACT.Exp).then_inc(s_re, 1)

            act.wait_ge(s_nb, 1)
            nb = act.value_load(nbi[0:1, 0:1], min_val=NE, max_val=NB)

            def x_hi(n, j):
                act.wait_ge(s_eT, n * 2 + (j + 1))
                act.activation(eTh[:, 4 * j:4 * j + 4, :].rearrange("p c k -> p (c k)"), ps[2 + j][:, :],
                               ACT.Copy).then_inc(s_eTh, 1)

            def e_hi(b, j):
                freed = ((s_pe, 3 * b + NCH), (s_h1, 2 * b + 1), (s_pe, 3 * b + (NCH + 1)),
                         (s_h1, 2 * b + 2), (s_pe, 3 * b + (NCH + 2)), (s_y, b + 1))[j]
                hi_piece(j, b + (7, 7, 7, 8, 3, 2)[j], j, freed)

            def e_block(b, last):
                act.activation(sdum[:, :], cst[:, 0:1], ACT.Sigmoid)
                if not last:
                    e_hi(b + 1, 0)
                act.wait_ge(s_h1, 2 * b + 3)
                act.wait_ge(s_h, b + 1)
                act.activation(sg[:, :], ps[0][:, :], ACT.Sigmoid).then_inc(s_sgm, 1)
                if not last:
                    e_hi(b + 1, 1)
                    e_hi(b + 1, 2)
                act.wait_ge(s_hT, b + 2)
                act.wait_ge(s_y, b + 1)
                act.activation(hTh[:, :, :].rearrange("p c k -> p (c k)"), ps[4][:, :], ACT.Copy).then_inc(s_hTh, 1)
                if not last:
                    x_hi(b + 1, 0)
                    x_hi(b + 1, 1)
                    e_hi(b + 1, 3)
                    e_hi(b + 1, 4)
                act.wait_ge(s_y, b + 2)
                act.wait_ge(s_ys, 16 * b + 16 * NZ)
                for n in range(2):
                    act.activation(ystage[:, n * 512:(n + 1) * 512], ps[6 + n][:, :], ACT.Copy).then_inc(s_yc, 1)
                if not last:
                    e_hi(b + 1, 5)

            x_hi(0, 0)
            x_hi(0, 1)
            act.sem_inc(s_yc, 2)
            with act.Fori(0, nb - 1) as b:
                e_block(b, last=False)
            e_block(nb - 1, last=True)
            for t in range(NT):
                act.wait_ge(s_c2, t + 1)
                if t >= 2:
                    act.wait_ge(s_sq3, t - 1)
                act.activation(fj[t % 2][:, :], x2[:, t, :], ACT.Square, accum_out=ssq[:, t:t + 1]).then_inc(s_sq3, 1)

        @block.vector
        def _(dve):
            n_link = [0]

            def link(ins):
                n_link[0] += 1
                ins.then_inc(s_dv, 1)
                dve.wait_ge(s_dv, n_link[0])

            def lo_piece(slot_raw, slot, q):
                dve.wait_ge(s_hi, q)
                dve.tensor_tensor(elo[slot][:, :], raw[slot_raw][:, :], ehi[slot][:, :].bitcast(F32),
                                  ALU.subtract).then_inc(s_lo, 1)

            def rsqrt(c0, c1, n_mean, link):
                v, y, a = ssq[:, c0:c1], rstd[:, c0:c1], rs_a[:, c0:c1]
                link(dve.tensor_scalar(v, v, 1.0 / n_mean, EPS, ALU.mult, ALU.add))
                link(dve.tensor_scalar(a.bitcast(I32), v.bitcast(I32), 1, None, ALU.arith_shift_right))
                link(dve.tensor_scalar(y.bitcast(I32), a.bitcast(I32), -1.0, float(0x5f3759df), ALU.mult, ALU.add))
                for _ in range(3):
                    link(dve.scalar_tensor_tensor(out=a, in0=y, scalar=-0.5, in1=y, op0=ALU.mult, op1=ALU.mult))
                    link(dve.tensor_tensor(a, a, v, ALU.mult))
                    link(dve.scalar_tensor_tensor(out=y, in0=a, scalar=1.5, in1=y, op0=ALU.add, op1=ALU.mult))

            dve.wait_ge(s_par, 16 * 8)
            for k in range(2):
                link(dve.tensor_tensor_reduce(out=lamr[:, 2 * k, :], in0=lamr[:, 2 * k, :], in1=lamr[:, 2 * k + 1, :],
                                              scale=1.0, scalar=0.0, op0=ALU.mult, op1=ALU.add,
                                              accum_out=lamv[:, k:k + 1]))
            dve.sem_inc(s_lame, 1)
            dve.wait_ge(s_lame, 2)
            link(dve.tensor_tensor(lamv[:, 0:1], lamv[:, 3:4], lamv[:, 2:3], ALU.subtract))
            link(dve.tensor_scalar(lamv[:, 0:1], lamv[:, 0:1], -LAM_INIT, None, ALU.add))
            link(dve.tensor_scalar(gsub[:, :], gsub[:, :], 1.0 - LAM_INIT, None, ALU.mult))
            dve.sem_inc(s_gsub, 1)
            dve.wait_ge(s_decay, 1)
            link(dve.tensor_scalar(decay[:, 0:4], decay[:, 0:4], -1.0, None, ALU.mult))
            for t in range(1, NT, 2):
                dve.wait_ge(s_x[t], 16)
                link(dve.tensor_tensor_reduce(out=rt_sq[:, :], in0=xin[:, t, :], in1=xin[:, t, :], scale=1.0, scalar=0.0,
                                              op0=ALU.mult, op1=ALU.add, accum_out=ssq[:, t:t + 1]))
            dve.wait_ge(s_sq, NT // 2)
            rsqrt(0, NT, D, link)
            dve.sem_inc(s_rstd1, 1)
            for j in range(2):
                lo_piece(j, j, j + 1)

            def half_columns(n):
                return junk[:, n % 2 * 512:(n % 2 + 1) * 512].rearrange("p (c k) -> p c k", k=P)

            def input_gain(n):
                dve.wait_ge(s_nT, n + 1)
                if n >= 2:
                    dve.wait_ge(s_ntl, n - 1)
                    dve.wait_ge(s_nth, n - 1)
                dve.tensor_tensor(half_columns(n), ps[4 + n % 4][:, :].rearrange("p (c k) -> p c k", k=P),
                                  gn1[:, 4 * (n % 2):4 * (n % 2) + 4].unsqueeze(2).to_broadcast([P, 4, P]),
                                  ALU.mult).then_inc(s_ntc, 1)
            input_gain(0)
            for n in range(2 * NT):
                if n + 1 < 2 * NT:
                    input_gain(n + 1)
                dve.wait_ge(s_nth, n + 1)
                sl = (slice(None), slice(4 * (n % 2), 4 * (n % 2) + 4), slice(n // 2 * P, (n // 2 + 1) * P))
                dve.tensor_tensor(xTl[sl], half_columns(n), xTh[sl].bitcast(F32), ALU.subtract).then_inc(s_ntl, 1)
            for j in range(2, 4):
                lo_piece(j, j, j + 1)
            def z_lo(i):
                for j in range(4):
                    lo_piece(j, j, 4 * i + (j + 1))
            for h in range(H):
                link(dve.tensor_scalar(wdec[:, h, :], C("rel"), 0.0, decay[:, h:h + 1], ALU.max, ALU.mult))
                link(dve.tensor_scalar(junk[:, 0:RELW], C("rel"), 0.0, decay[:, 4 + h:5 + h], ALU.min, ALU.mult))
                link(dve.tensor_tensor(wdec[:, h, :], wdec[:, h, :], junk[:, 0:RELW], ALU.add))
            dve.sem_inc(s_warg, 1)
            with dve.Fori(1, NCH // 2 - 1) as i:
                z_lo(i)
            z_lo(NCH // 2 - 1)

            dve.wait_ge(s_zlq[0], 32)
            for t in range(4):
                v = zqk[0][:, t, :].rearrange("p (g d) -> p g d", d=HD)
                rotary(dve, link, v, 8, C("cosA")[:, t * 8:(t + 1) * 8], C("sinA")[:, t * 8:(t + 1) * 8], rt_v)
                for k in range(2):
                    v = zr[0][:, t, k * 256:(k + 1) * 256].rearrange("p (g d) -> p g d", d=HD)
                    rotary(dve, link, v, 32, C("cosR")[:, t * 32:(t + 1) * 32], C("sinR")[:, t * 32:(t + 1) * 32],
                           rt_v)
            dve.sem_inc(s_rotv, 1)

            def attend(s, i0):
                nt = SEQ_NT[s]
                S = nt * P
                i1 = i0 + H * nt

                def maxes(n):
                    b = 2 * (n % 2)
                    dve.wait_ge(s_sc, n + 1)
                    dve.tensor_reduce(mx[:, n % 2, 0:1], ps[b][:, 0:S], AX.X, ALU.max)
                    link(dve.tensor_reduce(mx[:, n % 2, 1:2], ps[b + 1][:, 0:S], AX.X, ALU.max))
                    dve.tensor_scalar(nm[:, n % 2, :], mx[:, n % 2, :], -HD ** -0.5, None,
                                      ALU.mult).then_inc(s_mx, 1)

                def weights(n):
                    dve.wait_ge(s_ex, n + 1)
                    if n >= 2:
                        dve.wait_ge(s_aT, n - 1)
                        dve.wait_ge(s_oc, n - 1)
                    link(dve.reciprocal(rc[:, n % 2, :], sume[:, n % 2, :]))
                    link(dve.scalar_tensor_tensor(out=rc[:, n % 2, 1:2], in0=rc[:, n % 2, 1:2], scalar=lamv[:, 0:1],
                                                  in1=sume[:, n % 2, 0:1], op0=ALU.mult, op1=ALU.mult))
                    dve.scalar_tensor_tensor(out=att[n % 2][:, 0:S], in0=prob[n % 2][:, 1, 0:S],
                                             scalar=rc[:, n % 2, 1:2], in1=prob[n % 2][:, 0, 0:S],
                                             op0=ALU.mult, op1=ALU.add).then_inc(s_a, 1)

                def decayed(n):
                    _, h, kt = ITS[n]
                    dve.wait_ge(s_rs, n + 1)
                    if n >= 2:
                        dve.wait_ge(s_ry, n - 1)
                    dve.scalar_tensor_tensor(out=smk[n % 2][:, 0:S], in0=ps[6][:, 0:S], scalar=HD ** -0.5,
                                             in1=wdec[:, h, (3 - kt) * P:(3 - kt) * P + S],
                                             op0=ALU.mult, op1=ALU.mult).then_inc(s_rm, 1)

                def outputs(n):
                    _, h, qt = ITS[n]
                    dve.wait_ge(s_o, n + 1)
                    dve.tensor_scalar(oun[:, qt, h * VD:(h + 1) * VD], ps[5][:, (n % 4) * VD:(n % 4 + 1) * VD],
                                      rc[:, n % 2, 0:1], None, ALU.mult).then_inc(s_oc, 1)
                    if qt == nt - 1:
                        dve.wait_ge(s_ry, n + 1)
                        dve.tensor_copy(yun[:, 0:nt, h * VD:(h + 1) * VD],
                                        ps[7][:, 0:S].rearrange("p (t v) -> p t v", v=VD)).then_inc(s_ryc, 1)
                maxes(i0)
                for n in range(i0, i1):
                    weights(n)
                    if n + 1 < i1:
                        maxes(n + 1)
                    decayed(n)
                    if n > i0:
                        outputs(n - 1)
                outputs(i1 - 1)

            def normalise(s):
                nt = SEQ_NT[s]
                w = 8 * nt
                dve.wait_ge(s_osq, w if s == 0 else 32 + w)
                rsqrt(0, w, VD, link)
                dve.sem_inc(s_rstd2, 1)
                dve.wait_ge(s_silu, s + 1)
                for h in range(H):
                    for t in range(nt):
                        v = yun[:, t, h * VD:(h + 1) * VD]
                        o = dve.scalar_tensor_tensor(out=v, in0=v, scalar=rstd[:, 4 * nt + 4 * t + h:4 * nt + 4 * t + h + 1],
                                                     in1=silu[s][:, t, h * VD:(h + 1) * VD],
                                                     op0=ALU.mult, op1=ALU.mult)
                    o.then_inc(s_ony, 1)

            def columns_lo(s, b):
                for h in range(H):
                    O = 8 * s + 4 * b + h
                    dve.wait_ge(s_oTh, O + 1)
                    cols = slice(SEQ_T0[s] * P, (SEQ_T0[s] + SEQ_NT[s]) * P)
                    dve.scalar_tensor_tensor(out=oTl[b][:, h, cols], in0=ps[5 + 2 * (h % 2)][:, 0:SEQ_NT[s] * P],
                                             scalar=gsub[:, 0:1] if b == 0 else 1.0,
                                             in1=oTh[b][:, h, cols].bitcast(F32),
                                             op0=ALU.mult, op1=ALU.subtract).then_inc(s_oTl, 1)

            dve.wait_ge(s_wexp, 1)
            for k in range(4):
                dve.wait_ge(s_zst[k], 16 * NCH * NT // 4)
            attend(0, 0)
            normalise(0)
            columns_lo(0, 0)
            columns_lo(0, 1)
            attend(1, 16)
            normalise(1)
            for p in range(2):
                lo_piece((3 + p) % RAWS, p, ZP + p + 1)
            columns_lo(1, 0)
            columns_lo(1, 1)

            for p in range(2, 4):
                lo_piece((3 + p) % RAWS, p, ZP + p + 1)
            for n in range(4 * NT):
                k, b = n // 2, n % 2
                g = gat[k % 2][:, b, :]
                dst = mg[:, k % NT, k // NT * 512:k // NT * 512 + 512]
                if b == 0:
                    dve.wait_ge(s_sgm, k + 1)
                dve.wait_ge(s_gs, n + 1)
                if b == 0:
                    dve.tensor_tensor(dst, ps[n % 4][:, :], g, ALU.mult).then_inc(s_pm, 1)
                else:
                    if k >= 2:
                        dve.wait_ge(s_mgd, k - 1)
                    dve.tensor_tensor(prd[k % 2][:, :], ps[n % 4][:, :], g, ALU.mult).then_inc(s_pm, 1)
                    dve.wait_ge(s_pm, n + 1)
                    dve.tensor_tensor(dst, dst, prd[k % 2][:, :], ALU.add).then_inc(s_mgd, 1)
                if n == 2 * NT + 5:
                    for p in range(4, 6):
                        lo_piece((3 + p) % RAWS, p % 4, ZP + p + 1)
            for p in range(6, 8):
                lo_piece((3 + p) % RAWS, p % 4, ZP + p + 1)
            def merged_lo(t):
                for j in range(2):
                    n = 2 * t + j
                    dve.wait_ge(s_mTh, n + 1)
                    dve.tensor_tensor(mTl[t % 2][:, 4 * j:4 * j + 4, :].rearrange("p c k -> p (c k)"),
                                      ps[4 + n % 2][:, :],
                                      mTh[t % 2][:, 4 * j:4 * j + 4, :].rearrange("p c k -> p (c k)").bitcast(F32),
                                      ALU.subtract).then_inc(s_mTl, 1)
            def route_logits(t):
                dve.wait_ge(s_lg, t + 1)
                dve.tensor_tensor(lg[:, t, :], ps[2][:, 0:NG + NE], brt[:, :], ALU.add).then_inc(s_rx, 1)
            merged_lo(0)
            for t in range(NT):
                if t + 1 < NT:
                    merged_lo(t + 1)
                dve.wait_ge(s_xr, 16 * (t + 1))
                for n in range(2):
                    dve.wait_ge(s_w, 2 * t + n + 1)
                    dve.tensor_tensor(x2[:, t, n * 512:(n + 1) * 512], ps[6 + n][:, :],
                                      xres[:, n * 512:(n + 1) * 512], ALU.add).then_inc(s_x2, 1)
                dve.wait_ge(s_sq2, t + 1)
                rsqrt(t, t + 1, D, link)
                if t == 0:
                    dve.wait_ge(s_rp, 16 * 8)
                dve.scalar_tensor_tensor(out=rrow[t % 2][:, :], in0=x2[:, t, :], scalar=rstd[:, t:t + 1],
                                         in1=g2[:, :], op0=ALU.mult, op1=ALU.mult).then_inc(s_rr, 1)
                if t >= 1:
                    route_logits(t - 1)
            route_logits(NT - 1)
            dve.wait_ge(s_rx, NT)

            def b4(v):
                return v.unsqueeze(2).to_broadcast([P, NT, NG])

            def b32(v):
                return v.unsqueeze(2).to_broadcast([P, NT, NE])

            grp = lg[:, :, 0:NG]
            link(dve.tensor_reduce(v6[:, 0, :], grp, AX.X, ALU.max))
            link(dve.tensor_tensor(gq[:, 0, :, :], grp, b4(v6[:, 0, :]), ALU.subtract))
            link(dve.scalar_tensor_tensor(out=gq[:, 2, :, :], in0=gq[:, 0, :, :], scalar=0.0,
                                          in1=C("grank").unsqueeze(1).to_broadcast([P, NT, NG]),
                                          op0=ALU.is_equal, op1=ALU.mult))
            link(dve.tensor_reduce(v6[:, 1, :], gq[:, 2, :, :], AX.X, ALU.max))
            link(dve.tensor_tensor(gq[:, 3, :, :], gq[:, 2, :, :], b4(v6[:, 1, :]), ALU.is_equal))
            BIG = 1.0e30
            link(dve.tensor_scalar(gq[:, 3, :, :], gq[:, 3, :, :], -1.0, BIG, ALU.add, ALU.mult))
            link(dve.tensor_tensor(sel[:, :, :].rearrange("p t (g e) -> p t g e", e=EPG),
                                   lg[:, :, NG:].rearrange("p t (g e) -> p t g e", e=EPG),
                                   gq[:, 3, :, :].unsqueeze(3).to_broadcast([P, NT, NG, EPG]), ALU.add))

            def pick(out, vals, top):
                link(dve.tensor_reduce(top, vals, AX.X, ALU.max))
                link(dve.tensor_tensor(t1[:, :, :], vals, b32(top), ALU.is_equal))
                link(dve.tensor_tensor(t1[:, :, :], t1[:, :, :], C("erank").unsqueeze(1).to_broadcast([P, NT, NE]),
                                       ALU.mult))
                link(dve.tensor_reduce(v6[:, 4, :], t1[:, :, :], AX.X, ALU.max))
                link(dve.tensor_tensor(out, t1[:, :, :], b32(v6[:, 4, :]), ALU.is_equal))

            pick(A1[:, :, :], sel[:, :, :], v6[:, 5, :])
            link(dve.scalar_tensor_tensor(out=sel[:, :, :], in0=A1[:, :, :], scalar=-BIG, in1=sel[:, :, :],
                                          op0=ALU.mult, op1=ALU.add))
            pick(A2[:, :, :], sel[:, :, :], v6[:, 6, :])
            link(dve.tensor_tensor(Ab[:, :, :], A1[:, :, :], A2[:, :, :], ALU.add))
            dve.sem_inc(s_Ab, 1)
            dve.memset(quarters[:, :], 3)
            link(dve.memset(run[:, :, :], 0.0))
            link(dve.tensor_tensor(v6[:, 2, :], v6[:, 6, :], v6[:, 5, :], ALU.subtract))
            dve.sem_inc(s_re, 1)
            dve.wait_ge(s_rk, 1)
            cnt = ps[3][:, NT * NE:(NT + 1) * NE]
            over = bt[:, 0:NE * (MAXB - 1)].rearrange("p (e j) -> p e j", j=MAXB - 1)
            link(dve.tensor_tensor(over, cnt.unsqueeze(2).to_broadcast([P, NE, MAXB - 1]),
                                   C("thr").unsqueeze(1).to_broadcast([P, NE, MAXB - 1]), ALU.is_gt))
            link(dve.tensor_reduce(nov[:, :], over, AX.X, ALU.add))
            more = bt[0:1, 0:NE * 3].rearrange("p (e j) -> p e j", j=3)
            link(dve.tensor_tensor(more, cnt[0:1, :].unsqueeze(2).to_broadcast([1, NE, 3]),
                                   C("quart")[0:1, :].unsqueeze(1).to_broadcast([1, NE, 3]), ALU.is_gt))
            link(dve.tensor_reduce(bts[:, 0:NE], more, AX.X, ALU.add))
            dve.tensor_copy(quarters[:, 0:NE], bts[:, 0:NE])
            Z0 = NE // 2
            link(dve.tensor_copy(run[:, 0, Z0:], nov[:, :]))
            a, d = 0, 1
            while d < NE:
                link(dve.tensor_tensor(run[:, 1 - a, Z0:], run[:, a, Z0:], run[:, a, Z0 - d:Z0 + NE - d], ALU.add))
                a, d = 1 - a, 2 * d
            incl = run[:, a, Z0:]
            link(dve.tensor_tensor(ovb[:, :], incl, nov[:, :], ALU.subtract))
            link(dve.tensor_scalar(ovb[:, :], ovb[:, :], float(CAP), float((NE - 1) * CAP), ALU.mult, ALU.add))
            link(dve.tensor_tensor(ovb[:, :], ovb[:, :], C("e128"), ALU.subtract))
            rank = ps[3][:, 0:NT * NE].rearrange("p (t e) -> p t e", e=NE)
            link(dve.scalar_tensor_tensor(out=t1[:, :, :], in0=rank, scalar=float(CAP),
                                          in1=ovb[:, :].unsqueeze(1).to_broadcast([P, NT, NE]),
                                          op0=ALU.is_ge, op1=ALU.mult))
            link(dve.tensor_tensor(t1[:, :, :], t1[:, :, :], rank, ALU.add))
            link(dve.tensor_tensor(t1[:, :, :], t1[:, :, :], C("e128").unsqueeze(1).to_broadcast([P, NT, NE]), ALU.add))
            for k, Ak in enumerate((A1, A2)):
                link(dve.tensor_tensor(t2[:, :, :], t1[:, :, :], Ak[:, :, :], ALU.mult))
                link(dve.tensor_reduce(slotf[:, k, :], t2[:, :, :], AX.X, ALU.add))
            link(dve.tensor_copy(sloti[:, :, :], slotf[:, :, :]))
            bp = bt[:, 0:4 * NT].bitcast(U32).rearrange("p (a k t) -> p a k t", a=2, k=2)
            dve.tensor_scalar(bp[:, 0, :, :], sloti[:, :, :], 7, None, ALU.logical_shift_right)
            link(dve.tensor_scalar(bp[:, 1, :, :], sloti[:, :, :], CAP - 1, None, ALU.bitwise_and))
            link(dve.tensor_copy(sbf[:, :, :, :], bp))
            for q in range(2 * NT):
                k, t = q // NT, q % NT
                if q >= NT:
                    dve.wait_ge(s_tbm, q - NT + 1)
                dve.tensor_scalar(Rt[:, t, :], C("iota"), sbf[:, 1, k, t:t + 1], None, ALU.is_equal)
                dve.tensor_scalar(Bt[:, q, :], C("iota")[:, 0:NB + 1], sbf[:, 0, k, t:t + 1],
                                  C("tok")[:, t:t + 1], ALU.is_equal, ALU.mult).then_inc(s_tb, 1)
            dve.wait_ge(s_tb, 2 * NT)
            bto = bt[0:1, :].rearrange("p (m e) -> p m e", e=NE)
            link(dve.tensor_tensor(bto, run[0:1, a, Z0:].unsqueeze(1).to_broadcast([1, NOV, NE]),
                                   C("iota")[0:1, 0:NOV].unsqueeze(2).to_broadcast([1, NOV, NE]), ALU.is_le))
            link(dve.tensor_reduce(bts[:, 0:NOV], bto, AX.X, ALU.add))
            link(dve.tensor_scalar(nbi[:, 1:1 + NOV], bts[:, 0:NOV], float(NE - 1), None, ALU.min))
            link(dve.tensor_scalar(nbi[:, 0:1], run[0:1, a, Z0 + NE - 1:Z0 + NE], float(NE), None, ALU.add))
            dve.wait_ge(s_tbm, 2 * NT)
            link(dve.tensor_copy(idxt[:, :], ps[4][:, 0:NB + 1]))
            dve.sem_inc(s_nb, 1)
            dve.wait_ge(s_re, 3)
            link(dve.tensor_reduce(v6[:, 7, :], gq[:, 1, :, :], AX.X, ALU.add))
            link(dve.tensor_scalar(v6[:, 8, :], v6[:, 3, :], 1.0, None, ALU.add))
            link(dve.tensor_tensor(v6[:, 7, :], v6[:, 7, :], v6[:, 8, :], ALU.mult))
            link(dve.reciprocal(gates[:, 0, :], v6[:, 7, :]))
            link(dve.tensor_tensor(gates[:, 1, :], gates[:, 0, :], v6[:, 3, :], ALU.mult))

            nb = dve.value_load(nbi[0:1, 0:1], min_val=NE, max_val=NB)

            def x_lo(n, j):
                dve.wait_ge(s_eTh, n * 2 + (j + 1))
                dve.tensor_tensor(eTl[:, 4 * j:4 * j + 4, :].rearrange("p c k -> p (c k)"), ps[2 + j][:, :],
                                  eTh[:, 4 * j:4 * j + 4, :].rearrange("p c k -> p (c k)").bitcast(F32),
                                  ALU.subtract).then_inc(s_eTl, 1)

            def e_lo(b, j):
                lo_piece(j, j, 6 * b + (PRE + j + 1))

            def e_block(b, last):
                if not last:
                    e_lo(b + 1, 0)
                dve.wait_ge(s_sgm, b + (2 * NT + 1))
                dve.wait_ge(s_hT, b + 1)
                dve.tensor_tensor(hh[:, :], ps[0][:, :], sg[:, :], ALU.mult).then_inc(s_h13, 1)
                dve.wait_ge(s_h13, b + 1)
                dve.wait_ge(s_h1, 2 * b + 4)
                dve.tensor_tensor(hh[:, :], ps[1][:, :], hh[:, :], ALU.mult).then_inc(s_h, 1)
                dve.wait_ge(s_hTh, b + 1)
                dve.tensor_tensor(hTl[:, :, :].rearrange("p c k -> p (c k)"), ps[4][:, :],
                                  hTh[:, :, :].rearrange("p c k -> p (c k)").bitcast(F32),
                                  ALU.subtract).then_inc(s_hTl, 1)
                if not last:
                    x_lo(b + 1, 0)
                    x_lo(b + 1, 1)
                    for j in (2, 3, 4, 5):
                        e_lo(b + 1, j)

            dve.wait_ge(s_lo, PRE + 3)
            dve.wait_ge(s_rst[0], 16 * NT // 2)
            for j in range(4, 6):
                e_lo(0, j)
            x_lo(0, 0)
            x_lo(0, 1)
            dve.sem_inc(s_h, 1)
            with dve.Fori(0, nb - 1) as b:
                e_block(b, last=False)
            e_block(nb - 1, last=True)
            def last_norm(t0):
                dve.wait_ge(s_sq3, t0 + 2)
                rsqrt(t0, t0 + 2, D, link)
                for t in range(t0, t0 + 2):
                    dve.scalar_tensor_tensor(out=yo[t][:, :], in0=x2[:, t, :], scalar=rstd[:, t:t + 1],
                                             in1=gf[:, :], op0=ALU.mult, op1=ALU.mult).then_inc(s_yf, 1)
            for t in range(NT):
                dve.wait_ge(s_g1[t], 32)
                link(dve.scalar_tensor_tensor(out=x2[:, t, :], in0=ya[t][0][:, :], scalar=gates[:, 0, t:t + 1],
                                              in1=x2[:, t, :], op0=ALU.mult, op1=ALU.add))
                dve.scalar_tensor_tensor(out=x2[:, t, :], in0=ya[t][1][:, :], scalar=gates[:, 1, t:t + 1],
                                         in1=x2[:, t, :], op0=ALU.mult, op1=ALU.add).then_inc(s_c2, 1)
                if t == 2:
                    dve.wait_ge(s_gf, 16)
                if t >= 2 and t % 2 == 0:
                    last_norm(t - 2)
            last_norm(NT - 2)

        @block.gpsimd
        def _(pool):
            def z_store(i, u):
                pool.wait_ge(s_zev, 12 * i + (u + 1))
                pool.dma_start(z_d[(u % 6) * P:(u % 6 + 1) * P, bass.ds(i * 1024 + (u // 6) * 512, 512)],
                               zst[u % 4][:, :]).then_inc(s_zst[u % 4], 16)
            with pool.Fori(0, NCH // 2) as i:
                for u in range(12):
                    z_store(i, u)
            n_link = [0]

            def link(ins):
                n_link[0] += 1
                ins.then_inc(s_pl, 1)
                pool.wait_ge(s_pl, n_link[0])

            def rotary_r(s, t):
                for k in range(2):
                    rotary(pool, link, zr[s][:, t, k * 256:(k + 1) * 256].rearrange("p (g d) -> p g d", d=HD), 32,
                           C("cosR")[:, t * 32:(t + 1) * 32], C("sinR")[:, t * 32:(t + 1) * 32], rt_p)

            def silu_steps(s):
                pool.wait_ge(s_sg, s + 1)
                pool.tensor_tensor(silu[s][:, :, :], silu[s][:, :, :], zgr[s][:, :, :], ALU.mult).then_inc(s_silu, 1)
            silu_steps(0)
            pool.wait_ge(s_zlq[1], 32)
            pool.wait_ge(s_warg, 1)
            for t in range(2):
                rotary(pool, link, zqk[1][:, t, :].rearrange("p (g d) -> p g d", d=HD), 8,
                       C("cosA")[:, t * 8:(t + 1) * 8], C("sinA")[:, t * 8:(t + 1) * 8], rt_p)
                rotary_r(1, t)
            pool.sem_inc(s_rotp, 1)
            silu_steps(1)
            pool.memset(zrow[:, :], 0.0).then_inc(s_zr, 1)
            pool.wait_ge(s_zr, 1)
            by_quarter = y_d.rearrange("(e q r) n -> q e (r n)", q=4, r=QR)
            for q, e0, e1 in ZEROS:
                pool.dma_start(by_quarter[q, e0:e1].rearrange("e (p c) -> p e c", c=256),
                               zrow[:, :].unsqueeze(1).to_broadcast([P, e1 - e0, 256])).then_inc(s_ys, 16)
            for t in range(NT):
                pool.wait_ge(s_rr, t + 1)
                pool.dma_start(xn_d[t * P:(t + 1) * P, :], rrow[t % 2][:, :]).then_inc(s_rst[t % 2], 16)
            for j in range(4):
                pool.wait_ge(s_hi, PRE + j + 1)
                pool.tensor_tensor(elo[j][:, :], raw[j][:, :], ehi[j][:, :].bitcast(F32),
                                   ALU.subtract).then_inc(s_lo1 if j == 1 else s_lo, 1)
            for k in range(2):
                pool.wait_ge(s_rst[k], 16 * NT // 2)
            pool.wait_ge(s_nb, 1)
            nb = pool.value_load(nbi[0:1, 0:1], min_val=NE, max_val=NB)

            def rows_in(n):
                pool.indirect_dma_start(out=xg[0:n, :], out_offset=None, in_=xn_d,
                                        in_offset=bass.IndirectOffsetOnAxis(ap=idxb[0:n, 0:1], axis=0)).then_inc(s_gx, 16)

            def gather(b):
                pool.tensor_copy(idxb[:, :], idxt[:, bass.ds(b, 1)]).then_inc(s_ic, 1)
                pool.wait_ge(s_ic, b + 1)
                pool.sem_inc(s_idx, 1)
                if isinstance(b, int) and b == 0:
                    rows_in(CAP)
                else:
                    q = pool.value_load(quarters[0:1, bass.ds(b, 1)], min_val=0, max_val=3)
                    for k in range(4):
                        with pool.If(q == k):
                            rows_in((k + 1) * QR)

            def store(b):
                pool.wait_ge(s_yc, 2 * b + 4)
                q = pool.value_load(quarters[0:1, bass.ds(b, 1)], min_val=0, max_val=3)
                for k in range(4):
                    n = (k + 1) * QR
                    with pool.If(q == k):
                        pool.dma_start(y_d[bass.ds(b * CAP, n), :], ystage[0:n, :]).then_inc(s_ys, 16)
            gather(0)
            pool.wait_ge(s_eT, 2)
            gather(1)
            with pool.Fori(0, nb - 1) as b:
                pool.wait_ge(s_hi, 6 * b + (PRE + 8))
                pool.tensor_tensor(elo[1][:, :], raw[1][:, :], ehi[1][:, :].bitcast(F32),
                                   ALU.subtract).then_inc(s_lo1, 1)
                pool.wait_ge(s_eT, 2 * b + 4)
                gather(b + 2)
                store(b)
            store(nb - 1)
            pool.wait_ge(s_ys, 16 * nb + 16 * NZ)
            pool.wait_ge(s_gx, 16 * nb + 16)
            pool.sem_inc(s_md, 1)
            for t in range(NT):
                for k in range(2):
                    pool.indirect_dma_start(out=ya[t][k][:, :], out_offset=None, in_=y_d,
                                            in_offset=bass.IndirectOffsetOnAxis(ap=sloti[:, k, t:t + 1], axis=0)
                                            ).then_inc(s_g1[t], 16)


_INS = ['x_prompt', 'x_sample', 'attn_norm_g', 'w_in', 'lam_q1', 'lam_k1', 'lam_q2', 'lam_k2', 'subln_g',
        'ret_decay_f', 'ret_decay_b', 'w_pa', 'w_pb', 'w_out', 'ffn_norm_g', 'w_rg', 'b_rg', 'w_re', 'b_re',
        'w1', 'w3', 'w2', 'final_norm_g']
_OUTS = [('y_prompt', (1, 512, D)), ('y_sample', (1, 256, D))]


def kernel(**inputs):
    import numpy as _np
    import concourse.bacc as _bacc
    from concourse import mybir as _mybir
    from concourse.bass_utils import run_bass_kernel_spmd as _run

    nc = _bacc.Bacc("TRN2", target_bir_lowering=False, num_devices=1)
    arrays, aps = {}, {}
    for name in _INS + ["consts"]:
        a = constants() if name == "consts" else _np.ascontiguousarray(inputs[name])
        arrays[f"in_{name}"] = a
        aps[name] = nc.dram_tensor(f"in_{name}", a.shape, _mybir.dt.from_np(a.dtype), kind="ExternalInput").ap()
    for name, shape in _OUTS:
        aps[name] = nc.dram_tensor(f"out_{name}", shape, _mybir.dt.float32, kind="ExternalOutput").ap()
    hybrid_layer(nc, aps)
    r = _run(nc, [arrays], core_ids=[0])
    return tuple(r.results[0][f"out_{name}"] for name, _ in _OUTS)
```

```python
from contextlib import ExitStack

import concourse.bass as bass
from concourse import mybir

F32 = mybir.dt.float32
F32R = mybir.dt.float32r
I32 = mybir.dt.int32
U32 = mybir.dt.uint32
ALU = mybir.AluOpType
ACT = mybir.ActivationFunctionType
AX = mybir.AxisListType

P = 128
D = 1024
KC = D // P
SEQS = (512, 256)
T = sum(SEQS)
NT = T // P
H = 4
HD = 64
VD = 128
D_IN = 5120
NCH = D_IN // 512
C_Q, C_V, C_R, C_VR, C_GR, C_GA, C_GB = 0, 1024, 1536, 2048, 2560, 3072, 4096
NG, EPG = 4, 8
NE = NG * EPG
FF = 512
CAP = 128
MAXB = T // CAP
NOV = (2 * T) // (CAP + 1)
NB = NE + NOV
QR = CAP // 4
EPS = 1e-6
LAM_INIT = 0.8 - 0.6
KB = 1024
RELW = 7 * P
PIECE = 2048
RAWS = 6
HLS = 4
ZP = 2 * NCH
PP = 8
PRE = ZP + PP
P_HI = (3, 0, 1, 2)
P_LO = (0, 1, 2, 3)

_c = {}
_n = 0
for _name, _w in (("ident", P), ("tri", P), ("ones", P), ("rel", RELW), ("cosA", 32), ("sinA", 32),
                  ("cosR", 128), ("sinR", 128), ("e128", NE), ("grank", NG), ("erank", NE),
                  ("iota", P), ("thr", MAXB - 1), ("quart", 3), ("tok", NT)):
    _c[_name] = (_n, _n + _w)
    _n += _w
NCST = _n


def constants():
    import numpy as np
    t = np.zeros((P, NCST), np.float32)

    def put(name, v):
        a, b = _c[name]
        t[:, a:b] = v
    i = np.arange(P)
    put("ident", np.eye(P))
    put("tri", (i[:, None] < i[None, :]).astype(np.float32))
    put("ones", 1.0)
    put("rel", np.arange(RELW)[None, :] - 3 * P - i[:, None])
    for rot, theta, cn, sn in ((16, 500000.0, "cosA", "sinA"), (64, 10000.0, "cosR", "sinR")):
        inv = np.float32(theta) ** (-np.arange(0, rot, 2, dtype=np.float32) / np.float32(rot))
        inv = inv.astype(np.float32)
        ang = (np.arange(512, dtype=np.float32)[:, None] * inv[None, :]).astype(np.float32)
        for f, n in ((np.cos, cn), (np.sin, sn)):
            v = f(ang.astype(np.float64)).astype(np.float32).reshape(4, P, rot // 2)
            put(n, v.transpose(1, 0, 2).reshape(P, -1))
    e = np.arange(NE)
    put("e128", e * CAP)
    put("grank", NG - np.arange(NG))
    put("erank", EPG - e % EPG)
    put("iota", np.arange(P))
    put("thr", CAP * np.arange(1, MAXB))
    put("quart", QR * np.arange(1, 4))
    put("tok", i[:, None] + P * np.arange(NT)[None, :])
    return t


def hybrid_layer(nc, A):
    ctx = ExitStack()
    base = (nc.sbuf_base + 63) // 64 * 64
    RAW_O, HL_O, D_O, E_O = 0, 48 * KB, 112 * KB, 160 * KB

    def at(name, off, shape, dt=F32):
        return nc.alloc_sbuf_tensor_at(name, shape, dt, offset=base + off)

    raw = [at(f"raw{s}", RAW_O + s * 8 * KB, [P, PIECE]) for s in range(RAWS)]
    whi = [at(f"whi{s}", HL_O + s * 8 * KB, [P, PIECE], F32R) for s in range(HLS)]
    wlo = [at(f"wlo{s}", HL_O + (HLS + s) * 8 * KB, [P, PIECE], F32R) for s in range(HLS)]
    xTh = at("xTh", D_O, [P, KC, T], F32R)
    xTl = at("xTl", D_O + 24 * KB, [P, KC, T], F32R)
    oTh = [at(f"oTh{b}", D_O + b * 12 * KB, [P, H, T], F32R) for b in range(2)]
    oTl = [at(f"oTl{b}", D_O + (2 + b) * 12 * KB, [P, H, T], F32R) for b in range(2)]
    mTh = [at(f"mTh{s}", D_O + s * 4 * KB, [P, KC, P], F32R) for s in range(2)]
    mTl = [at(f"mTl{s}", D_O + 8 * KB + s * 4 * KB, [P, KC, P], F32R) for s in range(2)]
    x2 = at("x2", D_O + 16 * KB, [P, NT, D])
    CST_O = E_O
    cst = at("cst", CST_O, [P, NCST])
    W_O = CST_O + (NCST * 4 + 63) // 64 * 64
    off = [W_O]

    def small(name, shape, dt=F32):
        n = 4
        for s in shape[1:]:
            n *= s
        t = at(name, off[0], shape, dt)
        off[0] += (n + 31) // 32 * 32
        return t
    gn1 = small("gn1", [P, KC])
    ssq = small("ssq", [P, 32])
    rstd = small("rstd", [P, 32])
    rs_a = small("rs_a", [P, 32])
    gsub = small("gsub", [P, 1])
    lamv = small("lamv", [P, 4])
    decay = small("decay", [P, 8])
    mx = small("mx", [P, 2, 2])
    nm = small("nm", [P, 2, 2])
    sume = small("sume", [P, 2, 2])
    rc = small("rc", [P, 2, 2])
    gates = small("gates", [P, 2, NT])
    slotf = small("slotf", [P, 2, NT])
    sloti = small("sloti", [P, 2, NT], U32)
    idxt = small("idxt", [P, NB + 1], I32)
    gq = small("gq", [P, 4, NT, NG])
    v6 = small("v6", [P, 9, NT])
    nbi = small("nbi", [1, 1], I32)
    quarters = small("quarters", [1, NB + 1], I32)
    served = small("served", [1, NB + 1], I32)
    bcol = small("bcol", [P, 8])
    idxb = small("idxb", [P, 1], I32)
    sdum = small("sdum", [P, 1])
    F_O = off[0]
    FREE = 212800 - F_O
    assert FREE >= 36 * KB + 2400, FREE
    xin = at("xin", F_O, [P, NT, D])
    zst = [at(f"zst{s}", F_O + 24 * KB + s * 2 * KB, [P, 512]) for s in range(4)]
    junk = at("junk", F_O + 32 * KB, [P, D])
    sqx = [at(f"sqx{s}", F_O + (24 + 4 * s) * KB, [P, D]) for s in range(2)]
    zrow = at("zrow", F_O + 36 * KB, [P, 256])
    lamr = at("lamr", F_O + 36 * KB, [P, 4, HD])
    rt_v = at("rt_v", F_O + 32 * KB, [P, 4, 128])
    rt_p = at("rt_p", F_O + 36 * KB, [P, 4, 128])
    zqk = [at("zqk0", F_O, [P, 4, 1024]), at("zqk1", RAW_O, [P, 2, 1024])]
    zr = [at("zr0", F_O + 16 * KB, [P, 4, 512]), at("zr1", RAW_O + 8 * KB, [P, 2, 512])]
    zv = [at("zv0", HL_O + 24 * KB, [P, 4, 512]), at("zv1", RAW_O + 12 * KB, [P, 2, 512])]
    zvr = [at("zvr0", HL_O + 32 * KB, [P, 4, 512]), at("zvr1", RAW_O + 16 * KB, [P, 2, 512])]
    zgr = [at("zgr0", HL_O + 40 * KB, [P, 4, 512]), at("zgr1", RAW_O + 20 * KB, [P, 2, 512])]
    silu = [at("silu0", HL_O + 48 * KB, [P, 4, 512]), at("silu1", HL_O + 56 * KB, [P, 2, 512])]
    sqj = at("sqj", HL_O + 60 * KB, [P, 4, VD])
    qkT = at("qkT", HL_O, [P, 2, H, 512])
    rqkT = at("rqkT", HL_O + 16 * KB, [P, 2, 2, 512])
    wdec = at("wdec", RAW_O + 32 * KB, [P, H, RELW])
    prob = [at(f"prob{s}", F_O + s * 4 * KB, [P, 2, 512]) for s in range(2)]
    att = [at(f"att{s}", F_O + 8 * KB + s * 2 * KB, [P, 512]) for s in range(2)]
    attT = [at(f"attT{s}", F_O + 12 * KB + s * 2 * KB, [P, 512]) for s in range(2)]
    smk = [at(f"smk{s}", F_O + 16 * KB + s * 2 * KB, [P, 512]) for s in range(2)]
    oun = [at("oun0", F_O + 20 * KB, [P, 4, 512]), at("oun1", RAW_O, [P, 2, 512])]
    yun = [at("yun0", F_O + 28 * KB, [P, 4, 512]), at("yun1", RAW_O + 4 * KB, [P, 2, 512])]
    mg = at("mg", F_O, [P, NT, D])
    gat = [at(f"gat{s}", F_O + (24 + 4 * s) * KB, [P, 2, 512]) for s in range(2)]
    prd = [at(f"prd{s}", F_O + 32 * KB + s * 2 * KB, [P, 512]) for s in range(2)]
    xres = at("xres", F_O + 24 * KB, [P, D])
    g2 = at("g2", D_O + 40 * KB, [P, D])
    rT = at("rT", D_O + 44 * KB, [P, KC, P])
    rrow = [at(f"rrow{s}", F_O + (28 + 4 * s) * KB, [P, D]) for s in range(2)]
    wrt = at("wrt", F_O + 36 * KB, [P, KC, NG + NE])
    brt = at("brt", F_O + 36 * KB + 1280, [P, NG + NE])
    lg = at("lg", F_O + 36 * KB + 1536, [P, NT, NG + NE])
    sel = at("sel", D_O + 1 * KB, [P, NT, NE])
    A1 = at("A1", D_O + 2 * KB, [P, NT, NE])
    A2 = at("A2", D_O + 3 * KB, [P, NT, NE])
    t1 = at("t1", D_O + 4 * KB, [P, NT, NE])
    t2 = at("t2", D_O + 5 * KB, [P, NT, NE])
    Ab = at("Ab", D_O + 6 * KB, [P, NT, NE])
    nov = at("nov", D_O + 7 * KB, [P, NE])
    run = at("run", D_O + 7 * KB + 128, [P, 2, NE // 2 + NE])
    first = at("first", D_O + 7 * KB + 512, [P, NE])
    last_row = at("last_row", D_O + 7 * KB + 640, [P, NE])
    bt = at("bt", D_O + 8 * KB, [P, (MAXB - 1) * NE])
    sbf = at("sbf", D_O + 9 * KB + 640, [P, 2, 2, NT])
    Bt = at("Bt", D_O + 10 * KB, [P, 2 * NT, NB + 1])
    Rt = at("Rt", D_O + 12 * KB + 512, [P, NT, P])
    XT_O = D_O
    eTh = at("eTh", XT_O, [P, KC, P], F32R)
    eTl = at("eTl", XT_O + 4 * KB, [P, KC, P], F32R)
    hTh = at("hTh", XT_O + 8 * KB, [P, 4, P], F32R)
    hTl = at("hTl", XT_O + 10 * KB, [P, 4, P], F32R)
    sg = at("sg", XT_O + 12 * KB, [P, 512])
    hh = at("hh", XT_O + 14 * KB, [P, 512])
    xg = at("xg", XT_O + 40 * KB, [P, D])
    ystage = at("ystage", XT_O + 44 * KB, [P, D])
    ehi = whi + [at(f"whi{s}", F_O + s % 4 * 8 * KB, [P, PIECE], F32R) for s in (4, 5)]
    elo = wlo + [at(f"wlo{s}", F_O + (2 + s % 4) * 8 * KB, [P, PIECE], F32R) for s in (4, 5)]
    ya = [[at(f"ya{t}{k}", RAW_O + (2 * t + k) * 4 * KB, [P, D]) for k in range(2)] for t in range(NT)]
    gf = at("gf", HL_O, [P, D])
    yo = [at(f"yo{t}", HL_O + (1 + t) * 4 * KB, [P, D]) for t in range(NT)]
    fj = [at(f"fj{s}", HL_O + (7 + s) * 4 * KB, [P, D]) for s in range(2)]

    ps = [ctx.enter_context(nc.psum_tensor(f"ps{i}", [P, 512], F32)) for i in range(8)]

    def C(name):
        a, b = _c[name]
        return cst[:, a:b]
    ident = C("ident")

    z_d = nc.dram_tensor("z_scratch", [T, D_IN], F32, kind="Internal").ap()
    xn_d = nc.dram_tensor("xn_scratch", [T, D], F32, kind="Internal").ap()
    y_d = nc.dram_tensor("y_scratch", [NB * CAP, D], F32, kind="Internal").ap()

    def sem(name):
        return ctx.enter_context(nc.semaphore(name))
    with ctx:
        s_cst = sem("s_cst")
        s_par = sem("s_par")
        s_x = [sem(f"s_xt{t}") for t in range(NT)]
        s_raw = [sem(f"s_raw{s}") for s in range(RAWS)]
        s_hi = sem("s_hi")
        s_lo = sem("s_lo")
        s_lo1 = sem("s_lo1")
        s_pe = sem("s_pe")
        s_sq = sem("s_sq")
        s_dv = sem("s_dv")
        s_rstd1 = sem("s_rstd1")
        s_xs = sem("s_xs")
        s_nT = sem("s_nT")
        s_nth = sem("s_nth")
        s_ntc = sem("s_ntc")
        s_ntl = sem("s_ntl")
        s_zmm = sem("s_zmm")
        s_zev = sem("s_zev")
        s_zst = [sem(f"s_zst{s}") for s in range(4)]
        s_zlq = [sem(f"s_zlq{s}") for s in range(2)]
        s_zlv = [sem(f"s_zlv{s}") for s in range(2)]
        s_decay = sem("s_decay")
        s_lame = sem("s_lame")
        s_warg = sem("s_warg")
        s_wexp = sem("s_wexp")
        s_gsub = sem("s_gsub")
        s_rotv = sem("s_rotv")
        s_rotp = sem("s_rotp")
        s_pl = sem("s_pl")
        s_osq = sem("s_osq")
        s_sg = sem("s_sg")
        s_silu = sem("s_silu")
        s_rstd2 = sem("s_rstd2")
        s_ony = sem("s_ony")
        s_qT = sem("s_qT")
        s_qTc = sem("s_qTc")
        s_sc = sem("s_sc")
        s_sc0 = sem("s_sc0")
        s_mx = sem("s_mx")
        s_ex = sem("s_ex")
        s_a = sem("s_a")
        s_aT = sem("s_aT")
        s_aTc = sem("s_aTc")
        s_o = sem("s_o")
        s_oc = sem("s_oc")
        s_rs = sem("s_rs")
        s_rm = sem("s_rm")
        s_ry = sem("s_ry")
        s_ryc = sem("s_ryc")
        s_on = sem("s_on")
        s_oT = sem("s_oT")
        s_oTh = sem("s_oTh")
        s_oTl = sem("s_oTl")
        s_gl = [sem(f"s_gl{s}") for s in range(2)]
        s_gs = sem("s_gs")
        s_pm = sem("s_pm")
        s_mgd = sem("s_mgd")
        s_mT = sem("s_mT")
        s_mTh = sem("s_mTh")
        s_mTl = sem("s_mTl")
        s_xr = sem("s_xr")
        s_w = sem("s_w")
        s_x2 = sem("s_x2")
        s_rp = sem("s_rp")
        s_sq2 = sem("s_sq2")
        s_rr = sem("s_rr")
        s_rst = [sem(f"s_rst{s}") for s in range(2)]
        s_rTm = sem("s_rTm")
        s_rTc = sem("s_rTc")
        s_lg = sem("s_lg")
        s_rx = sem("s_rx")
        s_re = sem("s_re")
        s_Ab = sem("s_Ab")
        s_rk = sem("s_rk")
        s_bc = sem("s_bc")
        s_br = sem("s_br")
        s_tb = sem("s_tb")
        s_tbm = sem("s_tbm")
        s_ic = sem("s_ic")
        s_nb = sem("s_nb")
        s_h13 = sem("s_h13")
        s_gx = sem("s_gx")
        s_idx = sem("s_idx")
        s_eT = sem("s_eT")
        s_eTh = sem("s_eTh")
        s_eTl = sem("s_eTl")
        s_h1 = sem("s_h1")
        s_sgm = sem("s_sgm")
        s_h = sem("s_h")
        s_hT = sem("s_hT")
        s_hTh = sem("s_hTh")
        s_hTl = sem("s_hTl")
        s_y = sem("s_y")
        s_yc = sem("s_yc")
        s_ys = sem("s_ys")
        s_md = sem("s_md")
        s_zr = sem("s_zr")
        s_g1 = [sem(f"s_g1{t}") for t in range(NT)]
        s_c2 = sem("s_c2")
        s_sq3 = sem("s_sq3")
        s_rstd3 = sem("s_rstd3")
        s_ym = sem("s_ym")
        s_yf = sem("s_yf")
        s_yl = sem("s_yl")
        s_gf = sem("s_gf")
        s_out = sem("s_out")
        block = ctx.enter_context(nc.Block())

        x_tiles = [A["x_prompt"][0, t * P:(t + 1) * P, :] for t in range(4)] + \
                  [A["x_sample"][0, t * P:(t + 1) * P, :] for t in range(2)]
        o_tiles = [A["y_prompt"][0, t * P:(t + 1) * P, :] for t in range(4)] + \
                  [A["y_sample"][0, t * P:(t + 1) * P, :] for t in range(2)]
        w_in = A["w_in"][0].rearrange("(p c) n -> p c n", c=KC)
        w_out = A["w_out"][0].rearrange("(p c) n -> p c n", c=KC)
        w_pab = [A[n][0].rearrange("(h p) n -> p h n", p=P) for n in ("w_pa", "w_pb")]
        e_w = {"w1": A["w1"][0].rearrange("e (p c) f -> e p (c f)", c=KC),
               "w3": A["w3"][0].rearrange("e (p c) f -> e p (c f)", c=KC),
               "w2": A["w2"][0].rearrange("e (p c) n -> e p (c n)", c=4)}

        ZEROS = [(q, e, e + 8) for q in range(1, 4) for e in range(0, NE, 8)] + [(q, NE, NB) for q in range(4)]
        NZ = len(ZEROS)
        O_BANK = ((2, 3, 2, 3), (5, 7, 4, 6))

        def rest_done(eng, e, j):
            if j == 1:
                eng.wait_ge(s_lo1, e + 1)
            else:
                eng.wait_ge(s_lo, 5 * e + (PRE + j + (j == 0)))

        def expert_of(eng, b):
            return eng.value_load(served[0:1, bass.ds(b, 1)], min_val=0, max_val=NE)
        SEQ_T0 = (0, 4)
        SEQ_NT = (4, 2)
        ITS = [(s, h, qt) for s in range(2) for h in range(H) for qt in range(SEQ_NT[s])]

        def rotary(eng, link, v, half, cs, sn, tmp):
            groups = v.shape[1]
            x1, x2_ = v[:, :, 0:half], v[:, :, half:2 * half]
            cb, sb = (a.unsqueeze(1).to_broadcast([P, groups, half]) for a in (cs, sn))
            r = [tmp[:, k, :].rearrange("p (g d) -> p g d", d=half) for k in range(4)]
            eng.tensor_tensor(r[0], x1, cb, ALU.mult)
            eng.tensor_tensor(r[1], x2_, sb, ALU.mult)
            eng.tensor_tensor(r[2], x2_, cb, ALU.mult)
            link(eng.tensor_tensor(r[3], x1, sb, ALU.mult))
            eng.tensor_tensor(x1, r[0], r[1], ALU.subtract)
            link(eng.tensor_tensor(x2_, r[2], r[3], ALU.add))

        @block.sync
        def _(sp):
            for t in range(2):
                sp.dma_start(xin[:, t, :], x_tiles[t]).then_inc(s_x[t], 16)
            sp.dma_start(cst[:, :], A["consts"]).then_inc(s_cst, 16)
            sp.dma_start(gn1[:, :], A["attn_norm_g"][0].rearrange("(p c) -> p c", c=KC)).then_inc(s_par, 16)
            sp.dma_start(gsub[:, :], A["subln_g"][0].rearrange("(p c) -> p c", c=1)).then_inc(s_par, 16)
            sp.dma_start(decay[:, 0:4], A["ret_decay_f"].partition_broadcast(P)[:, 0, :]).then_inc(s_par, 16)
            sp.dma_start(decay[:, 4:8], A["ret_decay_b"].partition_broadcast(P)[:, 0, :]).then_inc(s_par, 16)
            for k, n in enumerate(("lam_q1", "lam_k1", "lam_q2", "lam_k2")):
                sp.dma_start(lamr[:, k, :], A[n].partition_broadcast(P)[:, 0, :]).then_inc(s_par, 16)
            def z_piece(i, j):
                c = bass.ds(i * 1024 + (j // 2) * 512, 512)
                sp.dma_start(raw[j][:, :].rearrange("p (c n) -> p c n", n=512),
                             w_in[:, 4 * (j % 2):4 * (j % 2) + 4, c]).then_inc(s_raw[j], 16)
            z_piece(0, 0)
            for t in range(2, NT):
                sp.dma_start(xin[:, t, :], x_tiles[t]).then_inc(s_x[t], 16)
                if t == 3:
                    z_piece(0, 1)
            z_piece(0, 2)
            z_piece(0, 3)

            def z_pieces(i):
                for j in range(4):
                    sp.wait_ge(s_lo, 4 * i + (j - 3))
                    z_piece(i, j)
            with sp.Fori(1, NCH // 2 - 1) as i:
                z_pieces(i)

            def z_rows(s, dst, c0, n, done):
                t0, nt = SEQ_T0[s], SEQ_NT[s]
                rows = z_d[t0 * P:(t0 + nt) * P, :].rearrange("(t p) n -> p t n", p=P)
                sp.dma_start(dst[s][:, :, :], rows[:, :, c0:c0 + n]).then_inc(done[s], 16)
            for k in range(4):
                sp.wait_ge(s_zst[k], 16 * 6 * NT // 4)
            z_rows(0, zqk, C_Q, 1024, s_zlq)
            z_rows(0, zr, C_R, 512, s_zlq)
            z_pieces(NCH // 2 - 1)
            sp.wait_ge(s_zmm, NCH * NT)
            z_rows(0, zv, C_V, 512, s_zlv)
            z_rows(0, zvr, C_VR, 512, s_zlv)
            z_rows(0, zgr, C_GR, 512, s_zlv)
            sp.wait_ge(s_lo, ZP)
            z_rows(1, zqk, C_Q, 1024, s_zlq)
            z_rows(1, zr, C_R, 512, s_zlq)
            z_rows(1, zv, C_V, 512, s_zlv)
            z_rows(1, zvr, C_VR, 512, s_zlv)
            z_rows(1, zgr, C_GR, 512, s_zlv)

            def p_piece(p):
                slot = (3 + p) % RAWS
                dst = raw[slot][:, :].rearrange("p (c n) -> p c n", n=512)
                if p < 4:
                    src = w_pab[p % 2][:, :, (p // 2) * 512:(p // 2) * 512 + 512]
                else:
                    q = p - 4
                    src = w_out[:, 4 * (q % 2):4 * (q % 2) + 4, (q // 2) * 512:(q // 2) * 512 + 512]
                sp.dma_start(dst, src).then_inc(s_raw[slot], 16)
            def gate_half(k):
                m, t = k // NT, k % NT
                if k >= 2:
                    sp.wait_ge(s_mgd, k - 1)
                rows = z_d[t * P:(t + 1) * P, C_GA:C_GA + 2 * D].rearrange("p (b n) -> p b n", b=2)
                sp.dma_start(gat[k % 2][:, :, :], rows[:, :, m * 512:(m + 1) * 512]).then_inc(s_gl[k % 2], 16)
            p_piece(0)
            for k in range(4):
                sp.wait_ge(s_zst[k], 16 * NCH * NT // 4)
            sp.wait_ge(s_rm, 24)
            p_piece(1)
            p_piece(2)
            sp.wait_ge(s_oTl, 8)
            gate_half(0)
            gate_half(1)
            sp.wait_ge(s_ry, 24)
            sp.wait_ge(s_o, 24)
            sp.wait_ge(s_silu, 2)
            p_piece(4)
            p_piece(5)
            gate_half(2)
            sp.wait_ge(s_oT, 16)
            p_piece(3)
            for k in range(3, 2 * NT):
                gate_half(k)
                if k in (4, 6):
                    p = 4 + k // 2
                    sp.wait_ge(s_lo, ZP + p - 5)
                    p_piece(p)
            sp.wait_ge(s_mgd, 2 * NT)
            sp.wait_ge(s_ys, 16 * NZ)
            sp.dma_start(g2[:, :], A["ffn_norm_g"].partition_broadcast(P)[:, 0, :]).then_inc(s_rp, 16)
            sp.dma_start(wrt[:, :, 0:NG], A["w_rg"][0].rearrange("(p c) g -> p c g", c=KC)).then_inc(s_rp, 16)
            for g in range(NG):
                sp.dma_start(wrt[:, :, NG + g * EPG:NG + (g + 1) * EPG],
                             A["w_re"][0, g].rearrange("(p c) e -> p c e", c=KC)).then_inc(s_rp, 16)
            sp.dma_start(brt[:, 0:NG], A["b_rg"].partition_broadcast(P)[:, 0, :]).then_inc(s_rp, 16)
            sp.dma_start(brt[:, NG:NG + NE],
                         A["b_re"].rearrange("a g e -> a (g e)").partition_broadcast(P)[:, 0, :]).then_inc(s_rp, 16)
            for t in range(NT):
                if t == 0:
                    sp.wait_ge(s_mgd, 2 * NT)
                else:
                    sp.wait_ge(s_x2, 2 * t)
                sp.dma_start(xres[:, :], x_tiles[t]).then_inc(s_xr, 16)
            def e_pieces(e):
                for j in range(6):
                    if not isinstance(e, int):
                        rest_done(sp, e - 1, j)
                    src = e_w[("w1", "w3", "w2")[j // 2]][bass.ds(e, 1), :, (j % 2) * PIECE:(j % 2 + 1) * PIECE]
                    sp.dma_start(raw[j][:, :], src[0]).then_inc(s_raw[j], 16)
            sp.wait_ge(s_lo, PRE)
            e_pieces(0)
            with sp.Fori(1, NE) as e:
                e_pieces(e)
            sp.wait_ge(s_md, 1)
            sp.dma_start(gf[:, :], A["final_norm_g"].rearrange("(a n) -> a n", a=1).partition_broadcast(P)[:, 0, :]).then_inc(s_gf, 16)
            for t in (0, 1, 3, 4, 2, 5):
                if t < 3:
                    sp.wait_ge(s_yf, t + 1)
                else:
                    sp.wait_ge(s_yl, t - 2)
                sp.dma_start(o_tiles[t], yo[t][:, :]).then_inc(s_out, 16)
            sp.wait_ge(s_out, 16 * NT)

        @block.tensor
        def _(pe):
            def split_mm(out, ah, al, bh, bl, first, last):
                pe.matmul(out, ah, bh, start=first, stop=False)
                pe.matmul(out, ah, bl, start=False, stop=False)
                return pe.matmul(out, al, bh, start=False, stop=last)

            def input_columns(t):
                pe.wait_ge(s_xs, t + 1)
                for j in range(2):
                    n = 2 * t + j
                    if n >= 4:
                        pe.wait_ge(s_ntc, n - 3)
                    for c in range(4):
                        mm = pe.transpose(ps[4 + n % 4][:, c * P:(c + 1) * P],
                                          xin[:, t, 4 * j + c::KC], ident)
                    mm.then_inc(s_nT, 1)

            pe.wait_ge(s_cst, 16)
            input_columns(0)
            input_columns(1)
            def z_chunk(i, m):
                for t in range(NT):
                    if isinstance(i, int) and m == 0:
                        pe.wait_ge(s_nth, 2 * t + 2)
                        pe.wait_ge(s_ntl, 2 * t + 2)
                    bank = ps[(6 * m + t) % 4]
                    n = 12 * i + 6 * m + t
                    if not (isinstance(i, int) and i == 0 and 6 * m + t < 4):
                        pe.wait_ge(s_zev, n - 3)
                    for j in range(2):
                        s = 2 * m + j
                        if t == 0:
                            pe.wait_ge(s_lo, 4 * i + (s + 1))
                        for k in range(4):
                            c = 4 * j + k
                            mm = split_mm(bank[:, :], xTh[:, c, t * P:(t + 1) * P], xTl[:, c, t * P:(t + 1) * P],
                                          whi[s][:, k * 512:(k + 1) * 512], wlo[s][:, k * 512:(k + 1) * 512],
                                          c == 0, c == KC - 1)
                        if t == NT - 1 and j == 0:
                            mm.then_inc(s_pe, 1)
                        if isinstance(i, int) and m == 0 and (t, j) in ((1, 0), (2, 0), (3, 0), (3, 1)):
                            input_columns(t + 1 + j)
                    mm.then_inc(s_zmm, 1)

            z_chunk(0, 0)
            z_chunk(0, 1)
            with pe.Fori(1, NCH // 2) as i:
                z_chunk(i, 0)
                z_chunk(i, 1)

            def to_columns(s):
                for g in range(12):
                    G = 12 * s + g
                    if g == 0:
                        pe.wait_ge((s_rotv, s_rotp)[s], 1)
                    if g >= 2:
                        pe.wait_ge(s_qTc, G - 1)
                    for t in range(SEQ_NT[s]):
                        src = zqk[s][:, t, g * P:(g + 1) * P] if g < 8 else zr[s][:, t, (g - 8) * P:(g - 7) * P]
                        mm = pe.transpose(ps[4 + 2 * (g % 2)][:, t * P:(t + 1) * P], src, ident)
                    mm.then_inc(s_qT, 1)

            def outputs_to_columns(s, b, h):
                O = 8 * s + 4 * b + h
                pe.wait_ge((s_on, s_ony)[b], 4 * s + h + 1)
                if O == 0:
                    pe.wait_ge(s_ex, 16)
                elif O == 8:
                    pe.wait_ge(s_oc, 24)
                    pe.wait_ge(s_ryc, 8)
                    pe.wait_ge(s_aTc, 24)
                    pe.wait_ge(s_rm, 24)
                elif s == 0 and O >= 2:
                    pe.wait_ge(s_oTl, O - 1)
                elif O >= 12:
                    pe.wait_ge(s_oTl, O - 3)
                for t in range(SEQ_NT[s]):
                    mm = pe.transpose(ps[O_BANK[s][h]][:, t * P:(t + 1) * P],
                                      (oun, yun)[b][s][:, t, h * VD:(h + 1) * VD], ident)
                mm.then_inc(s_oT, 1)

            def attend(s, i0):
                nt = SEQ_NT[s]
                S = nt * P
                i1 = i0 + H * nt

                def scores(n):
                    _, h, qt = ITS[n]
                    if n >= 2:
                        pe.wait_ge(s_ex, n - 1)
                    for c in range(2):
                        rows = slice(c * HD, (c + 1) * HD)
                        out = ps[2 * (n % 2) + c][:, 0:S] if s == 0 else ps[n % 2][:, c * S:(c + 1) * S]
                        mm = pe.matmul(out, qkT[rows, 0, h, qt * P:(qt + 1) * P],
                                       qkT[rows, 1, h, 0:S], start=True, stop=True)
                        if s == 1 and c == 0:
                            mm.then_inc(s_sc0, 1)
                            pe.wait_ge(s_sc0, n - i0 + 1)
                    mm.then_inc(s_sc, 1)

                def ret_scores(n):
                    _, h, kt = ITS[n]
                    rows = slice((h % 2) * HD, (h % 2 + 1) * HD)
                    if n >= 1:
                        pe.wait_ge(s_rm, n)
                    pe.matmul(ps[6][:, 0:S], rqkT[rows, 1, h // 2, kt * P:(kt + 1) * P],
                              rqkT[rows, 0, h // 2, 0:S], start=True, stop=True).then_inc(s_rs, 1)

                def values(n):
                    _, h, qt = ITS[n]
                    pe.wait_ge(s_aTc, n + 1)
                    if n >= 1:
                        pe.wait_ge(s_oc, n)
                    for kt in range(nt):
                        mm = pe.matmul(ps[5][:, (n % 4) * VD:(n % 4 + 1) * VD],
                                       attT[n % 2][:, kt * P:(kt + 1) * P],
                                       zv[s][:, kt, h * VD:(h + 1) * VD], start=(kt == 0), stop=(kt == nt - 1))
                    mm.then_inc(s_o, 1)

                def ret_values(n):
                    _, h, kt = ITS[n]
                    pe.wait_ge(s_rm, n + 1)
                    if kt == 0 and 4 * s + h >= 1:
                        pe.wait_ge(s_ryc, 4 * s + h)
                    for qt in range(nt):
                        mm = pe.matmul(ps[7][:, qt * VD:(qt + 1) * VD], smk[n % 2][:, qt * P:(qt + 1) * P],
                                       zvr[s][:, kt, h * VD:(h + 1) * VD], start=(kt == 0 and qt == 0),
                                       stop=(kt == nt - 1 and qt == nt - 1), skip_group_check=True)
                    mm.then_inc(s_ry, 1)

                pe.wait_ge(s_qTc, 12 * (s + 1))
                if s == 0:
                    pe.wait_ge(s_zev, NCH * NT)
                scores(i0)
                for n in range(i0, i1):
                    if n + 1 < i1:
                        scores(n + 1)
                    ret_scores(n)
                    if n == i0:
                        pe.wait_ge(s_zlv[s], 16 * 3)
                    if n > i0:
                        values(n - 1)
                        ret_values(n - 1)
                        if s == 1:
                            outputs_to_columns(0, (n - i0 - 1) // H, (n - i0 - 1) % H)
                    pe.wait_ge(s_a, n + 1)
                    if n >= 1:
                        pe.wait_ge(s_aTc, n)
                    for kt in range(nt):
                        mm = pe.transpose(ps[4][:, kt * P:(kt + 1) * P], att[n % 2][:, kt * P:(kt + 1) * P], ident)
                    mm.then_inc(s_aT, 1)
                values(i1 - 1)
                ret_values(i1 - 1)

            to_columns(0)
            attend(0, 0)
            pe.wait_ge(s_aTc, 16)
            pe.wait_ge(s_rm, 16)
            to_columns(1)
            attend(1, 16)
            outputs_to_columns(0, 1, H - 1)

            pe.wait_ge(s_oTh, 8)
            pe.wait_ge(s_oTl, 8)
            for n in range(4 * NT):
                t, m = n % (2 * NT) // 2, n // (2 * NT) * 2 + n % 2
                if n in (2, 4):
                    for h in range(H):
                        outputs_to_columns(1, n // 2 - 1, h)
                if n == 8:
                    pe.wait_ge(s_oTh, 16)
                    pe.wait_ge(s_oTl, 16)
                if n >= 4:
                    pe.wait_ge(s_pm, n - 3)
                if t == 0:
                    pe.wait_ge(s_lo, ZP + m + 1)
                for h in range(H):
                    mm = split_mm(ps[n % 4][:, :], oTh[m % 2][:, h, t * P:(t + 1) * P],
                                  oTl[m % 2][:, h, t * P:(t + 1) * P], whi[P_HI[m]][:, h * 512:(h + 1) * 512],
                                  wlo[P_LO[m]][:, h * 512:(h + 1) * 512], h == 0, h == H - 1)
                mm.then_inc(s_gs, 1)
            def merged_to_columns(t):
                pe.wait_ge(s_mgd, NT + t + 1)
                for j in range(2):
                    n = 2 * t + j
                    if n >= 2:
                        pe.wait_ge(s_mTl, n - 1)
                    for c in range(4):
                        mm = pe.transpose(ps[4 + n % 2][:, c * P:(c + 1) * P], mg[:, t, 4 * j + c::KC], ident)
                    mm.then_inc(s_mT, 1)

            def route_columns(t):
                pe.wait_ge(s_rr, t + 1)
                if t >= 1:
                    pe.wait_ge(s_rTc, 2 * t)
                for j in range(2):
                    for c in range(4):
                        mm = pe.transpose(ps[j][:, c * P:(c + 1) * P], rrow[t % 2][:, 4 * j + c::KC], ident)
                    mm.then_inc(s_rTm, 1)

            def logits(t):
                pe.wait_ge(s_rTc, 2 * t + 2)
                if t == 0:
                    pe.wait_ge(s_rp, 16 * 8)
                if t >= 1:
                    pe.wait_ge(s_rx, t)
                for c in range(KC):
                    mm = pe.matmul(ps[2][:, 0:NG + NE], rT[:, c, :], wrt[:, c, :],
                                   start=(c == 0), stop=(c == KC - 1))
                mm.then_inc(s_lg, 1)
            merged_to_columns(0)
            for t in range(NT):
                if t + 1 < NT:
                    merged_to_columns(t + 1)
                pe.wait_ge(s_mTl, 2 * t + 2)
                for n in range(2):
                    if t >= 1:
                        pe.wait_ge(s_x2, 2 * t + n - 1)
                    for j in range(2):
                        p = 2 * n + j
                        if t == 0:
                            pe.wait_ge(s_lo, ZP + 4 + p + 1)
                        for k in range(4):
                            c = 4 * j + k
                            mm = split_mm(ps[6 + n][:, :], mTh[t % 2][:, c, :], mTl[t % 2][:, c, :],
                                          whi[P_HI[p]][:, k * 512:(k + 1) * 512],
                                          wlo[P_LO[p]][:, k * 512:(k + 1) * 512],
                                          c == 0, c == KC - 1)
                        if t == NT - 1 and j == 0:
                            mm.then_inc(s_pe, 1)
                    mm.then_inc(s_w, 1)
                    if t >= 1 and n == 0:
                        route_columns(t - 1)
                if t >= 1:
                    logits(t - 1)
            route_columns(NT - 1)
            logits(NT - 1)
            pe.wait_ge(s_Ab, 1)
            picked = Ab[:, :, :].rearrange("p t e -> p (t e)")
            pe.matmul(ps[3][:, 0:NT * NE], C("tri"), picked, start=True, stop=False, skip_group_check=True)
            for u in range(1, NT + 1):
                mm = pe.matmul(ps[3][:, u * NE:(NT + 1) * NE], C("ones"), picked[:, 0:(NT + 1 - u) * NE],
                               start=False, stop=(u == NT), skip_group_check=True)
            mm.then_inc(s_rk, 1)
            pe.wait_ge(s_bc, 1)
            for k in range(2):
                mm = pe.matmul(ps[5][0:1, k * P:(k + 1) * P], bcol[:, k:k + 1], ident,
                               start=True, stop=True, skip_group_check=True)
            mm.then_inc(s_br, 1)
            for q in range(2 * NT):
                pe.wait_ge(s_tb, q + 1)
                pe.matmul(ps[4][:, 0:NB + 1], Rt[:, q % NT, :], Bt[:, q, :],
                          start=(q == 0), stop=(q == 2 * NT - 1)).then_inc(s_tbm, 1)

            pe.wait_ge(s_nb, 1)
            nb = pe.value_load(nbi[0:1, 0:1], min_val=NE, max_val=NB)

            def x_to_columns(b, j):
                pe.wait_ge(s_gx, 16 * b + 16)
                for c in range(4):
                    mm = pe.transpose(ps[2 + j][:, c * P:(c + 1) * P], xg[:, 4 * j + c::KC], ident)
                mm.then_inc(s_eT, 1)

            def e_block(b, last):
                e = expert_of(pe, b)
                pe.wait_ge(s_eTl, 2 * b + 2)
                for m in range(2):
                    for j in range(2):
                        q = 2 * m + j
                        rest_done(pe, e, q)
                        for k in range(4):
                            c = 4 * j + k
                            mm = split_mm(ps[m][:, :], eTh[:, c, :], eTl[:, c, :],
                                          ehi[q][:, k * 512:(k + 1) * 512], elo[q][:, k * 512:(k + 1) * 512],
                                          c == 0, c == KC - 1)
                        if j == 0:
                            mm.then_inc(s_pe, 1)
                    mm.then_inc(s_h1, 1)
                if not last:
                    x_to_columns(b + 1, 0)
                pe.wait_ge(s_h, b + 2)
                for c in range(4):
                    mm = pe.transpose(ps[4][:, c * P:(c + 1) * P], hh[:, c::4], ident)
                mm.then_inc(s_hT, 1)
                if not last:
                    x_to_columns(b + 1, 1)
                pe.wait_ge(s_hTh, b + 1)
                pe.wait_ge(s_yc, 2 * b + 2)
                for j in range(2):
                    q = 4 + j
                    rest_done(pe, e, q)
                    parts = [(k, n, slice(k * D + n * 512, k * D + n * 512 + 512)) for k in range(2) for n in range(2)]
                    for k, n, w in parts:
                        c = 2 * j + k
                        pe.matmul(ps[6 + n][:, :], hTh[:, c, :], ehi[q][:, w], start=(c == 0), stop=False)
                        pe.matmul(ps[6 + n][:, :], hTh[:, c, :], elo[q][:, w], start=False, stop=False)
                    if j == 0:
                        pe.wait_ge(s_hTl, b + 1)
                    for k, n, w in parts:
                        c = 2 * j + k
                        mm = pe.matmul(ps[6 + n][:, :], hTl[:, c, :], ehi[q][:, w], start=False, stop=(c == 3))
                    if j == 0:
                        mm.then_inc(s_pe, 1)
                mm.then_inc(s_y, 1)

            x_to_columns(0, 0)
            x_to_columns(0, 1)
            pe.sem_inc(s_h1, 2)
            pe.sem_inc(s_hT, 1)
            pe.sem_inc(s_y, 1)
            with pe.Fori(0, nb - 1) as b:
                e_block(b, last=False)
            e_block(nb - 1, last=True)

        @block.scalar
        def _(act):
            def hi_piece(slot_raw, use, slot, freed=None):
                act.wait_ge(s_raw[slot_raw], 16 * use)
                if freed is not None:
                    act.wait_ge(*freed)
                act.activation(ehi[slot][:, :], raw[slot_raw][:, :], ACT.Copy).then_inc(s_hi, 1)

            act.wait_ge(s_lame, 1)
            act.activation(lamv[:, 2:4], lamv[:, 0:2], ACT.Exp).then_inc(s_lame, 1)
            act.activation(decay[:, :], decay[:, :], ACT.Exp).then_inc(s_decay, 1)

            def square_row(t):
                act.wait_ge(s_x[t], 16)
                if t:
                    act.wait_ge(s_sq, t - 1)
                act.activation(sqx[0][:, :], xin[:, t, :], ACT.Square, accum_out=ssq[:, t:t + 1]).then_inc(s_sq, 1)

            def scale_row(t):
                act.mul(xin[:, t, :], xin[:, t, :], rstd[:, t:t + 1]).then_inc(s_xs, 1)

            def input_hi(t):
                for n in (2 * t, 2 * t + 1):
                    act.wait_ge(s_ntc, n + 1)
                    act.activation(xTh[:, 4 * (n % 2):4 * (n % 2) + 4, t * P:(t + 1) * P],
                                   junk[:, (n % 2) * 512:(n % 2 + 1) * 512].rearrange("p (c k) -> p c k", k=P),
                                   ACT.Copy).then_inc(s_nth, 1)
            square_row(0)
            act.wait_ge(s_rstd1, 1)
            scale_row(0)
            scale_row(1)
            hi_piece(0, 1, 0)
            square_row(2)
            square_row(3)
            input_hi(0)
            hi_piece(1, 1, 1)
            square_row(4)
            square_row(5)
            input_hi(1)
            act.wait_ge(s_rstd1, 2)
            scale_row(2)
            scale_row(3)
            input_hi(2)
            scale_row(4)
            input_hi(3)
            scale_row(5)
            input_hi(4)
            input_hi(5)

            def z_out(i, m, t):
                n = 12 * i + 6 * m + t
                k = (6 * m + t) % 4
                act.wait_ge(s_zmm, n + 1)
                if not (isinstance(i, int) and i == 0 and 6 * m + t < 4):
                    act.wait_ge(s_zst[k], 48 * i + 16 * ((6 * m + t) // 4))
                act.activation(zst[k][:, :], ps[k][:, :], ACT.Copy).then_inc(s_zev, 1)

            def z_step(i, last=False):
                first = isinstance(i, int) and i == 0
                for m in range(2):
                    for t in range(NT):
                        z_out(i, m, t)
                        if t in (0, 2):
                            j = t // 2
                            if m == 0:
                                hi_piece(2 + j, i + 1, 2 + j,
                                         None if first else (s_zmm, 12 * i) if j else (s_pe, 2 * i))
                            elif not last:
                                hi_piece(j, i + 2, j, (s_zmm, 12 * i + 6) if j else (s_pe, 2 * i + 1))
            z_step(0)
            with act.Fori(1, NCH // 2 - 1) as i:
                z_step(i)
            act.wait_ge(s_warg, 1)
            act.activation(wdec[:, :, :], wdec[:, :, :], ACT.Exp).then_inc(s_wexp, 1)
            z_step(NCH // 2 - 1, last=True)
            act.wait_ge(s_gsub, 1)

            def columns_out(s):
                S = SEQ_NT[s] * P
                for g in range(12):
                    act.wait_ge(s_qT, 12 * s + g + 1)
                    if s == 0 and g == 0:
                        act.wait_ge(s_zmm, NCH * NT)
                    dst = qkT[:, g // 4, g % 4, 0:S] if g < 8 else rqkT[:, (g - 8) // 2, g % 2, 0:S]
                    act.activation(dst, ps[4 + 2 * (g % 2)][:, 0:S], ACT.Copy).then_inc(s_qTc, 1)

            n_sq = [0]

            def square(src, col):
                q = n_sq[0]
                n_sq[0] += 1
                if q >= 4:
                    act.wait_ge(s_osq, q - 3)
                act.activation(sqj[:, q % 4, :], src, ACT.Square, accum_out=ssq[:, col:col + 1]).then_inc(s_osq, 1)

            def attend(s, i0):
                nt = SEQ_NT[s]
                S = nt * P
                i1 = i0 + H * nt

                def exps(n):
                    act.wait_ge(s_mx, n + 1)
                    if n >= 2:
                        act.wait_ge(s_a, n - 1)
                    for c in range(2):
                        src = ps[2 * (n % 2) + c][:, 0:S] if s == 0 else ps[n % 2][:, c * S:(c + 1) * S]
                        e = act.activation(prob[n % 2][:, c, 0:S], src, ACT.Exp,
                                           bias=nm[:, n % 2, c:c + 1], scale=HD ** -0.5,
                                           accum_out=sume[:, n % 2, c:c + 1])
                    e.then_inc(s_ex, 1)

                def squares(n):
                    _, h, qt = ITS[n]
                    act.wait_ge(s_oc, n + 1)
                    square(oun[s][:, qt, h * VD:(h + 1) * VD], 4 * qt + h)
                    if qt == nt - 1:
                        act.wait_ge(s_ryc, 4 * s + h + 1)
                        for t in range(nt):
                            square(yun[s][:, t, h * VD:(h + 1) * VD], 4 * nt + 4 * t + h)
                exps(i0)
                for n in range(i0, i1):
                    if n + 1 < i1:
                        exps(n + 1)
                    if n == 2:
                        for q in range(2):
                            act.wait_ge(s_zlv[q], 16 * 3)
                            act.activation(silu[q][:, :, :], zgr[q][:, :, :], ACT.Sigmoid).then_inc(s_sg, 1)
                    if s == 1 and n < i0 + H:
                        normalise(0, n - i0)
                    if n >= i0 + 2:
                        squares(n - 2)
                    act.wait_ge(s_aT, n + 1)
                    if n >= 2:
                        act.wait_ge(s_o, n - 1)
                    act.activation(attT[n % 2][:, 0:S], ps[4][:, 0:S], ACT.Copy).then_inc(s_aTc, 1)
                    if s == 1 and n > i0:
                        columns_hi(0, n - i0 - 1)
                    if s == 1 and n == i0 + 4:
                        act.wait_ge(s_o, 16)
                        act.wait_ge(s_ry, 16)
                        hi_piece(3, 6, P_HI[0])
                squares(i1 - 2)
                squares(i1 - 1)

            def normalise(s, h):
                if h == 0:
                    act.wait_ge(s_rstd2, s + 1)
                nt = SEQ_NT[s]
                for t in range(nt):
                    v = oun[s][:, t, h * VD:(h + 1) * VD]
                    o = act.mul(v, v, rstd[:, 4 * t + h:4 * t + h + 1])
                o.then_inc(s_on, 1)

            def columns_hi(s, q):
                b, h = q // H, q % H
                act.wait_ge(s_oT, 8 * s + q + 1)
                cols = slice(SEQ_T0[s] * P, (SEQ_T0[s] + SEQ_NT[s]) * P)
                act.activation(oTh[b][:, h, cols], ps[O_BANK[s][h]][:, 0:SEQ_NT[s] * P], ACT.Copy,
                               scale=gsub[:, 0:1] if b == 0 else 1.0).then_inc(s_oTh, 1)

            columns_out(0)
            attend(0, 0)
            columns_out(1)
            attend(1, 16)
            columns_hi(0, 7)

            def gate(k):
                act.wait_ge(s_gl[k % 2], 16 * (k // 2 + 1))
                act.activation(gat[k % 2][:, :, :], gat[k % 2][:, :, :], ACT.Sigmoid).then_inc(s_sgm, 1)

            def merge_hi(p):
                hi_piece((3 + p) % RAWS, (6, 1, 1, 6, 6, 6, 7, 2)[p], P_HI[p % 4],
                         (s_gs, (p // 2 - 1) * 2 * NT - (p + 1) % 2) if p >= 4 else None)
            act.wait_ge(s_o, 24)
            act.wait_ge(s_ry, 24)
            merge_hi(1)
            for h in range(H):
                normalise(1, h)
            gate(0)
            gate(1)
            for q in range(2 * H):
                columns_hi(1, q)
            merge_hi(2)
            gate(2)
            gate(3)
            merge_hi(3)
            for k in range(4, 2 * NT):
                gate(k)
                if k == NT + 1:
                    merge_hi(4)
                    merge_hi(5)
            def e_hi0(j):
                hi_piece(j, (7, 7, 7, 8, 3, 2)[j], j)

            def merged_hi(t):
                for j in range(2):
                    n = 2 * t + j
                    act.wait_ge(s_mT, n + 1)
                    if t >= 2:
                        act.wait_ge(s_w, 2 * (t - 1))
                    act.activation(mTh[t % 2][:, 4 * j:4 * j + 4, :].rearrange("p c k -> p (c k)"),
                                   ps[4 + n % 2][:, :], ACT.Copy).then_inc(s_mTh, 1)

            def route_copy(t):
                for j in range(2):
                    act.wait_ge(s_rTm, 2 * t + j + 1)
                    if t >= 1:
                        act.wait_ge(s_lg, t)
                    act.activation(rT[:, 4 * j:4 * j + 4, :].rearrange("p c k -> p (c k)"),
                                   ps[j][:, :], ACT.Copy).then_inc(s_rTc, 1)
            merged_hi(0)
            merge_hi(6)
            merge_hi(7)
            for t in range(NT):
                if t + 1 < NT:
                    merged_hi(t + 1)
                if t >= 1:
                    route_copy(t - 1)
                act.wait_ge(s_x2, 2 * t + 2)
                if t >= 2:
                    act.wait_ge(s_rst[t % 2], 16 * (t // 2))
                    act.wait_ge(s_rTm, 2 * (t - 1))
                act.activation(rrow[t % 2][:, :], x2[:, t, :], ACT.Square, accum_out=ssq[:, t:t + 1]).then_inc(s_sq2, 1)
            route_copy(NT - 1)
            for j in range(6):
                e_hi0(j)
            act.wait_ge(s_re, 1)
            act.activation(gq[:, 1, :, :], gq[:, 0, :, :], ACT.Exp).then_inc(s_re, 1)
            act.activation(v6[:, 3, :], v6[:, 2, :], ACT.Exp).then_inc(s_re, 1)

            act.wait_ge(s_nb, 1)
            nb = act.value_load(nbi[0:1, 0:1], min_val=NE, max_val=NB)

            def x_hi(n, j):
                act.wait_ge(s_eT, n * 2 + (j + 1))
                act.activation(eTh[:, 4 * j:4 * j + 4, :].rearrange("p c k -> p (c k)"), ps[2 + j][:, :],
                               ACT.Copy).then_inc(s_eTh, 1)

            def e_hi(b, e, j):
                freed = ((s_pe, 3 * b + NCH), (s_h1, 2 * b + 1), (s_pe, 3 * b + (NCH + 1)),
                         (s_h1, 2 * b + 2), (s_pe, 3 * b + (NCH + 2)), (s_y, b + 1))[j]
                hi_piece(j, e + (7, 7, 7, 8, 3, 2)[j], j, freed)

            def e_block(b, last):
                act.activation(sdum[:, :], cst[:, 0:1], ACT.Sigmoid)
                if not last:
                    e, e1 = expert_of(act, b), expert_of(act, b + 1)

                def next_pieces(js):
                    if not last:
                        with act.If(e1 > e):
                            for j in js:
                                e_hi(b + 1, e1, j)
                next_pieces((0,))
                act.wait_ge(s_h1, 2 * b + 3)
                act.wait_ge(s_h, b + 1)
                act.activation(sg[:, :], ps[0][:, :], ACT.Sigmoid).then_inc(s_sgm, 1)
                next_pieces((1,))
                act.wait_ge(s_hT, b + 2)
                act.wait_ge(s_y, b + 1)
                act.activation(hTh[:, :, :].rearrange("p c k -> p (c k)"), ps[4][:, :], ACT.Copy).then_inc(s_hTh, 1)
                if not last:
                    x_hi(b + 1, 0)
                    x_hi(b + 1, 1)
                next_pieces((2, 3, 4))
                act.wait_ge(s_y, b + 2)
                act.wait_ge(s_ys, 16 * b + 16 * NZ)
                for n in range(2):
                    act.activation(ystage[:, n * 512:(n + 1) * 512], ps[6 + n][:, :], ACT.Copy).then_inc(s_yc, 1)
                next_pieces((5,))

            x_hi(0, 0)
            x_hi(0, 1)
            act.sem_inc(s_yc, 2)
            with act.Fori(0, nb - 1) as b:
                e_block(b, last=False)
            e_block(nb - 1, last=True)
            for t in range(NT):
                act.wait_ge(s_c2, t + 1)
                if t >= 2:
                    act.wait_ge(s_sq3, t - 1)
                act.activation(fj[t % 2][:, :], x2[:, t, :], ACT.Square, accum_out=ssq[:, t:t + 1]).then_inc(s_sq3, 1)
                for u in {3: (0, 1), NT - 1: (2,)}.get(t, ()):
                    act.wait_ge(s_rstd3, 1 + u // 2)
                    act.mul(yo[u][:, :], x2[:, u, :], rstd[:, u:u + 1]).then_inc(s_ym, 1)

        @block.vector
        def _(dve):
            n_link = [0]

            def link(ins):
                n_link[0] += 1
                ins.then_inc(s_dv, 1)
                dve.wait_ge(s_dv, n_link[0])

            def lo_piece(slot_raw, slot, q, slot_hi=None):
                dve.wait_ge(s_hi, q)
                hi = ehi[slot if slot_hi is None else slot_hi]
                dve.tensor_tensor(elo[slot][:, :], raw[slot_raw][:, :], hi[:, :].bitcast(F32),
                                  ALU.subtract).then_inc(s_lo, 1)

            def rsqrt(c0, c1, n_mean, link):
                v, y, a = ssq[:, c0:c1], rstd[:, c0:c1], rs_a[:, c0:c1]
                link(dve.tensor_scalar(v, v, 1.0 / n_mean, EPS, ALU.mult, ALU.add))
                link(dve.tensor_scalar(a.bitcast(I32), v.bitcast(I32), 1, None, ALU.arith_shift_right))
                link(dve.tensor_scalar(y.bitcast(I32), a.bitcast(I32), -1.0, float(0x5f3759df), ALU.mult, ALU.add))
                for _ in range(3):
                    link(dve.scalar_tensor_tensor(out=a, in0=y, scalar=-0.5, in1=y, op0=ALU.mult, op1=ALU.mult))
                    link(dve.tensor_tensor(a, a, v, ALU.mult))
                    link(dve.scalar_tensor_tensor(out=y, in0=a, scalar=1.5, in1=y, op0=ALU.add, op1=ALU.mult))

            dve.wait_ge(s_par, 16 * 8)
            for k in range(2):
                link(dve.tensor_tensor_reduce(out=lamr[:, 2 * k, :], in0=lamr[:, 2 * k, :], in1=lamr[:, 2 * k + 1, :],
                                              scale=1.0, scalar=0.0, op0=ALU.mult, op1=ALU.add,
                                              accum_out=lamv[:, k:k + 1]))
            dve.sem_inc(s_lame, 1)
            dve.wait_ge(s_lame, 2)
            link(dve.tensor_tensor(lamv[:, 0:1], lamv[:, 3:4], lamv[:, 2:3], ALU.subtract))
            link(dve.tensor_scalar(lamv[:, 0:1], lamv[:, 0:1], -LAM_INIT, None, ALU.add))
            link(dve.tensor_scalar(gsub[:, :], gsub[:, :], 1.0 - LAM_INIT, None, ALU.mult))
            dve.sem_inc(s_gsub, 1)
            dve.wait_ge(s_decay, 1)
            link(dve.tensor_scalar(decay[:, 0:4], decay[:, 0:4], -1.0, None, ALU.mult))
            dve.wait_ge(s_x[1], 16)
            link(dve.tensor_tensor_reduce(out=sqx[1][:, :], in0=xin[:, 1, :], in1=xin[:, 1, :], scale=1.0, scalar=0.0,
                                          op0=ALU.mult, op1=ALU.add, accum_out=ssq[:, 1:2]))
            dve.wait_ge(s_sq, 1)
            rsqrt(0, 2, D, link)
            dve.sem_inc(s_rstd1, 1)

            def half_columns(n):
                return junk[:, n % 2 * 512:(n % 2 + 1) * 512].rearrange("p (c k) -> p c k", k=P)

            def input_gain(n):
                dve.wait_ge(s_nT, n + 1)
                if n >= 2:
                    dve.wait_ge(s_ntl, n - 1)
                    dve.wait_ge(s_nth, n - 1)
                dve.tensor_tensor(half_columns(n), ps[4 + n % 4][:, :].rearrange("p (c k) -> p c k", k=P),
                                  gn1[:, 4 * (n % 2):4 * (n % 2) + 4].unsqueeze(2).to_broadcast([P, 4, P]),
                                  ALU.mult).then_inc(s_ntc, 1)

            def input_columns(t):
                input_gain(2 * t)
                input_gain(2 * t + 1)
                for n in (2 * t, 2 * t + 1):
                    dve.wait_ge(s_nth, n + 1)
                    sl = (slice(None), slice(4 * (n % 2), 4 * (n % 2) + 4), slice(t * P, (t + 1) * P))
                    dve.tensor_tensor(xTl[sl], half_columns(n), xTh[sl].bitcast(F32), ALU.subtract).then_inc(s_ntl, 1)
            lo_piece(0, 0, 1)
            input_columns(0)
            lo_piece(1, 1, 2)
            input_columns(1)
            dve.wait_ge(s_sq, NT - 1)
            rsqrt(2, NT, D, link)
            dve.sem_inc(s_rstd1, 1)
            for t in range(2, NT):
                input_columns(t)
            for j in range(2, 4):
                lo_piece(j, j, j + 1)

            def z_lo(i):
                for j in range(4):
                    lo_piece(j, j, 4 * i + (j + 1))
            for h in range(H):
                link(dve.tensor_scalar(wdec[:, h, :], C("rel"), 0.0, decay[:, h:h + 1], ALU.max, ALU.mult))
                link(dve.tensor_scalar(junk[:, 0:RELW], C("rel"), 0.0, decay[:, 4 + h:5 + h], ALU.min, ALU.mult))
                link(dve.tensor_tensor(wdec[:, h, :], wdec[:, h, :], junk[:, 0:RELW], ALU.add))
            dve.sem_inc(s_warg, 1)
            with dve.Fori(1, NCH // 2 - 1) as i:
                z_lo(i)
            z_lo(NCH // 2 - 1)

            dve.wait_ge(s_zlq[0], 32)
            for t in range(4):
                v = zqk[0][:, t, :].rearrange("p (g d) -> p g d", d=HD)
                rotary(dve, link, v, 8, C("cosA")[:, t * 8:(t + 1) * 8], C("sinA")[:, t * 8:(t + 1) * 8], rt_v)
                for k in range(2):
                    v = zr[0][:, t, k * 256:(k + 1) * 256].rearrange("p (g d) -> p g d", d=HD)
                    rotary(dve, link, v, 32, C("cosR")[:, t * 32:(t + 1) * 32], C("sinR")[:, t * 32:(t + 1) * 32],
                           rt_v)
            dve.sem_inc(s_rotv, 1)

            def attend(s, i0):
                nt = SEQ_NT[s]
                S = nt * P
                i1 = i0 + H * nt

                def maxes(n):
                    b = 2 * (n % 2)
                    dve.wait_ge(s_sc, n + 1)
                    if s == 0:
                        dve.tensor_reduce(mx[:, n % 2, 0:1], ps[b][:, 0:S], AX.X, ALU.max)
                        link(dve.tensor_reduce(mx[:, n % 2, 1:2], ps[b + 1][:, 0:S], AX.X, ALU.max))
                    else:
                        link(dve.tensor_reduce(mx[:, n % 2, :], ps[n % 2][:, 0:2 * S].rearrange("p (c k) -> p c k", c=2),
                                               AX.X, ALU.max))
                    dve.tensor_scalar(nm[:, n % 2, :], mx[:, n % 2, :], -HD ** -0.5, None,
                                      ALU.mult).then_inc(s_mx, 1)

                def weights(n):
                    dve.wait_ge(s_ex, n + 1)
                    if n >= 2:
                        dve.wait_ge(s_aT, n - 1)
                        dve.wait_ge(s_oc, n - 1)
                    link(dve.reciprocal(rc[:, n % 2, :], sume[:, n % 2, :]))
                    link(dve.scalar_tensor_tensor(out=rc[:, n % 2, 1:2], in0=rc[:, n % 2, 1:2], scalar=lamv[:, 0:1],
                                                  in1=sume[:, n % 2, 0:1], op0=ALU.mult, op1=ALU.mult))
                    dve.scalar_tensor_tensor(out=att[n % 2][:, 0:S], in0=prob[n % 2][:, 1, 0:S],
                                             scalar=rc[:, n % 2, 1:2], in1=prob[n % 2][:, 0, 0:S],
                                             op0=ALU.mult, op1=ALU.add).then_inc(s_a, 1)

                def decayed(n):
                    _, h, kt = ITS[n]
                    dve.wait_ge(s_rs, n + 1)
                    if n >= 2:
                        dve.wait_ge(s_ry, n - 1)
                    dve.scalar_tensor_tensor(out=smk[n % 2][:, 0:S], in0=ps[6][:, 0:S], scalar=HD ** -0.5,
                                             in1=wdec[:, h, (3 - kt) * P:(3 - kt) * P + S],
                                             op0=ALU.mult, op1=ALU.mult).then_inc(s_rm, 1)

                def outputs(n):
                    _, h, qt = ITS[n]
                    dve.wait_ge(s_o, n + 1)
                    dve.tensor_scalar(oun[s][:, qt, h * VD:(h + 1) * VD], ps[5][:, (n % 4) * VD:(n % 4 + 1) * VD],
                                      rc[:, n % 2, 0:1], None, ALU.mult).then_inc(s_oc, 1)
                    if qt == nt - 1:
                        dve.wait_ge(s_ry, n + 1)
                        dve.tensor_copy(yun[s][:, 0:nt, h * VD:(h + 1) * VD],
                                        ps[7][:, 0:S].rearrange("p (t v) -> p t v", v=VD)).then_inc(s_ryc, 1)
                maxes(i0)
                if s == 1:
                    norms(0)
                for n in range(i0, i1):
                    if s == 1 and n + 1 < i1:
                        maxes(n + 1)
                    weights(n)
                    if s == 0 and n + 1 < i1:
                        maxes(n + 1)
                    decayed(n)
                    if n > i0:
                        outputs(n - 1)
                    if s == 1:
                        if n < i0 + H:
                            normalise(0, n - i0)
                        if n > i0:
                            columns_lo(0, n - i0 - 1)
                outputs(i1 - 1)

            def norms(s):
                w = 8 * SEQ_NT[s]
                dve.wait_ge(s_osq, w if s == 0 else 32 + w)
                rsqrt(0, w, VD, link)
                dve.sem_inc(s_rstd2, 1)

            def normalise(s, h):
                nt = SEQ_NT[s]
                if h == 0:
                    dve.wait_ge(s_silu, s + 1)
                for t in range(nt):
                    v = yun[s][:, t, h * VD:(h + 1) * VD]
                    col = 4 * nt + 4 * t + h
                    o = dve.scalar_tensor_tensor(out=v, in0=v, scalar=rstd[:, col:col + 1],
                                                 in1=silu[s][:, t, h * VD:(h + 1) * VD],
                                                 op0=ALU.mult, op1=ALU.mult)
                o.then_inc(s_ony, 1)

            def columns_lo(s, q):
                b, h = q // H, q % H
                dve.wait_ge(s_oTh, 8 * s + q + 1)
                cols = slice(SEQ_T0[s] * P, (SEQ_T0[s] + SEQ_NT[s]) * P)
                dve.scalar_tensor_tensor(out=oTl[b][:, h, cols], in0=ps[O_BANK[s][h]][:, 0:SEQ_NT[s] * P],
                                         scalar=gsub[:, 0:1] if b == 0 else 1.0,
                                         in1=oTh[b][:, h, cols].bitcast(F32),
                                         op0=ALU.mult, op1=ALU.subtract).then_inc(s_oTl, 1)

            def merge_lo(p):
                lo_piece((3 + p) % RAWS, P_LO[p % 4], ZP + p + 1, P_HI[p % 4])

            dve.wait_ge(s_wexp, 1)
            for k in range(4):
                dve.wait_ge(s_zst[k], 16 * NCH * NT // 4)
            attend(0, 0)
            attend(1, 16)
            columns_lo(0, 7)
            dve.wait_ge(s_ony, H)
            dve.wait_ge(s_on, H)
            norms(1)
            dve.wait_ge(s_lo, ZP + 1)
            merge_lo(1)
            for h in range(H):
                normalise(1, h)
            for n in range(4 * NT):
                k, b = n // 2, n % 2
                g = gat[k % 2][:, b, :]
                dst = mg[:, k % NT, k // NT * 512:k // NT * 512 + 512]
                if b == 0:
                    dve.wait_ge(s_sgm, k + 1)
                dve.wait_ge(s_gs, n + 1)
                if b == 0:
                    dve.tensor_tensor(dst, ps[n % 4][:, :], g, ALU.mult).then_inc(s_pm, 1)
                else:
                    if k >= 2:
                        dve.wait_ge(s_mgd, k - 1)
                    dve.tensor_tensor(prd[k % 2][:, :], ps[n % 4][:, :], g, ALU.mult).then_inc(s_pm, 1)
                    dve.wait_ge(s_pm, n + 1)
                    dve.tensor_tensor(dst, dst, prd[k % 2][:, :], ALU.add).then_inc(s_mgd, 1)
                if n in (1, 3):
                    for h in range(H):
                        columns_lo(1, n // 2 * H + h)
                if n == 3:
                    merge_lo(2)
                if n == 5:
                    merge_lo(3)
                if n == 2 * NT + 5:
                    merge_lo(4)
                    merge_lo(5)
            def merged_lo(t):
                for j in range(2):
                    n = 2 * t + j
                    dve.wait_ge(s_mTh, n + 1)
                    dve.tensor_tensor(mTl[t % 2][:, 4 * j:4 * j + 4, :].rearrange("p c k -> p (c k)"),
                                      ps[4 + n % 2][:, :],
                                      mTh[t % 2][:, 4 * j:4 * j + 4, :].rearrange("p c k -> p (c k)").bitcast(F32),
                                      ALU.subtract).then_inc(s_mTl, 1)
            def route_logits(t):
                dve.wait_ge(s_lg, t + 1)
                dve.tensor_tensor(lg[:, t, :], ps[2][:, 0:NG + NE], brt[:, :], ALU.add).then_inc(s_rx, 1)
            merged_lo(0)
            merge_lo(6)
            merge_lo(7)
            for t in range(NT):
                if t + 1 < NT:
                    merged_lo(t + 1)
                dve.wait_ge(s_xr, 16 * (t + 1))
                for n in range(2):
                    dve.wait_ge(s_w, 2 * t + n + 1)
                    dve.tensor_tensor(x2[:, t, n * 512:(n + 1) * 512], ps[6 + n][:, :],
                                      xres[:, n * 512:(n + 1) * 512], ALU.add).then_inc(s_x2, 1)
                dve.wait_ge(s_sq2, t + 1)
                rsqrt(t, t + 1, D, link)
                if t == 0:
                    dve.wait_ge(s_rp, 16 * 8)
                dve.scalar_tensor_tensor(out=rrow[t % 2][:, :], in0=x2[:, t, :], scalar=rstd[:, t:t + 1],
                                         in1=g2[:, :], op0=ALU.mult, op1=ALU.mult).then_inc(s_rr, 1)
                if t >= 1:
                    route_logits(t - 1)

            def choose(a, b):
                nt = b - a

                def b4(v):
                    return v.unsqueeze(2).to_broadcast([P, nt, NG])

                def b32(v):
                    return v.unsqueeze(2).to_broadcast([P, nt, NE])
                dve.wait_ge(s_rx, b)
                g, v = gq[:, :, a:b, :], v6[:, :, a:b]
                grp = lg[:, a:b, 0:NG]
                link(dve.tensor_reduce(v[:, 0, :], grp, AX.X, ALU.max))
                link(dve.tensor_tensor(g[:, 0, :, :], grp, b4(v[:, 0, :]), ALU.subtract))
                link(dve.scalar_tensor_tensor(out=g[:, 2, :, :], in0=g[:, 0, :, :], scalar=0.0,
                                              in1=C("grank").unsqueeze(1).to_broadcast([P, nt, NG]),
                                              op0=ALU.is_equal, op1=ALU.mult))
                link(dve.tensor_reduce(v[:, 1, :], g[:, 2, :, :], AX.X, ALU.max))
                link(dve.tensor_tensor(g[:, 3, :, :], g[:, 2, :, :], b4(v[:, 1, :]), ALU.is_equal))
                link(dve.tensor_scalar(g[:, 3, :, :], g[:, 3, :, :], -1.0, BIG, ALU.add, ALU.mult))
                link(dve.tensor_tensor(sel[:, a:b, :].rearrange("p t (g e) -> p t g e", e=EPG),
                                       lg[:, a:b, NG:].rearrange("p t (g e) -> p t g e", e=EPG),
                                       g[:, 3, :, :].unsqueeze(3).to_broadcast([P, nt, NG, EPG]), ALU.add))

                def pick(out, top):
                    vals, t = sel[:, a:b, :], t1[:, a:b, :]
                    link(dve.tensor_reduce(top, vals, AX.X, ALU.max))
                    link(dve.tensor_tensor(t, vals, b32(top), ALU.is_equal))
                    link(dve.tensor_tensor(t, t, C("erank").unsqueeze(1).to_broadcast([P, nt, NE]), ALU.mult))
                    link(dve.tensor_reduce(v[:, 4, :], t, AX.X, ALU.max))
                    link(dve.tensor_tensor(out, t, b32(v[:, 4, :]), ALU.is_equal))
                pick(A1[:, a:b, :], v[:, 5, :])
                link(dve.scalar_tensor_tensor(out=sel[:, a:b, :], in0=A1[:, a:b, :], scalar=-BIG, in1=sel[:, a:b, :],
                                              op0=ALU.mult, op1=ALU.add))
                pick(A2[:, a:b, :], v[:, 6, :])
                link(dve.tensor_tensor(Ab[:, a:b, :], A1[:, a:b, :], A2[:, a:b, :], ALU.add))
            BIG = 1.0e30
            choose(0, NT - 1)
            route_logits(NT - 1)
            choose(NT - 1, NT)
            dve.sem_inc(s_Ab, 1)
            link(dve.memset(run[:, :, :], 0.0))
            link(dve.tensor_tensor(v6[:, 2, :], v6[:, 6, :], v6[:, 5, :], ALU.subtract))
            dve.sem_inc(s_re, 1)
            dve.wait_ge(s_rk, 1)
            cnt = ps[3][:, NT * NE:(NT + 1) * NE]
            over = bt[:, 0:NE * (MAXB - 1)].rearrange("p (e j) -> p e j", j=MAXB - 1)
            link(dve.tensor_tensor(over, cnt.unsqueeze(2).to_broadcast([P, NE, MAXB - 1]),
                                   C("thr").unsqueeze(1).to_broadcast([P, NE, MAXB - 1]), ALU.is_gt))
            link(dve.tensor_reduce(nov[:, :], over, AX.X, ALU.add))
            Z0 = NE // 2
            link(dve.tensor_copy(run[:, 0, Z0:], nov[:, :]))
            a, d = 0, 1
            while d < NE:
                link(dve.tensor_tensor(run[:, 1 - a, Z0:], run[:, a, Z0:], run[:, a, Z0 - d:Z0 + NE - d], ALU.add))
                a, d = 1 - a, 2 * d
            incl = run[:, a, Z0:]
            link(dve.tensor_tensor(first[:, :], incl, nov[:, :], ALU.subtract))
            link(dve.scalar_tensor_tensor(out=first[:, :], in0=first[:, :], scalar=float(CAP), in1=C("e128"),
                                          op0=ALU.mult, op1=ALU.add))
            rank = ps[3][:, 0:NT * NE].rearrange("p (t e) -> p t e", e=NE)
            link(dve.tensor_tensor(t1[:, :, :], rank, first[:, :].unsqueeze(1).to_broadcast([P, NT, NE]), ALU.add))
            for k, Ak in enumerate((A1, A2)):
                link(dve.tensor_tensor(t2[:, :, :], t1[:, :, :], Ak[:, :, :], ALU.mult))
                link(dve.tensor_reduce(slotf[:, k, :], t2[:, :, :], AX.X, ALU.add))
            link(dve.tensor_copy(sloti[:, :, :], slotf[:, :, :]))
            bp = bt[:, 0:4 * NT].bitcast(U32).rearrange("p (a k t) -> p a k t", a=2, k=2)
            dve.tensor_scalar(bp[:, 0, :, :], sloti[:, :, :], 7, None, ALU.logical_shift_right)
            link(dve.tensor_scalar(bp[:, 1, :, :], sloti[:, :, :], CAP - 1, None, ALU.bitwise_and))
            link(dve.tensor_copy(sbf[:, :, :, :], bp))
            here = C("tok")[:, 0:1]
            link(dve.scalar_tensor_tensor(out=last_row[:, :], in0=here.to_broadcast([P, NE]), scalar=float(CAP),
                                          in1=first[:, :], op0=ALU.mult, op1=ALU.subtract))
            link(dve.tensor_scalar(t2[:, 0, :], last_row[:, :], 0.0, None, ALU.is_ge))
            link(dve.tensor_reduce(bcol[:, 2:3], t2[:, 0, :], AX.X, ALU.add))
            link(dve.tensor_scalar(bcol[:, 0:1], bcol[:, 2:3], -1.0, None, ALU.add))
            link(dve.tensor_tensor(last_row[:, :], cnt, last_row[:, :], ALU.subtract))
            link(dve.scalar_tensor_tensor(out=t2[:, 1, :], in0=C("e128"), scalar=1.0 / CAP,
                                          in1=bcol[:, 0:1].to_broadcast([P, NE]),
                                          op0=ALU.mult, op1=ALU.is_equal))
            link(dve.tensor_tensor(t2[:, 1, :], t2[:, 1, :], last_row[:, :], ALU.mult))
            link(dve.tensor_reduce(bcol[:, 3:4], t2[:, 1, :], AX.X, ALU.add))
            link(dve.tensor_tensor(bcol[:, 4:7], bcol[:, 3:4].to_broadcast([P, 3]), C("quart"), ALU.is_gt))
            link(dve.tensor_reduce(bcol[:, 1:2], bcol[:, 4:7], AX.X, ALU.add))
            dve.sem_inc(s_bc, 1)
            for q in range(2 * NT):
                k, t = q // NT, q % NT
                if q >= NT:
                    dve.wait_ge(s_tbm, q - NT + 1)
                dve.tensor_scalar(Rt[:, t, :], C("iota"), sbf[:, 1, k, t:t + 1], None, ALU.is_equal)
                dve.tensor_scalar(Bt[:, q, :], C("iota")[:, 0:NB + 1], sbf[:, 0, k, t:t + 1],
                                  C("tok")[:, t:t + 1], ALU.is_equal, ALU.mult).then_inc(s_tb, 1)
            link(dve.tensor_scalar(nbi[:, 0:1], run[0:1, a, Z0 + NE - 1:Z0 + NE], float(NE), None, ALU.add))
            dve.wait_ge(s_br, 1)
            dve.tensor_copy(served[:, :], ps[5][0:1, 0:NB + 1])
            link(dve.tensor_copy(quarters[:, :], ps[5][0:1, P:P + NB + 1]))
            dve.wait_ge(s_tbm, 2 * NT)
            link(dve.tensor_copy(idxt[:, :], ps[4][:, 0:NB + 1]))
            dve.sem_inc(s_nb, 1)
            dve.wait_ge(s_re, 3)
            link(dve.tensor_reduce(v6[:, 7, :], gq[:, 1, :, :], AX.X, ALU.add))
            link(dve.tensor_scalar(v6[:, 8, :], v6[:, 3, :], 1.0, None, ALU.add))
            link(dve.tensor_tensor(v6[:, 7, :], v6[:, 7, :], v6[:, 8, :], ALU.mult))
            link(dve.reciprocal(gates[:, 0, :], v6[:, 7, :]))
            link(dve.tensor_tensor(gates[:, 1, :], gates[:, 0, :], v6[:, 3, :], ALU.mult))

            nb = dve.value_load(nbi[0:1, 0:1], min_val=NE, max_val=NB)

            def x_lo(n, j):
                dve.wait_ge(s_eTh, n * 2 + (j + 1))
                dve.tensor_tensor(eTl[:, 4 * j:4 * j + 4, :].rearrange("p c k -> p (c k)"), ps[2 + j][:, :],
                                  eTh[:, 4 * j:4 * j + 4, :].rearrange("p c k -> p (c k)").bitcast(F32),
                                  ALU.subtract).then_inc(s_eTl, 1)

            def e_lo(e, j):
                lo_piece(j, j, 6 * e + (PRE + j + 1))

            def e_block(b, last):
                if not last:
                    e, e1 = expert_of(dve, b), expert_of(dve, b + 1)
                    with dve.If(e1 > e):
                        e_lo(e1, 0)
                dve.wait_ge(s_sgm, b + (2 * NT + 1))
                dve.wait_ge(s_hT, b + 1)
                dve.tensor_tensor(hh[:, :], ps[0][:, :], sg[:, :], ALU.mult).then_inc(s_h13, 1)
                dve.wait_ge(s_h13, b + 1)
                dve.wait_ge(s_h1, 2 * b + 4)
                dve.tensor_tensor(hh[:, :], ps[1][:, :], hh[:, :], ALU.mult).then_inc(s_h, 1)
                dve.wait_ge(s_hTh, b + 1)
                dve.tensor_tensor(hTl[:, :, :].rearrange("p c k -> p (c k)"), ps[4][:, :],
                                  hTh[:, :, :].rearrange("p c k -> p (c k)").bitcast(F32),
                                  ALU.subtract).then_inc(s_hTl, 1)
                if not last:
                    x_lo(b + 1, 0)
                    x_lo(b + 1, 1)
                    with dve.If(e1 > e):
                        for j in (2, 3, 4, 5):
                            e_lo(e1, j)

            dve.wait_ge(s_lo, PRE + 3)
            dve.wait_ge(s_rst[0], 16 * NT // 2)
            for j in range(4, 6):
                e_lo(0, j)
            x_lo(0, 0)
            x_lo(0, 1)
            dve.sem_inc(s_h, 1)
            with dve.Fori(0, nb - 1) as b:
                e_block(b, last=False)
            e_block(nb - 1, last=True)
            def last_norm(a, b):
                dve.wait_ge(s_sq3, b)
                rsqrt(a, b, D, link)
                dve.sem_inc(s_rstd3, 1)
            for t in range(NT):
                dve.wait_ge(s_g1[t], 32)
                link(dve.scalar_tensor_tensor(out=x2[:, t, :], in0=ya[t][0][:, :], scalar=gates[:, 0, t:t + 1],
                                              in1=x2[:, t, :], op0=ALU.mult, op1=ALU.add))
                dve.scalar_tensor_tensor(out=x2[:, t, :], in0=ya[t][1][:, :], scalar=gates[:, 1, t:t + 1],
                                         in1=x2[:, t, :], op0=ALU.mult, op1=ALU.add).then_inc(s_c2, 1)
                if t == 2:
                    last_norm(0, 2)
            last_norm(2, NT)
            dve.wait_ge(s_gf, 16)
            for t in range(3, NT):
                dve.scalar_tensor_tensor(out=yo[t][:, :], in0=x2[:, t, :], scalar=rstd[:, t:t + 1],
                                         in1=gf[:, :], op0=ALU.mult, op1=ALU.mult).then_inc(s_yl, 1)

        @block.gpsimd
        def _(pool):
            def z_store(i, u):
                pool.wait_ge(s_zev, 12 * i + (u + 1))
                pool.dma_start(z_d[(u % 6) * P:(u % 6 + 1) * P, bass.ds(i * 1024 + (u // 6) * 512, 512)],
                               zst[u % 4][:, :]).then_inc(s_zst[u % 4], 16)
            with pool.Fori(0, NCH // 2) as i:
                for u in range(12):
                    z_store(i, u)
            n_link = [0]

            def link(ins):
                n_link[0] += 1
                ins.then_inc(s_pl, 1)
                pool.wait_ge(s_pl, n_link[0])

            def rotary_r(s, t):
                for k in range(2):
                    rotary(pool, link, zr[s][:, t, k * 256:(k + 1) * 256].rearrange("p (g d) -> p g d", d=HD), 32,
                           C("cosR")[:, t * 32:(t + 1) * 32], C("sinR")[:, t * 32:(t + 1) * 32], rt_p)

            def silu_steps(s):
                pool.wait_ge(s_sg, s + 1)
                pool.tensor_tensor(silu[s][:, :, :], silu[s][:, :, :], zgr[s][:, :, :], ALU.mult).then_inc(s_silu, 1)
            silu_steps(0)
            pool.wait_ge(s_zlq[1], 32)
            pool.wait_ge(s_warg, 1)
            for t in range(2):
                rotary(pool, link, zqk[1][:, t, :].rearrange("p (g d) -> p g d", d=HD), 8,
                       C("cosA")[:, t * 8:(t + 1) * 8], C("sinA")[:, t * 8:(t + 1) * 8], rt_p)
                rotary_r(1, t)
            pool.sem_inc(s_rotp, 1)
            silu_steps(1)
            pool.memset(zrow[:, :], 0.0).then_inc(s_zr, 1)
            pool.wait_ge(s_zr, 1)
            by_quarter = y_d.rearrange("(e q r) n -> q e (r n)", q=4, r=QR)
            for q, e0, e1 in ZEROS:
                pool.dma_start(by_quarter[q, e0:e1].rearrange("e (p c) -> p e c", c=256),
                               zrow[:, :].unsqueeze(1).to_broadcast([P, e1 - e0, 256])).then_inc(s_ys, 16)
            pool.wait_ge(s_hi, ZP + 1)
            pool.tensor_tensor(elo[P_LO[0]][:, :], raw[3][:, :], ehi[P_HI[0]][:, :].bitcast(F32),
                               ALU.subtract).then_inc(s_lo, 1)
            for t in range(NT):
                pool.wait_ge(s_rr, t + 1)
                pool.dma_start(xn_d[t * P:(t + 1) * P, :], rrow[t % 2][:, :]).then_inc(s_rst[t % 2], 16)
            for j in range(4):
                pool.wait_ge(s_hi, PRE + j + 1)
                pool.tensor_tensor(elo[j][:, :], raw[j][:, :], ehi[j][:, :].bitcast(F32),
                                   ALU.subtract).then_inc(s_lo1 if j == 1 else s_lo, 1)
            for k in range(2):
                pool.wait_ge(s_rst[k], 16 * NT // 2)
            pool.wait_ge(s_nb, 1)
            nb = pool.value_load(nbi[0:1, 0:1], min_val=NE, max_val=NB)

            def rows_in(n):
                pool.indirect_dma_start(out=xg[0:n, :], out_offset=None, in_=xn_d,
                                        in_offset=bass.IndirectOffsetOnAxis(ap=idxb[0:n, 0:1], axis=0)).then_inc(s_gx, 16)

            def gather(b):
                pool.tensor_copy(idxb[:, :], idxt[:, bass.ds(b, 1)]).then_inc(s_ic, 1)
                pool.wait_ge(s_ic, b + 1)
                pool.sem_inc(s_idx, 1)
                if isinstance(b, int) and b == 0:
                    rows_in(CAP)
                else:
                    q = pool.value_load(quarters[0:1, bass.ds(b, 1)], min_val=0, max_val=3)
                    for k in range(4):
                        with pool.If(q == k):
                            rows_in((k + 1) * QR)

            def store(b):
                pool.wait_ge(s_yc, 2 * b + 4)
                q = pool.value_load(quarters[0:1, bass.ds(b, 1)], min_val=0, max_val=3)
                for k in range(4):
                    n = (k + 1) * QR
                    with pool.If(q == k):
                        pool.dma_start(y_d[bass.ds(b * CAP, n), :], ystage[0:n, :]).then_inc(s_ys, 16)
            gather(0)
            pool.wait_ge(s_eT, 2)
            gather(1)
            with pool.Fori(0, nb - 1) as b:
                e, e1 = expert_of(pool, b), expert_of(pool, b + 1)
                with pool.If(e1 > e):
                    pool.wait_ge(s_hi, 6 * e1 + (PRE + 2))
                    pool.tensor_tensor(elo[1][:, :], raw[1][:, :], ehi[1][:, :].bitcast(F32),
                                       ALU.subtract).then_inc(s_lo1, 1)
                pool.wait_ge(s_eT, 2 * b + 4)
                gather(b + 2)
                store(b)
            store(nb - 1)
            pool.wait_ge(s_ys, 16 * nb + 16 * NZ)
            pool.wait_ge(s_gx, 16 * nb + 16)
            pool.sem_inc(s_md, 1)
            for t in range(NT):
                for k in range(2):
                    pool.indirect_dma_start(out=ya[t][k][:, :], out_offset=None, in_=y_d,
                                            in_offset=bass.IndirectOffsetOnAxis(ap=sloti[:, k, t:t + 1], axis=0)
                                            ).then_inc(s_g1[t], 16)
            pool.wait_ge(s_gf, 16)
            for t in range(3):
                pool.wait_ge(s_ym, t + 1)
                pool.tensor_tensor(yo[t][:, :], yo[t][:, :], gf[:, :], ALU.mult).then_inc(s_yf, 1)


_INS = ['x_prompt', 'x_sample', 'attn_norm_g', 'w_in', 'lam_q1', 'lam_k1', 'lam_q2', 'lam_k2', 'subln_g',
        'ret_decay_f', 'ret_decay_b', 'w_pa', 'w_pb', 'w_out', 'ffn_norm_g', 'w_rg', 'b_rg', 'w_re', 'b_re',
        'w1', 'w3', 'w2', 'final_norm_g']
_OUTS = [('y_prompt', (1, 512, D)), ('y_sample', (1, 256, D))]


def kernel(**inputs):
    import numpy as _np
    import concourse.bacc as _bacc
    from concourse import mybir as _mybir
    from concourse.bass_utils import run_bass_kernel_spmd as _run

    nc = _bacc.Bacc("TRN2", target_bir_lowering=False, num_devices=1)
    arrays, aps = {}, {}
    for name in _INS + ["consts"]:
        a = constants() if name == "consts" else _np.ascontiguousarray(inputs[name])
        arrays[f"in_{name}"] = a
        aps[name] = nc.dram_tensor(f"in_{name}", a.shape, _mybir.dt.from_np(a.dtype), kind="ExternalInput").ap()
    for name, shape in _OUTS:
        aps[name] = nc.dram_tensor(f"out_{name}", shape, _mybir.dt.float32, kind="ExternalOutput").ap()
    hybrid_layer(nc, aps)
    r = _run(nc, [arrays], core_ids=[0])
    return tuple(r.results[0][f"out_{name}"] for name, _ in _OUTS)
```
